# Optimizing a Trainium2 kernel written in Bass

```python
import numpy as np
import jax
import jax.numpy as jnp
from jax import lax

D_MODEL = 1024
BATCH = 1
SEQ = 1024
DEPTH = 1

BRANCH_WIDTH = D_MODEL // 2
N_BRANCH = 3
FOX_HEAD_DIM = 64
FOX_HEADS = BRANCH_WIDTH // FOX_HEAD_DIM
FOX_BLOCK = 128
FOX_FORGET_BIAS = 2.0
ML_HEADS = 4
ML_DV = BRANCH_WIDTH // ML_HEADS
ML_DQK = ML_DV // 2
ML_CONV = 4
ML_CHUNK = 128
HG_HEADS = 4
HG_DV = BRANCH_WIDTH // HG_HEADS
HG_DK = 128
HG_CHUNK = 64
N_EXPERTS = 64
N_GROUPS = 8
TOPK_GROUPS = 4
TOP_K = 8
D_FF_EXPERT = D_MODEL // 4
D_FF_SHARED = D_MODEL // 4
ROUTE_SCALE = 2.5
MOE_BLOCK = 256
EPS = 1e-6

IN_SPLITS = (
    FOX_HEADS * FOX_HEAD_DIM, FOX_HEADS * FOX_HEAD_DIM, FOX_HEADS * FOX_HEAD_DIM, FOX_HEADS,
    2 * ML_HEADS * ML_DQK, ML_HEADS * ML_DV, ML_HEADS, ML_HEADS, ML_HEADS * ML_DV,
    HG_HEADS * HG_DK, HG_HEADS * HG_DK, HG_HEADS * HG_DV, HG_HEADS * HG_DV,
    N_BRANCH * D_MODEL,
)
D_IN = 3 * FOX_HEADS * FOX_HEAD_DIM + FOX_HEADS + 2 * ML_HEADS * ML_DQK + 2 * ML_HEADS * ML_DV + 2 * ML_HEADS + 2 * HG_HEADS * HG_DK + 2 * HG_HEADS * HG_DV + N_BRANCH * D_MODEL

kernel_name = "hybrid_fox_mlstm_hgrn2_moe_adaln"

def _rms(x):
    xf = x.astype(jnp.float32)
    return xf * lax.rsqrt(jnp.mean(xf * xf, axis=-1, keepdims=True) + EPS)

def _heads(a, n_heads):
    b, s, _ = a.shape
    return a.reshape(b, s, n_heads, -1).transpose(0, 2, 1, 3)

def _merge_heads(a):
    b, h, s, d = a.shape
    return a.transpose(0, 2, 1, 3).reshape(b, s, h * d)

def _to_chunks(a, chunk):
    b, h, s = a.shape[:3]
    return jnp.moveaxis(a.reshape(b, h, s // chunk, chunk, *a.shape[3:]), 2, 0)

def _from_chunks(a):
    nc, b, h, chunk = a.shape[:4]
    return jnp.moveaxis(a, 0, 2).reshape(b, h, nc * chunk, *a.shape[4:])

def _causal_depthwise_conv(x, w):
    width, ch = w.shape
    return lax.conv_general_dilated(
        x, w.astype(x.dtype)[:, None, :], window_strides=(1,), padding=[(width - 1, 0)],
        dimension_numbers=("NWC", "WIO", "NWC"), feature_group_count=ch)

def _forgetting_attention(q, k, v, logf):
    b, h, s, dh = q.shape
    cum = jnp.cumsum(logf, axis=-1)
    k_pos = jnp.arange(s)
    scale = dh ** -0.5

    def block(i):
        start = i * FOX_BLOCK
        qb = lax.dynamic_slice_in_dim(q, start, FOX_BLOCK, axis=2)
        fq = lax.dynamic_slice_in_dim(cum, start, FOX_BLOCK, axis=2)
        logits = jnp.einsum("bhtd,bhsd->bhts", qb, k).astype(jnp.float32) * scale
        logits = logits + fq[..., :, None] - cum[..., None, :]
        q_pos = start + jnp.arange(FOX_BLOCK)
        logits = jnp.where(k_pos[None, :] <= q_pos[:, None], logits, -jnp.inf)
        p = jax.nn.softmax(logits, axis=-1)
        return jnp.einsum("bhts,bhsd->bhtd", p.astype(v.dtype), v)

    out = lax.map(block, jnp.arange(s // FOX_BLOCK))
    return jnp.moveaxis(out, 0, 2).reshape(b, h, s, dh)

def _mlstm_chunkwise(q, k, v, i_pre, logf):
    b, h, s, dqk = q.shape
    dv = v.shape[-1]
    causal = jnp.tril(jnp.ones((ML_CHUNK, ML_CHUNK), dtype=bool))
    xs = tuple(_to_chunks(a, ML_CHUNK) for a in (q, k, v, i_pre, logf))

    def step(carry, xs_c):
        c_mat, n_vec, m_prev = carry
        qb, kb, vb, ib, fb = xs_c
        bcum = jnp.cumsum(fb, axis=-1)
        log_d = bcum[..., :, None] - bcum[..., None, :] + ib[..., None, :]
        log_d = jnp.where(causal, log_d, -jnp.inf)
        log_inter = bcum + m_prev[..., None]
        m_t = jnp.maximum(jnp.max(log_d, axis=-1), log_inter)
        w_intra = jnp.exp(log_d - m_t[..., None])
        w_inter = jnp.exp(log_inter - m_t)
        sc = jnp.einsum("bhtd,bhsd->bhts", qb, kb) * w_intra
        num = jnp.einsum("bhts,bhsv->bhtv", sc, vb) + w_inter[..., None] * jnp.einsum("bhtd,bhdv->bhtv", qb, c_mat)
        den = jnp.sum(sc, axis=-1) + w_inter * jnp.einsum("bhtd,bhd->bht", qb, n_vec)
        h_out = num / jnp.maximum(jnp.abs(den), jnp.exp(-m_t))[..., None]
        b_last = bcum[..., -1]
        log_w_in = b_last[..., None] - bcum + ib
        m_new = jnp.maximum(b_last + m_prev, jnp.max(log_w_in, axis=-1))
        w_in = jnp.exp(log_w_in - m_new[..., None])
        decay = jnp.exp(b_last + m_prev - m_new)
        c_mat = decay[..., None, None] * c_mat + jnp.einsum("bhs,bhsd,bhsv->bhdv", w_in, kb, vb)
        n_vec = decay[..., None] * n_vec + jnp.einsum("bhs,bhsd->bhd", w_in, kb)
        return (c_mat, n_vec, m_new), h_out

    init = (jnp.zeros((b, h, dqk, dv), jnp.float32), jnp.zeros((b, h, dqk), jnp.float32), jnp.zeros((b, h), jnp.float32))
    _, hs = lax.scan(step, init, xs)
    return _from_chunks(hs)

def _hgrn2_chunkwise(q, k, v, logf):
    b, h, s, dk = q.shape
    dv = v.shape[-1]
    causal = jnp.tril(jnp.ones((HG_CHUNK, HG_CHUNK), dtype=bool))
    xs = tuple(_to_chunks(a, HG_CHUNK) for a in (q, k, v, logf))

    def step(state, xs_c):
        qb, kb, vb, gb = xs_c
        a = jnp.cumsum(gb, axis=2)
        rel = a[:, :, :, None, :] - a[:, :, None, :, :]
        decay = jnp.exp(jnp.where(causal[:, :, None], rel, -jnp.inf))
        sc = jnp.einsum("bhtd,bhsd,bhtsd->bhts", qb, kb, decay)
        out = jnp.einsum("bhts,bhsv->bhtv", sc, vb) + jnp.einsum("bhtd,bhdv->bhtv", qb * jnp.exp(a), state)
        a_last = a[:, :, -1]
        state = jnp.exp(a_last)[..., None] * state + jnp.einsum("bhsd,bhsv->bhdv", kb * jnp.exp(a_last[:, :, None] - a), vb)
        return state, out

    _, outs = lax.scan(step, jnp.zeros((b, h, dk, dv), jnp.float32), xs)
    return _from_chunks(outs)

def _hybrid_mixer(h, w_in, fox_bf, fox_q_g, fox_k_g, mlstm_conv, mlstm_bi, mlstm_bf, mlstm_norm_g,
                  hgrn_lb, hgrn_norm_g, w_branch, w_out):
    dt = h.dtype
    b, s, _ = h.shape
    proj = h @ w_in
    split_idx = np.cumsum(IN_SPLITS)[:-1].tolist()
    (fq, fk, fv, ff, mqk, mv, mi, mf, mo, hf, hq, hi, hg, gates) = jnp.split(proj, split_idx, axis=-1)

    qh = (_rms(_heads(fq, FOX_HEADS)) * fox_q_g).astype(dt)
    kh = (_rms(_heads(fk, FOX_HEADS)) * fox_k_g).astype(dt)
    logf_fox = jax.nn.log_sigmoid(ff.astype(jnp.float32) + fox_bf).transpose(0, 2, 1)
    y_fox = _merge_heads(_forgetting_attention(qh, kh, _heads(fv, FOX_HEADS), logf_fox))

    qk = jax.nn.silu(_causal_depthwise_conv(mqk, mlstm_conv))
    mq, mk = jnp.split(qk, 2, axis=-1)
    i_pre = (mi.astype(jnp.float32) + mlstm_bi).transpose(0, 2, 1)
    logf_ml = jax.nn.log_sigmoid(mf.astype(jnp.float32) + mlstm_bf).transpose(0, 2, 1)
    hm = _mlstm_chunkwise(_heads(mq, ML_HEADS), _heads(mk, ML_HEADS) * (ML_DQK ** -0.5), _heads(mv, ML_HEADS), i_pre, logf_ml)
    y_ml = (jax.nn.sigmoid(mo.astype(jnp.float32)) * _merge_heads(_rms(hm)) * mlstm_norm_g).astype(dt)

    fz = _heads(hf, HG_HEADS).astype(jnp.float32)
    lb = hgrn_lb.reshape(HG_HEADS, HG_DK)[None, :, None, :]
    logf_hg = jnp.logaddexp(jnp.log(lb), jnp.log1p(-lb) + jax.nn.log_sigmoid(fz))
    k_hg = (1.0 - lb) * jax.nn.sigmoid(-fz)
    q_hg = jax.nn.silu(_heads(hq, HG_HEADS))
    oh = _hgrn2_chunkwise(q_hg, k_hg, _heads(hi, HG_HEADS), logf_hg)
    y_hg = (_merge_heads(_rms(oh)) * hgrn_norm_g * jax.nn.silu(hg.astype(jnp.float32))).astype(dt)

    g = jax.nn.sigmoid(gates).reshape(b, s, N_BRANCH, D_MODEL)
    merged = g[:, :, 0] * (y_fox @ w_branch[0]) + g[:, :, 1] * (y_ml @ w_branch[1]) + g[:, :, 2] * (y_hg @ w_branch[2])
    return merged @ w_out

def _moe_ffn(h, router_w, router_bias, w1, w3, w2, ws1, ws3, ws2):
    t, d = h.shape
    scores = jax.nn.sigmoid((h @ router_w).astype(jnp.float32))
    choice = scores + router_bias
    grp_score = lax.top_k(choice.reshape(t, N_GROUPS, N_EXPERTS // N_GROUPS), 2)[0].sum(-1)
    _, grp_idx = lax.top_k(grp_score, TOPK_GROUPS)
    grp_mask = jnp.any(grp_idx[:, :, None] == jnp.arange(N_GROUPS)[None, None, :], axis=1)
    masked = jnp.where(jnp.repeat(grp_mask, N_EXPERTS // N_GROUPS, axis=1), choice, -jnp.inf)
    _, idx = lax.top_k(masked, TOP_K)
    wts = jnp.take_along_axis(scores, idx, axis=-1)
    wts = wts / jnp.sum(wts, axis=-1, keepdims=True) * ROUTE_SCALE

    n_assign = t * TOP_K
    flat_e = idx.reshape(n_assign)
    order = jnp.argsort(flat_e)
    sorted_e = flat_e[order]
    tok = (order // TOP_K).astype(jnp.int32)
    counts = jax.ops.segment_sum(jnp.ones((n_assign,), jnp.int32), flat_e, num_segments=N_EXPERTS)
    padded = (counts + MOE_BLOCK - 1) // MOE_BLOCK * MOE_BLOCK
    pad_end = jnp.cumsum(padded)
    pad_start = pad_end - padded
    start = jnp.cumsum(counts) - counts
    dest = pad_start[sorted_e] + jnp.arange(n_assign) - start[sorted_e]
    n_blocks = -(-n_assign // MOE_BLOCK) + N_EXPERTS
    n_rows = n_blocks * MOE_BLOCK
    row_tok = jnp.full((n_rows,), t, jnp.int32).at[dest].set(tok)
    row_w = jnp.zeros((n_rows,), jnp.float32).at[dest].set(wts.reshape(n_assign)[order])
    blk_exp = jnp.minimum(jnp.searchsorted(pad_end, jnp.arange(n_blocks) * MOE_BLOCK, side="right"), N_EXPERTS - 1)
    h_pad = jnp.concatenate([h, jnp.zeros((1, d), h.dtype)], axis=0)

    def body(y, xs_b):
        rt, rw, e = xs_b
        xb = h_pad[rt]
        hid = jax.nn.silu(xb @ w1[e]) * (xb @ w3[e])
        ob = (hid @ w2[e]) * rw[:, None]
        return y.at[rt].add(ob.astype(y.dtype)), None

    y, _ = lax.scan(body, jnp.zeros((t + 1, d), h.dtype),
                    (row_tok.reshape(n_blocks, MOE_BLOCK), row_w.reshape(n_blocks, MOE_BLOCK), blk_exp))
    shared = (jax.nn.silu(h @ ws1) * (h @ ws3)) @ ws2
    return y[:t] + shared

def setup_inputs(seed: int = 0) -> dict:
    key = jax.random.key(seed)
    ks = jax.random.split(key, 32)
    f32 = jnp.float32
    D = D_MODEL

    def nrm(k, shape, scale):
        return jax.random.normal(k, shape, f32) * scale

    return {
        "x": nrm(ks[0], (BATCH, SEQ, D), 1.0),
        "c": nrm(ks[1], (BATCH, D), 1.0),
        "ada_w": nrm(ks[2], (DEPTH, D, 6 * D), 0.5 * D ** -0.5),
        "ada_b": nrm(ks[3], (DEPTH, 6 * D), 0.02),
        "norm1_g": 1.0 + nrm(ks[4], (DEPTH, D), 0.05),
        "norm2_g": 1.0 + nrm(ks[5], (DEPTH, D), 0.05),
        "w_in": nrm(ks[6], (DEPTH, D, D_IN), D ** -0.5),
        "fox_bf": FOX_FORGET_BIAS + nrm(ks[7], (DEPTH, FOX_HEADS), 0.5),
        "fox_q_g": 1.0 + nrm(ks[8], (DEPTH, FOX_HEAD_DIM), 0.05),
        "fox_k_g": 1.0 + nrm(ks[9], (DEPTH, FOX_HEAD_DIM), 0.05),
        "mlstm_conv": nrm(ks[10], (DEPTH, ML_CONV, 2 * ML_HEADS * ML_DQK), ML_CONV ** -0.5),
        "mlstm_bi": nrm(ks[11], (DEPTH, ML_HEADS), 0.1),
        "mlstm_bf": jnp.linspace(3.0, 6.0, ML_HEADS, dtype=f32)[None, :] + nrm(ks[12], (DEPTH, ML_HEADS), 0.1),
        "mlstm_norm_g": 1.0 + nrm(ks[13], (DEPTH, ML_HEADS * ML_DV), 0.05),
        "hgrn_lower_bounds": nrm(ks[14], (DEPTH, HG_HEADS * HG_DK), 0.1),
        "hgrn_norm_g": 1.0 + nrm(ks[15], (DEPTH, HG_HEADS * HG_DV), 0.05),
        "w_branch": nrm(ks[16], (DEPTH, N_BRANCH, BRANCH_WIDTH, D), BRANCH_WIDTH ** -0.5),
        "w_out": nrm(ks[17], (DEPTH, D, D), D ** -0.5),
        "router_w": nrm(ks[18], (DEPTH, D, N_EXPERTS), D ** -0.5),
        "router_bias": nrm(ks[19], (DEPTH, N_EXPERTS), 0.01),
        "exp_w1": nrm(ks[20], (DEPTH, N_EXPERTS, D, D_FF_EXPERT), D ** -0.5),
        "exp_w3": nrm(ks[21], (DEPTH, N_EXPERTS, D, D_FF_EXPERT), D ** -0.5),
        "exp_w2": nrm(ks[22], (DEPTH, N_EXPERTS, D_FF_EXPERT, D), D_FF_EXPERT ** -0.5),
        "sh_w1": nrm(ks[23], (DEPTH, D, D_FF_SHARED), D ** -0.5),
        "sh_w3": nrm(ks[24], (DEPTH, D, D_FF_SHARED), D ** -0.5),
        "sh_w2": nrm(ks[25], (DEPTH, D_FF_SHARED, D), D_FF_SHARED ** -0.5),
    }

def reference(x, c, ada_w, ada_b, norm1_g, norm2_g, w_in, fox_bf, fox_q_g, fox_k_g, mlstm_conv, mlstm_bi,
              mlstm_bf, mlstm_norm_g, hgrn_lower_bounds, hgrn_norm_g, w_branch, w_out, router_w, router_bias,
              exp_w1, exp_w3, exp_w2, sh_w1, sh_w3, sh_w2):
    b, s, d = x.shape
    dt = x.dtype
    cond = jax.nn.silu(c)
    lb_all = jnp.cumsum(jax.nn.softmax(hgrn_lower_bounds.astype(jnp.float32), axis=0), axis=0)
    lb_all = lb_all - lb_all[0]
    for l in range(DEPTH):
        mod = (cond @ ada_w[l] + ada_b[l])[:, None, :]
        sh1, sc1, g1, sh2, sc2, g2 = jnp.split(mod, 6, axis=-1)
        h = (_rms(x) * norm1_g[l] * (1.0 + sc1) + sh1).astype(dt)
        mixed = _hybrid_mixer(h, w_in[l], fox_bf[l], fox_q_g[l], fox_k_g[l], mlstm_conv[l], mlstm_bi[l],
                              mlstm_bf[l], mlstm_norm_g[l], lb_all[l], hgrn_norm_g[l], w_branch[l], w_out[l])
        x = x + g1 * mixed
        h = (_rms(x) * norm2_g[l] * (1.0 + sc2) + sh2).astype(dt)
        y = _moe_ffn(h.reshape(b * s, d), router_w[l], router_bias[l], exp_w1[l], exp_w3[l], exp_w2[l],
                     sh_w1[l], sh_w3[l], sh_w2[l]).reshape(b, s, d)
        x = x + g2 * y
    return x


_drawn_inputs = setup_inputs


def setup_inputs(seed=0):
    import zlib

    import numpy as np

    out = dict(_drawn_inputs(seed))
    spreads = {}
    factors = {'fox_q_g': 5.725,
     'fox_k_g': 4.974,
     'mlstm_bi': 8.0,
     'mlstm_norm_g': 4.455,
     'hgrn_norm_g': 3.579}
    for name, (base, spread) in spreads.items():
        noise = np.random.default_rng([zlib.crc32(name.encode()), seed]).standard_normal(out[name].shape)
        drawn = base * np.exp(spread * noise) if base else spread * noise
        out[name] = jnp.asarray(drawn.astype(out[name].dtype))
    for name, factor in factors.items():
        out[name] = (out[name] * factor).astype(out[name].dtype)
    return out
```

```python
from contextlib import ExitStack

import concourse.bass as bass
from concourse import mybir

F32 = mybir.dt.float32
I32 = mybir.dt.int32
ALU = mybir.AluOpType
ACT = mybir.ActivationFunctionType
AX = mybir.AxisListType
P = 128
BW = 512
EPS = 1e-6
NEG = -1.0e30
FAR = 2048


def layer_kernel(nc, a, out):
    T, D = a["x"].shape[1:]
    NT, KD = T // P, D // P
    FH, FD = a["fox_bf"].shape[1], a["fox_q_g"].shape[1]
    MH = a["mlstm_bi"].shape[1]
    W = FH * FD
    MV = W // MH
    MQ = MV // 2
    HH = W // P
    TAPS = a["mlstm_conv"].shape[1]
    NE = a["router_w"].shape[2]
    NG, TOPG, TOPK, ROUTE = 8, 4, 8, 2.5
    GE = NE // NG
    FF = a["exp_w1"].shape[3]
    FK = FF // P
    assert a["x"].shape[0] == 1 and a["w_in"].shape[0] == 1
    assert W == BW and MH * MQ * 2 == BW and 2 * FF == BW and D == 2 * BW and NT == 8 and KD == 8
    w_in = a["w_in"][0]
    widths = [W, W, W, FH, 2 * MH * MQ, W, MH, MH, W, W, W, W, W, 3 * D]
    names = ["fq", "fk", "fv", "ff", "mqk", "mv", "mi", "mf", "mo", "hf", "hq", "hi", "hg", "gates"]
    col = {n: sum(widths[:j]) for j, n in enumerate(names)}

    ctx = ExitStack()
    with ctx:
        sb = lambda name, shape, dt=F32: ctx.enter_context(nc.sbuf_tensor(name, shape, dt))
        sem = lambda name: ctx.enter_context(nc.semaphore(name))
        dram = lambda name, shape: nc.dram_tensor(name, shape, F32, kind="Internal").ap()

        proj_d = dram("proj_d", [13 * 8, P, BW])
        frow_d = dram("frow_d", [FH, T])
        mrow_d = dram("mrow_d", [MH, T])
        mdec_d = dram("mdec_d", [MH, NT])
        x2_d = dram("x2_d", [T, D])
        h2_d = dram("h2_d", [T, D])
        y_d = dram("y_d", [T + P, D])

        psum = ctx.enter_context(nc.psum_tensor("psum", [P, 8, BW], F32))
        bank = lambda b: psum[:, b, :]
        banks = lambda b, n, **kw: psum[:, b:b + n, :].rearrange("p b n -> p (b n)")

        hT = sb("hT", [P, KD, T])
        ring = sb("ring", [P, 3, 8, BW])
        work = sb("work", [P, 27648])
        ident = sb("ident", [P, P])
        ones = sb("ones", [P, P])
        col_i = sb("col_i", [P, P])
        upper = sb("upper", [P, P])
        strict = sb("strict", [P, P])
        foxmask = sb("foxmask", [P, P])
        levels = sb("levels", [P, 8, P], I32)
        vcol = sb("vcol", [P, 88])
        cond = sb("cond", [P, KD])
        mod = sb("mod", [P, 48])
        a1 = sb("a1", [P, KD])
        a2 = sb("a2", [P, KD])
        wsm = sb("wsm", [P, KD, 16])
        sm = sb("sm", [P, NT, 16])
        gq = sb("gq", [P, FD])
        gk = sb("gk", [P, FD])
        gml = sb("gml", [P, W])
        ghg = sb("ghg", [P, W])
        bff = sb("bff", [FH, 1])
        bmi = sb("bmi", [MH, 1])
        bmf = sb("bmf", [MH, 1])
        mcol = sb("mcol", [P, 4, NT, MH])
        mdec = sb("mdec", [P, MH, NT])
        stat = sb("stat", [P, 64])
        newton = sb("newton", [P, 3, 8])
        tok = sb("tok", [P, NT])
        dump = sb("dump", [P, 1])
        cst = sb("cst", [P, 2])

        def view(at, *shape):
            n = 1
            for s in shape:
                n *= s
            v = work[:, at:at + n]
            if len(shape) == 2:
                v = v.rearrange("p (a b) -> p a b", b=shape[1])
            if len(shape) == 3:
                v = v.rearrange("p (a b c) -> p a b c", b=shape[1], c=shape[2])
            return v

        xs, xn = view(0, NT, D), view(8192, NT, D)
        R = [view(12288 + 1024 * j, T) for j in range(10)]
        vrow = view(24000, P)
        sI, tI, xI, shI = (view(24200 + 128 * j, P).bitcast(I32) for j in range(4))
        eqf = view(24800, P)
        tokI = view(25000, NT).bitcast(I32)
        qT, kT, vf = view(0, 4, T), view(4096, 4, T), view(8192, NT, W)
        yf = view(12288, NT, W)
        pl = [view(16384 + 1024 * j, T) for j in range(2)]
        pT = [view(18432 + 1024 * j, NT, P) for j in range(2)]
        ncb = [view(20480 + 1024 * j, T) for j in range(2)]
        raw = [view(22528 + 512 * j, W) for j in range(2)]
        qn = [view(23552 + 512 * j, W) for j in range(2)]
        sqb = view(24576, W)
        ncd = view(25088, P)
        stg = [view(25600 + 512 * j, BW) for j in range(4)]
        yTf, yTm, yTh = view(0, 4, T), view(4096, 4, T), view(8192, 4, T)
        yT = [yTf, yTm, yTh]
        mo = view(8192, NT, W)
        vaug = view(12288, NT, MH, MV + 1)
        mqkT = view(16416, 4, T)
        conv_in = [view(20512 + 1032 * j, T + TAPS - 1) for j in range(2)]
        at = 20512
        nmb = [view(at + 512 * j, MH, P) for j in range(2)]
        mw, msc = view(at + 1024, MH, P), view(at + 1536, MH, P)
        mkt, mkw = view(at + 2048, MH * MQ), view(at + 2304, MH, MQ)
        mnum, mtmp, my = view(at + 2560, MH, MV + 1), view(at + 3076, W), view(at + 3588, W)
        mC = view(at + 4100, 2, MV + 1)
        hz, hq, hv, hg, ha, hk, hqe, hkd, hE0, hE1, hsc, hkT, hst = (view(12288 + 1024 * j, T) for j in range(13))
        hE = [hE0, hE1]
        gt = [view(12288 + 512 * j, BW) for j in range(3)]
        prod = [view(13824 + 512 * j, BW) for j in range(2)]
        dgb = [view(24256 + 512 * j, 4, P) for j in range(2)]
        h2T = view(0, KD, T)
        xin = [view(12288 + 1024 * j, D) for j in range(2)]
        g1b, a2b, b2b = (view(14336 + 1024 * j, D) for j in range(3))
        g2b = view(10288, D)
        slotn = view(0, T)
        x2 = [view(18432 + 1024 * j, D) for j in range(2)]
        h2 = [view(20480 + 1024 * j, D) for j in range(2)]
        dsc = view(22528, D)
        rwt = view(23680, KD, NE)
        shw2 = ring[:, 1, 0:4, :].rearrange("p a n -> p (a n)").rearrange("p (k n) -> p k n", k=2)
        rbias = view(24192, NE)
        sco, cho, msk, sel, cum, eqt = (view(24256 + 64 * j, NE) for j in range(6))
        m8 = view(24640, NG, 8)
        gsc, gmk, geq, gcu, top = (view(24704 + 8 * j, 8) for j in range(5))
        sgm, shh = view(24768, FF), view(25024, FF)
        shT = view(25280, FK, P)
        ysh = [view(25600 + 1024 * j, D) for j in range(2)]
        NX = NE + 2
        selall = view(8192, NT, NE)
        posm = view(8704, NT, NX)
        tw = view(9232, NT, NX, 2)
        w13 = [hT[:, 4 * b:4 * b + 4, :].rearrange("p k n -> p (k n)").rearrange("p (k n) -> p k n", k=KD) for b in range(2)]
        w2 = [ring[:, 2, 4 * b:4 * b + 4, :].rearrange("p k n -> p (k n)").rearrange("p (k n) -> p k n", k=FK) for b in range(2)]
        xg = [view(12288 + 1024 * j, D) for j in range(3)]
        xgT = [view(15360 + 1024 * j, KD, P) for j in range(3)]
        oh = [view(18432 + 1024 * j, NT, P) for j in range(3)]
        ob = [view(21504 + 1024 * j, D) for j in range(3)]
        sg = [view(24576 + 256 * j, FF) for j in range(3)]
        hid = [view(25344 + 256 * j, FF) for j in range(3)]
        hidT = [view(26112 + 256 * j, FK, P) for j in range(3)]
        idx = sb("idx", [P, 6], I32)
        wts = sb("wts", [P, 6])
        fy = [view(12288 + 1024 * j, D) for j in range(4)]
        fx = [view(16384 + 1024 * j, D) for j in range(4)]
        cnt = sb("cnt", [P, NX], I32)

        TBLOCKS = ["fq", "fk", "fv", "mqk", "mv", "mo", "hf", "hq", "hi", "hg"]
        order = [("ada", 0), ("ada", 1), ("ada", 2), ("ada", 3), ("w", 0), ("ada", 4), ("ada", 5), ("ada", 6), ("w", 1),
                 ("ada", 7), ("ada", 8), ("ada", 9), ("w", 2), ("ada", 10), ("ada", 11)]
        order += [("w", q) for q in range(3, 16)]
        order += [("wb", 0), ("wb", 1), ("wb", 2), ("wo", 0), ("wo", 1), ("sh", 0), ("sh", 1)]
        place = {b: n for n, b in enumerate(order)}
        NDMA = {"sh0": 2}
        TRANSPOSED = {3, 6, 7} | set(range(10, 16))
        NU, U_B, U_C = 8 * 16, 24, 80
        FSTEPS = FH * NT
        slot = lambda b: ring[:, place[b] % 3]
        flat = lambda v: v.rearrange("p a n -> p (a n)")

        R_MQK, R_MV, R_MO, R_HF, R_HQ, R_HI, R_HG, R_G = (8 * j for j in range(8))

        early = ExitStack()
        whole, sem = sem, lambda name: early.enter_context(nc.semaphore(name))
        s_x = [sem(f"s_x{i}") for i in range(2)]
        s_wsm, s_vec, s_ring = sem("s_wsm"), sem("s_vec"), [whole(f"s_ring{i}") for i in range(3)]
        s_iota, s_pconst, s_dconst = sem("s_iota"), sem("s_pconst"), sem("s_dconst")
        s_dve, s_act, s_pool = whole("s_dve"), whole("s_act"), whole("s_pool")
        s_vt, s_vc, s_cond = sem("s_vt"), sem("s_vc"), sem("s_cond")
        s_mod, s_modc, s_a1 = sem("s_mod"), sem("s_modc"), sem("s_a1")
        s_ss, s_xn, s_xt, s_xea, s_xed = (sem(n) for n in ("s_ss", "s_xn", "s_xt", "s_xea", "s_xed"))
        s_sm, s_smc, s_rows, s_zr, s_lr, s_er = (sem(n) for n in ("s_sm", "s_smc", "s_rows", "s_zr", "s_lr", "s_er"))
        s_fr, s_mr, s_mf, s_mct, s_mcc, s_nd = (sem(n) for n in ("s_fr", "s_mr", "s_mf", "s_mct", "s_mcc", "s_nd"))
        s_rd = whole("s_rd")
        s_pj, s_ev = sem("s_pj"), sem("s_ev")
        s_st = [sem(f"s_st{i}") for i in range(4)]
        s_qn, s_qt, s_qe = sem("s_qn"), sem("s_qt"), sem("s_qe")
        s_nc = [whole(f"s_nc{i}") for i in range(2)]
        s_S, s_pl, s_p, s_T, s_pT, s_O, s_y = (sem(n) for n in ("s_S", "s_pl", "s_p", "s_T", "s_pT", "s_O", "s_y"))
        s_fyt, s_fyc = sem("s_fyt"), sem("s_fyc")
        s_pad, s_cv, s_sil, s_mo, s_mos = sem("s_pad"), sem("s_cv"), sem("s_sil"), whole("s_mo"), sem("s_mos")
        s_cin = [whole(f"s_cin{i}") for i in range(2)]
        s_va = whole("s_va")
        s_nm = [whole(f"s_nm{i}") for i in range(2)]
        m_w, m_e, m_k, m_ST, m_sc, m_kw, m_B, m_in, m_num, m_st, m_y, m_yt, m_yc = (sem("m_" + n) for n in (
            "w", "e", "k", "ST", "sc", "kw", "B", "in", "num", "st", "y", "yt", "yc"))
        h_zq, h_vg = whole("h_zq"), whole("h_vg")
        h_ab, h_lf, h_k, h_kd = (sem("h_" + n) for n in ("ab", "lf", "k", "kd"))
        h_a, h_ea, h_d, h_de, h_x, h_e, h_qk, h_S, h_sc = (sem("h_" + n) for n in ("a", "ea", "d", "de", "x", "e", "qk", "S", "sc"))
        h_kt, h_kc, h_up, h_st, h_O, h_y, h_yt, h_yc = (sem("h_" + n) for n in ("kt", "kc", "up", "st", "O", "y", "yt", "yc"))
        sem = whole
        s_g = [sem(f"s_g{i}") for i in range(3)]
        s_gs, s_br, s_pr, s_mg = sem("s_gs"), sem("s_br"), sem("s_pr"), sem("s_mg")
        s_dg, s_bc, s_bcc = sem("s_dg"), sem("s_bc"), sem("s_bcc")
        s_xi = [sem(f"s_xi{i}") for i in range(2)]
        s_rw, s_mx, s_x2, s_sq, s_h2, s_h2t, s_h2c, s_rt, s_sg = (sem(n) for n in (
            "s_rw", "s_mx", "s_x2", "s_sq", "s_h2", "s_h2t", "s_h2c", "s_rt", "s_sg"))
        s_so = [sem(f"s_so{i}") for i in range(2)]
        s_sel, s_pos, s_pm, s_cn, s_tab = (sem(n) for n in ("s_sel", "s_pos", "s_pm", "s_cn", "s_tab"))
        s_H, s_si, s_hd, s_ht, s_hc, s_sO, s_ya, s_yv = (sem(n) for n in ("s_H", "s_si", "s_hd", "s_ht", "s_hc", "s_sO", "s_ya", "s_yv"))
        s_ys = [sem(f"s_ys{i}") for i in range(2)]
        e_w = [sem(f"e_w{b}") for b in range(2)]
        e_clear = sem("e_clear")
        e_dma = sem("e_dma")
        f_y, f_o = [sem(f"f_y{j}") for j in range(4)], [sem(f"f_o{j}") for j in range(4)]
        f_s = sem("f_s")
        early.close()
        three = lambda n: [sem(f"e_{n}{j}") for j in range(3)]
        e_xg, e_sc = three("xg"), three("sc")
        e_oh, e_lst, e_idx, e_T, e_xT, e_H, e_si, e_hid, e_hT, e_hc, e_O, e_oba, e_obv = (
            three(n) for n in ("oh", "lst", "idx", "T", "xT", "H", "si", "hid", "hT", "hc", "O", "oba", "obv"))
        e_go = sem("e_go")

        class Chain:

            def __init__(self, eng, s):
                self.eng, self.s, self.n = eng, s, 0

            def __call__(self, ins):
                self.n += 1
                ins.then_inc(self.s, 1)
                self.eng.wait_ge(self.s, self.n)

        def block_ready(eng, b):
            n = sum(NDMA.get(f"{k}{j}", 1) for k, j in order[place[b] % 3:place[b] + 1:3])
            eng.wait_ge(s_ring[place[b] % 3], 16 * n)

        def block_done(eng, b):
            kind, j = b
            if kind == "ada":
                eng.wait_ge(s_mod, j + 1)
            elif kind == "w":
                eng.wait_ge(s_pj, 8 * (j + 1))
            elif kind == "wb":
                eng.wait_ge(s_br, 16 * (j + 1))
            else:
                eng.wait_ge(s_mx, NT)

        def rows_stored(eng, row, n):
            for r in range(max(row, row + n - 4), row + n):
                eng.wait_ge(s_st[r % 4], 16 * (r // 4 + 1))

        def rms_scale(link, ss, width, out_):
            v, n = nc.vector, ss.shape[1]
            x, y, z = (newton[:, j, 0:n] for j in range(3))
            link(v.tensor_scalar(x, ss, 1.0 / width, EPS, ALU.mult, ALU.add))
            link(v.tensor_scalar(y.bitcast(I32), x.bitcast(I32), 1, None, ALU.logical_shift_right))
            link(v.tensor_scalar(y.bitcast(I32), y.bitcast(I32), -1.0, float(0x5F3759DF), ALU.mult, ALU.add))
            for step in range(3):
                link(v.tensor_tensor(z, y, y, ALU.mult))
                link(v.tensor_tensor(z, z, x, ALU.mult))
                link(v.tensor_scalar(z, z, -0.5, 1.5, ALU.mult, ALU.add))
                link(v.tensor_tensor(out_ if step == 2 else y, y, z, ALU.mult))

        def done(eng, s, n):
            eng.wait_ge(s, n + 1)

        def all_done(eng, *items):
            for s, n in items:
                done(eng, s, n)
            eng.sem_inc(e_go, 1)

        def skipped(eng, s, n, k=1):
            done(eng, s, n)
            eng.sem_inc(s, k)

        NC = T // P
        ND = NC - 2
        block = ctx.enter_context(nc.Block())

        @block.sync
        def _(sp):
            for n in range(2):
                sp.dma_start(xs[:, 4 * n:4 * n + 4, :],
                             a["x"][0, 4 * P * n:4 * P * (n + 1), :].rearrange("(i p) d -> p i d", p=P)).then_inc(s_x[n], 16)
            for c0, n, name in ((0, FH, "ff"), (FH, 2 * MH, "mi")):
                sp.dma_start(wsm[:, :, c0:c0 + n],
                             w_in[:, col[name]:col[name] + n].rearrange("(k p) n -> p k n", p=P)).then_inc(s_wsm, 16)

            def load_block(n):
                kind, j = order[n]
                if n >= 3:
                    block_done(sp, order[n - 3])
                dst = ring[:, n % 3]
                if kind == "ada":
                    src = a["ada_w"][0][:, j * BW:(j + 1) * BW].rearrange("(k p) n -> p k n", p=P)
                elif kind == "w":
                    c0 = col[TBLOCKS[j]] if j < 10 else col["gates"] + BW * (j - 10)
                    src = w_in[:, c0:c0 + BW].rearrange("(k p) n -> p k n", p=P)
                elif kind == "wb":
                    src = a["w_branch"][0, j].rearrange("(k p) n -> p k n", p=P)
                    dst = flat(dst).rearrange("p (k n) -> p k n", k=4)
                elif kind == "wo":
                    src = a["w_out"][0][:, BW * j:BW * (j + 1)].rearrange("(k p) n -> p k n", p=P)
                elif j == 0:
                    sp.dma_start(dst[:, :, 0:FF], a["sh_w1"][0].rearrange("(p k) f -> p k f", k=KD)).then_inc(s_ring[n % 3], 16)
                    src, dst = a["sh_w3"][0].rearrange("(p k) f -> p k f", k=KD), dst[:, :, FF:2 * FF]
                else:
                    src, dst = a["sh_w2"][0].rearrange("(k p) n -> p k n", p=P), shw2
                sp.dma_start(dst, src).then_inc(s_ring[n % 3], 16)

            nxt = 0

            def store_rows(u):
                sp.wait_ge(s_ev, u + 1)
                sp.dma_start(proj_d[u - U_B], stg[u % 4]).then_inc(s_st[(u - U_B) % 4], 16)

            for u in range(U_B, NU + 1):
                while nxt < len(order) - 1 and (nxt < 3 or order[nxt - 3][0] == "ada" or
                                                (order[nxt - 3][0] == "w" and 8 * order[nxt - 3][1] + 7 <= u)):
                    load_block(nxt)
                    nxt += 1
                if u < NU:
                    store_rows(u)
            while nxt < len(order) - 1:
                load_block(nxt)
                nxt += 1
            for i in range(NT):
                sp.wait_ge(s_x2, i + 1)
                sp.dma_start(x2_d[i * P:(i + 1) * P, :], x2[i % 2]).then_inc(s_so[i % 2], 16)
                sp.wait_ge(s_h2, i + 1)
                sp.dma_start(h2_d[i * P:(i + 1) * P, :], h2[i % 2]).then_inc(s_so[i % 2], 16)
            load_block(len(order) - 1)

            def load_expert(e, b):
                sp.dma_start(w13[b][:, :, 0:FF], a["exp_w1"][0, e].rearrange("(p k) f -> p k f", k=KD)).then_inc(e_w[b], 16)
                sp.dma_start(w13[b][:, :, FF:2 * FF], a["exp_w3"][0, e].rearrange("(p k) f -> p k f", k=KD)).then_inc(e_w[b], 16)
                sp.dma_start(w2[b], a["exp_w2"][0, e].rearrange("(k p) n -> p k n", p=P)).then_inc(e_w[b], 16)

            for b in range(2):
                load_expert(b, b)
            for i in range(NT):
                sp.wait_ge(s_ya, i + 1)
                sp.wait_ge(s_yv, i + 1)
                if i == 0:
                    sp.dma_start(y_d[T:T + P, :], ysh[0]).then_inc(s_ys[0], 16)
                sp.dma_start(y_d[i * P:(i + 1) * P, :], ysh[i % 2]).then_inc(s_ys[i % 2], 16)
            sp.wait_ge(e_clear, 1)
            with sp.Fori(1, NE // 2) as it:
                for b in range(2):
                    e = 2 * it + b
                    for j, n in ((0, e - 1), (1, e - 1), (2, ND * (e - 1))):
                        done(sp, e_oba[j], n)
                        done(sp, e_obv[j], n)
                    load_expert(e, b)
            for j, n in ((0, NE), (1, NE), (2, ND * NE)):
                done(sp, e_sc[j], n)
            for i in range(NT):
                if i >= 4:
                    sp.wait_ge(f_o[i % 4], 16 * (i // 4))
                sp.dma_start(fy[i % 4], y_d[i * P:(i + 1) * P, :]).then_inc(f_y[i % 4], 16)
                sp.dma_start(fx[i % 4], x2_d[i * P:(i + 1) * P, :]).then_inc(f_y[i % 4], 16)
            for j in range(4):
                sp.wait_ge(f_o[j], 16 * (NT // 4))

        @block.gpsimd
        def _(pool):
            g = nc.gpsimd
            link = Chain(pool, s_pool)
            g.iota(sI, pattern=[[0, P]], base=0, channel_multiplier=1).then_inc(s_iota, 1)
            g.iota(tI, pattern=[[1, P]], base=0, channel_multiplier=0).then_inc(s_iota, 1)
            g.iota(tokI, pattern=[[P, NT]], base=-FAR, channel_multiplier=1).then_inc(s_iota, 1)
            link(g.memset(ident[:, :], 0.0))
            link(g.memset(ones[:, :], 1.0))
            link(g.memset(foxmask[:, :], 0.0))
            g.affine_select(out=ident[:, :], in_=ident[:, :], compare_op=ALU.not_equal, fill=1.0, base=0,
                            pattern=[[-1, P]], channel_multiplier=1).then_inc(s_pconst, 1)
            g.affine_select(out=upper[:, :], in_=ones[:, :], compare_op=ALU.is_ge, fill=0.0, base=0,
                            pattern=[[1, P]], channel_multiplier=-1).then_inc(s_pconst, 1)
            g.affine_select(out=strict[:, :], in_=ones[:, :], compare_op=ALU.is_ge, fill=0.0, base=-1,
                            pattern=[[1, P]], channel_multiplier=-1).then_inc(s_pconst, 1)
            g.affine_select(out=foxmask[:, :], in_=foxmask[:, :], compare_op=ALU.is_ge, fill=NEG, base=0,
                            pattern=[[-1, P]], channel_multiplier=1).then_inc(s_pconst, 1)
            pool.wait_ge(s_fr, 1)
            g.dma_start(frow_d, R[2][0:FH, :]).then_inc(s_rd, 16)
            pool.wait_ge(s_mr, 1)
            g.dma_start(mrow_d, R[7][0:MH, :]).then_inc(s_rd, 16)
            pool.wait_ge(s_mf, 1)
            g.dma_start(mdec_d, R[1][0:MH, 0:NT]).then_inc(s_rd, 16)
            pool.wait_ge(s_rd, 48)
            g.dma_start(mdec[:, :, :], mdec_d.partition_broadcast(P)).then_inc(s_rd, 16)
            pool.wait_ge(s_mct, 1)
            for h in range(FH):
                if h >= 2:
                    pool.wait_ge(s_pl, NT * (h - 1))
                g.dma_start(ncb[h % 2], frow_d[h:h + 1, :].partition_broadcast(P).rearrange("b o t -> b (o t)")
                            ).then_inc(s_nc[h % 2], 16)
            pool.wait_ge(s_y, FSTEPS)
            for j in range(2):
                g.memset(conv_in[j][:, 0:TAPS - 1], 0.0).then_inc(s_pad, 1)
            rows_stored(pool, R_MO, 8)
            g.dma_start(mo, proj_d[R_MO:R_MO + 8].rearrange("r p n -> p r n")).then_inc(s_mo, 16)
            for j in range(4):
                if j >= 2:
                    pool.wait_ge(s_cv, j - 1)
                if j == 0:
                    pool.wait_ge(s_pad, 2)
                rows_stored(pool, R_MQK + 2 * j, 2)
                g.dma_start(conv_in[j % 2][:, TAPS - 1:TAPS - 1 + T].rearrange("p (r n) -> p r n", r=2),
                            proj_d[R_MQK + 2 * j:R_MQK + 2 * j + 2].rearrange("r p n -> p r n")).then_inc(s_cin[j % 2], 16)
            pool.wait_ge(s_fyt, NT)
            g.memset(vaug[:, :, :, MV:MV + 1], 1.0).then_inc(s_pad, 1)
            rows_stored(pool, R_MV, 8)
            for i in range(NT):
                g.dma_start(vaug[:, i, :, 0:MV], proj_d[R_MV + i].rearrange("p (h v) -> p h v", h=MH)).then_inc(s_va, 16)
            pool.wait_ge(s_cv, 4)
            g.memset(mC, 0.0).then_inc(s_pad, 1)

            def spread_m(c):
                g.dma_start(nmb[c % 2], mrow_d[:, c * P:(c + 1) * P].partition_broadcast(P)).then_inc(s_nm[c % 2], 16)

            spread_m(0)
            spread_m(1)
            for c in range(NT):
                pool.wait_ge(m_e, c + 1)
                g.tensor_tensor(mw, mw, upper[:, :].unsqueeze(1).to_broadcast([P, MH, P]), ALU.mult).then_inc(m_k, 1)
                if c + 2 < NT:
                    pool.wait_ge(m_w, c + 1)
                    spread_m(c + 2)
            def load_zq(h):
                for dst, r in ((hz, R_HF), (hq, R_HQ)):
                    g.dma_start(dst.rearrange("p (r n) -> p r n", r=2),
                                proj_d[r + 2 * h:r + 2 * h + 2].rearrange("r p n -> p r n")).then_inc(h_zq, 16)

            def load_vg(h):
                for dst, r in ((hv, R_HI), (hg, R_HG)):
                    g.dma_start(dst.rearrange("p (r n) -> p r n", r=NT),
                                proj_d[r:r + NT, :, h * P:(h + 1) * P].rearrange("r p n -> p r n")).then_inc(h_vg, 16)

            pool.wait_ge(m_yt, NT)
            pool.wait_ge(m_st, NT)
            load_zq(0)
            load_vg(0)
            for h in range(1, HH):
                pool.wait_ge(h_S, 8 * h)
                load_zq(h)
                pool.wait_ge(h_y, h)
                load_vg(h)
            pool.wait_ge(h_yt, HH)
            for n in range(48):
                br, j, half = n // 16, n // 2 % 8, n % 2
                row = R_G + (br * 2 + j // 4) * 8 + (j % 4) * 2 + half
                if n >= 3:
                    pool.wait_ge(s_pr, n - 2)
                rows_stored(pool, row, 1)
                g.dma_start(gt[n % 3], proj_d[row]).then_inc(s_g[n % 3], 16)
            pool.wait_ge(s_mg, 32)
            g.dma_start(rwt, a["router_w"][0].rearrange("(p k) e -> p k e", k=KD)).then_inc(s_rw, 16)
            pool.wait_ge(s_bc, 8)
            g.dma_start(rbias, a["router_bias"][0:1, :].partition_broadcast(P).rearrange("b o e -> b (o e)")).then_inc(s_rw, 16)
            for i in range(NT):
                if i >= 2:
                    pool.wait_ge(s_x2, i - 1)
                g.dma_start(xin[i % 2], a["x"][0, i * P:(i + 1) * P, :]).then_inc(s_xi[i % 2], 16)
            pool.wait_ge(s_sO, NT)
            pool.wait_ge(s_ys[0], 16 * (NT // 2 + 1))
            pool.wait_ge(s_ys[1], 16 * (NT // 2))
            pool.wait_ge(s_so[0], 16 * NT)
            pool.wait_ge(s_so[1], 16 * NT)
            pool.wait_ge(s_ya, NT)
            pool.wait_ge(s_yv, NT)
            for q in (e_oh, e_lst, e_idx, e_xg, e_T, e_xT, e_H, e_si, e_hid, e_hT, e_hc, e_O, e_oba, e_obv, e_sc):
                for j in range(3):
                    pool.sem_clear(q[j])
            pool.sem_clear(e_go)
            pool.sem_inc(e_clear, 1)
            for j in range(3):
                link(g.memset(xg[j], 0.0))
            for q in (e_xg[1:], e_sc):
                for x in q:
                    pool.sem_inc(x, 1)

            def gather(j, b):
                return g.indirect_dma_start(xg[j], None, h2_d, bass.IndirectOffsetOnAxis(ap=idx[:, 2 * j + b:2 * j + b + 1], axis=0),
                                            bounds_check=T - 1, oob_is_err=False)

            landings = pool.alloc_register("landings")
            pool.reg_mov(landings, 0)

            def landed(s):
                pool.reg_add(landings, landings, 16)
                pool.wait_ge(e_dma, pool.snap(landings))
                pool.sem_inc(s, 1)

            def scatter(j, b):
                g.indirect_dma_start(y_d, bass.IndirectOffsetOnAxis(ap=idx[:, 2 * j + b:2 * j + b + 1], axis=0), ob[j], None,
                                     bounds_check=T + P - 1, oob_is_err=True, compute_op=ALU.add).then_inc(e_dma, 16)

            done(pool, e_idx[0], 1)
            done(pool, e_idx[1], 1)
            gather(0, 0).then_inc(e_xg[0], 16)
            gather(1, 0).then_inc(e_dma, 16)
            landed(e_xg[1])
            with pool.Fori(0, NE // 2) as it:
                for b in range(2):
                    e = 2 * it + b
                    n_e = pool.value_load(cnt[0:1, bass.ds(e, 1)], min_val=0, max_val=T)
                    n_next = pool.value_load(cnt[0:1, bass.ds(e + 1, 1)], min_val=0, max_val=T)
                    all_done(pool, (e_idx[0], e + 2), (e_T[0], e + 1))
                    gather(0, 1 - b).then_inc(e_xg[0], 16)
                    all_done(pool, (e_T[1], e + 1), (e_idx[1], e + 2))
                    with pool.If(n_next > P):
                        gather(1, 1 - b).then_inc(e_dma, 16)
                        landed(e_xg[1])
                    with pool.Else():
                        pool.sem_inc(e_xg[1], 1)
                    all_done(pool, (e_oba[0], e + 1), (e_obv[0], e + 1))
                    scatter(0, b)
                    landed(e_sc[0])
                    with pool.If(n_e > P):
                        all_done(pool, (e_oba[1], e + 1), (e_obv[1], e + 1))
                        scatter(1, b)
                        landed(e_sc[1])
                    with pool.Else():
                        pool.sem_inc(e_sc[1], 1)
                    with pool.If(n_e > 2 * P):
                        with pool.Fori(0, ND) as c:
                            n = ND * e + c
                            with pool.If(n_e > P * (c + 2)):
                                all_done(pool, (e_idx[2], n + 1), (e_T[2], n))
                                gather(2, 0).then_inc(e_dma, 16)
                                landed(e_xg[2])
                                all_done(pool, (e_oba[2], n + 1), (e_obv[2], n + 1))
                                scatter(2, 0)
                                landed(e_sc[2])
                            with pool.Else():
                                pool.sem_inc(e_xg[2], 1)
                                pool.sem_inc(e_sc[2], 1)
                            pool.nop()
                    with pool.Else():
                        pool.sem_inc(e_xg[2], ND)
                        pool.sem_inc(e_sc[2], ND)
                    pool.nop()

        @block.tensor
        def _(pe):
            t = nc.tensor

            def ada(j):
                block_ready(pe, ("ada", j))
                pe.wait_ge(s_cond, 1)
                if j > 0:
                    pe.wait_ge(s_modc, j)
                w = slot(("ada", j))
                for c in range(4):
                    for k in range(KD):
                        mm = t.matmul(psum[:, 7, 4 * j + c:4 * j + c + 1], w[:, k, c * P:(c + 1) * P], cond[:, k:k + 1],
                                      start=(k == 0), stop=(k == KD - 1))
                mm.then_inc(s_mod, 1)

            def project(u):
                q, v = divmod(u, 8)
                if v == 0:
                    block_ready(pe, ("w", q))
                if u >= 3:
                    pe.wait_ge(s_ev, u - 2)
                w = slot(("w", q))
                for k in range(KD):
                    if q in TRANSPOSED:
                        l, r = w[:, k, (v // 2) * P:(v // 2 + 1) * P], hT[:, k, (v % 2) * BW:(v % 2 + 1) * BW]
                    else:
                        l, r = hT[:, k, v * P:(v + 1) * P], w[:, k, :]
                    mm = t.matmul(bank(u % 3), l, r, start=(k == 0), stop=(k == KD - 1))
                mm.then_inc(s_pj, 1)

            pe.wait_ge(s_vec, 16 * 6)
            pe.wait_ge(s_pconst, 4)
            t.transpose(psum[:, 6, 0:88], vrow[0:88, :], ident[0:88, 0:88]).then_inc(s_vt, 1)
            for j in range(4):
                ada(j)
            for i in range(NT):
                pe.wait_ge(s_xn, i + 1)
                if i >= 2:
                    pe.wait_ge(s_xea, i - 1)
                    pe.wait_ge(s_xed, i - 1)
                for k in range(KD):
                    mm = t.transpose(psum[:, 2 * (i % 2) + k // 4, (k % 4) * P:(k % 4 + 1) * P],
                                     xn[:, i, k * P:(k + 1) * P], ident[:, :])
                mm.then_inc(s_xt, 1)
            pe.wait_ge(s_xea, NT)
            pe.wait_ge(s_xed, NT)
            pe.wait_ge(s_wsm, 32)
            for i in range(NT):
                for k in range(KD):
                    mm = t.matmul(psum[:, 4, i * 16:(i + 1) * 16], hT[:, k, i * P:(i + 1) * P], wsm[:, k, :],
                                  start=(k == 0), stop=(k == KD - 1))
            mm.then_inc(s_sm, 1)
            pe.wait_ge(s_smc, 1)
            for c0, n, b0 in ((0, FH, 0), (FH, MH, 2), (FH + MH, MH, 4)):
                for i in range(NT):
                    mm = t.transpose(psum[0:n, b0 + i // 4, (i % 4) * P:(i % 4 + 1) * P], sm[:, i, c0:c0 + n], ident[:, :])
            mm.then_inc(s_rows, 1)
            pe.wait_ge(s_zr, 3)

            def turn_qk(u):
                pe.wait_ge(s_qn, u + 1)
                if u >= 1:
                    pe.wait_ge(s_qe, u)
                for j in range(4):
                    mm = t.transpose(psum[:, 4, j * P:(j + 1) * P], qn[u % 2][:, j * P:(j + 1) * P], ident[:, :])
                mm.then_inc(s_qt, 1)

            for u in range(U_B):
                project(u)
                if 2 <= u < 18:
                    turn_qk(u - 2)
                if u % 8 == 7:
                    for j in (4, 5, 6) if u == 7 else (7, 8, 9) if u == 15 else (10, 11):
                        ada(j)
                if u == 18:
                    pe.wait_ge(s_mf, 1)
                    for q in range(4):
                        for i in range(NT):
                            mm = t.transpose(psum[:, 5, (q * NT + i) * MH:(q * NT + i + 1) * MH],
                                             R[[5, 6, 8, 9][q]][0:MH, i * P:(i + 1) * P], ident[0:MH, 0:MH])
                    mm.then_inc(s_mct, 1)
            pe.wait_ge(s_mcc, 1)
            pe.wait_ge(s_modc, 12)
            pe.wait_ge(s_qe, 16)
            pe.wait_ge(s_ev, U_B)

            def logits(n):
                h, i = divmod(n, NT)
                b, j, N = FD * (h % 2), h // 2, P * (i + 1)
                if n >= 1:
                    pe.wait_ge(s_pl, n)
                for z in range(-(-N // BW)):
                    m = min(BW, N - BW * z)
                    mm = t.matmul(psum[:, 4 + z, 0:m], qT[b:b + FD, j, i * P:(i + 1) * P],
                                  kT[b:b + FD, j, BW * z:BW * z + m], start=True, stop=True)
                mm.then_inc(s_S, 1)

            def turn_p(n):
                pe.wait_ge(s_p, n + 1)
                if n >= 1:
                    pe.wait_ge(s_pT, n)
                for s in range(n % NT + 1):
                    mm = t.transpose(psum[:, 6 + s // 4, (s % 4) * P:(s % 4 + 1) * P], pl[n % 2][:, s * P:(s + 1) * P], ident[:, :])
                mm.then_inc(s_T, 1)

            def weigh(n):
                h, i = divmod(n, NT)
                pe.wait_ge(s_pT, n + 1)
                if n >= 1:
                    pe.wait_ge(s_y, n)
                for s in range(i + 1):
                    mm = t.matmul(psum[:, 3, 0:FD], pT[n % 2][:, s, :], vf[:, s, h * FD:(h + 1) * FD],
                                  start=(s == 0), stop=(s == i))
                mm.then_inc(s_O, 1)

            for m in range(FSTEPS + 2):
                if m < U_C - U_B:
                    project(U_B + m)
                if m < FSTEPS:
                    logits(m)
                if 1 <= m < FSTEPS + 1:
                    turn_p(m - 1)
                if m >= 2:
                    weigh(m - 2)

            nu = U_C

            def turn4(b, src, s):
                for j in range(4):
                    mm = t.transpose(psum[:, b, j * P:(j + 1) * P], src[:, j * P:(j + 1) * P], ident[:, :])
                mm.then_inc(s, 1)

            pe.wait_ge(s_y, FSTEPS)
            for i in range(NT):
                if i >= 2:
                    pe.wait_ge(s_fyc, i - 1)
                turn4(3 + i % 2, yf[:, i, :], s_fyt)
                if i % 2 == 0:
                    project(nu)
                    nu += 1
            pe.wait_ge(s_fyc, NT)

            def ml_scores(c):
                if c >= 1:
                    pe.wait_ge(m_st, c)
                    pe.wait_ge(m_in, c)
                else:
                    pe.wait_ge(s_sil, 4)
                for j in range(2):
                    t.transpose(psum[:, 3, j * P:(j + 1) * P], mqkT[:, 2 + j, c * P:(c + 1) * P], ident[:, :])
                for h in range(MH):
                    b, j = MQ * (h % 2), h // 2
                    mm = t.matmul(psum[:, (4, 7)[h % 2], j * P:(j + 1) * P], mqkT[b:b + MQ, 2 + j, c * P:(c + 1) * P],
                                  mqkT[b:b + MQ, j, c * P:(c + 1) * P], start=True, stop=True)
                mm.then_inc(m_ST, 1)

            def ml_apply(c):
                pe.wait_ge(m_sc, c + 1)
                pe.wait_ge(m_kw, c + 1)
                if c == 0:
                    pe.wait_ge(s_va, 16 * NT)
                    pe.wait_ge(s_pad, 4)
                else:
                    pe.wait_ge(m_st, c)
                    pe.wait_ge(m_num, c)
                    pe.wait_ge(m_yc, c)
                M1 = MV + 1
                for h in range(MH):
                    b, j, o = MQ * (h % 2), h // 2, (h % 2) * M1
                    t.matmul(psum[:, 5 + j, o:o + M1], msc[:, h, :], vaug[:, c, h, :], start=True, stop=True)
                    t.matmul(psum[:, (4, 7)[h % 2], j * M1:(j + 1) * M1], mqkT[b:b + MQ, j, c * P:(c + 1) * P], mC[b:b + MQ, j, :],
                             start=True, stop=True)
                for h in range(MH):
                    b, j = MQ * (h % 2), h // 2
                    mm = t.matmul(psum[b:b + MQ, 3, j * M1:(j + 1) * M1], mkw[:, h, :], vaug[:, c, h, :], start=True, stop=True)
                mm.then_inc(m_B, 1)

            for c in range(NT):
                if c % 2 == 0:
                    project(nu)
                    nu += 1
                ml_scores(c)
                if c >= 1:
                    pe.wait_ge(m_y, c)
                    turn4(5, my, m_yt)
                project(nu)
                nu += 1
                ml_apply(c)
            project(nu)
            nu += 1
            pe.wait_ge(m_y, NT)
            turn4(5, my, m_yt)
            pe.wait_ge(m_yc, NT)

            for h in range(HH):
                step = 0

                def between():
                    nonlocal nu, step
                    if (step % 3 != 2 or h == HH - 1) and nu < NU:
                        project(nu)
                        nu += 1
                    step += 1

                for l in range(8):
                    between()
                    n = 8 * h + l
                    pe.wait_ge(h_qk, n + 1)
                    if l >= 2:
                        pe.wait_ge(h_sc, n - 1)
                    elif h >= 1:
                        pe.wait_ge(h_yc, h) if l == 1 else pe.wait_ge(h_y, h)
                    b0 = 4 + 2 * (l % 2)
                    for c in range(NT):
                        cs = slice(c * P, (c + 1) * P)
                        if l < 7:
                            x, y = hE[l % 2][:, cs], hE[l % 2][:, cs]
                        else:
                            x, y = hk[:, cs], hq[:, cs]
                        mm = t.matmul(psum[:, b0 + c // 4, (c % 4) * P:(c % 4 + 1) * P], x, y, start=True, stop=True)
                    mm.then_inc(h_S, 1)
                between()
                pe.wait_ge(h_kd, h + 1)
                pe.wait_ge(h_sc, 8 * h + 7)
                for c in range(NT):
                    mm = t.transpose(psum[:, 4 + c // 4, (c % 4) * P:(c % 4 + 1) * P], hkd[:, c * P:(c + 1) * P], ident[:, :])
                mm.then_inc(h_kt, 1)
                between()
                pe.wait_ge(h_kc, h + 1)
                pe.wait_ge(h_vg, 32 * (h + 1))
                pe.wait_ge(h_sc, 8 * h + 8)
                for c in range(NT):
                    mm = t.matmul(psum[:, 6 + c // 4, (c % 4) * P:(c % 4 + 1) * P], hkT[:, c * P:(c + 1) * P],
                                  hv[:, c * P:(c + 1) * P], start=True, stop=True)
                mm.then_inc(h_up, 1)
                between()
                pe.wait_ge(h_st, h + 1)
                for c in range(NT):
                    cs = slice(c * P, (c + 1) * P)
                    o = psum[:, 4 + c // 4, (c % 4) * P:(c % 4 + 1) * P]
                    t.matmul(o, hsc[:, cs], hv[:, cs], start=True, stop=False)
                    mm = t.matmul(o, hqe[:, cs], hst[:, cs], start=False, stop=True)
                mm.then_inc(h_O, 1)
                between()
                pe.wait_ge(h_y, h + 1)
                for c in range(NT):
                    mm = t.transpose(psum[:, 6 + c // 4, (c % 4) * P:(c % 4 + 1) * P], hkT[:, c * P:(c + 1) * P], ident[:, :])
                mm.then_inc(h_yt, 1)
            assert nu == NU

            pe.wait_ge(h_yc, HH)
            pe.wait_ge(s_ev, NU)
            for n in range(48):
                br, j, half = n // 16, n // 2 % 8, n % 2
                if n % 16 == 0:
                    block_ready(pe, ("wb", br))
                w = flat(slot(("wb", br))).rearrange("p (k n) -> p k n", k=4)
                if n >= 3:
                    pe.wait_ge(s_pr, n - 2)
                for k in range(4):
                    mm = t.matmul(bank(n % 3), w[:, k, j * P:(j + 1) * P], yT[br][:, k, half * BW:(half + 1) * BW],
                                  start=(k == 0), stop=(k == 3))
                mm.then_inc(s_br, 1)
            for n in range(8):
                pe.wait_ge(s_dg, n + 1)
                if n >= 2:
                    pe.wait_ge(s_bcc, n - 1)
                t.matmul(bank(4 + n % 2), ones[:, :], dgb[n % 2].rearrange("p k n -> p (k n)"),
                         start=True, stop=True).then_inc(s_bc, 1)
            pe.wait_ge(s_mg, 32)
            pe.wait_ge(s_bcc, 8)

            def out_proj(i):
                if i == 0:
                    block_ready(pe, ("wo", 0))
                    block_ready(pe, ("wo", 1))
                if i >= 2:
                    pe.wait_ge(s_x2, i - 1)
                for half in range(2):
                    for k in range(KD):
                        mm = t.matmul(bank(2 * (i % 2) + half), hT[:, k, i * P:(i + 1) * P], slot(("wo", half))[:, k, :],
                                      start=(k == 0), stop=(k == KD - 1))
                mm.then_inc(s_mx, 1)

            def route(i):
                pe.wait_ge(s_h2, i + 1)
                if i >= 1:
                    pe.wait_ge(s_h2c, i)
                for k in range(KD):
                    mm = t.transpose(psum[:, 4 + k // 4, (k % 4) * P:(k % 4 + 1) * P], h2[i % 2][:, k * P:(k + 1) * P], ident[:, :])
                mm.then_inc(s_h2t, 1)
                pe.wait_ge(s_h2c, i + 1)
                pe.wait_ge(s_rw, 32)
                if i >= 1:
                    pe.wait_ge(s_sg, i)
                for k in range(KD):
                    mm = t.matmul(psum[:, 6, 0:NE], h2T[:, k, i * P:(i + 1) * P], rwt[:, k, :], start=(k == 0), stop=(k == KD - 1))
                mm.then_inc(s_rt, 1)

            def rank(i):
                pe.wait_ge(s_sel, i + 1)
                if i >= 1:
                    pe.wait_ge(s_pm, i)
                for j in range(i + 1):
                    mm = t.matmul(psum[:, 7, 0:NE], strict[:, :] if j == i else ones[:, :], selall[:, j, :],
                                  start=(j == 0), stop=(j == i))
                mm.then_inc(s_pos, 1)

            for i in range(NT + 2):
                if i < NT:
                    out_proj(i)
                if 1 <= i <= NT:
                    route(i - 1)
                if i >= 2:
                    rank(i - 2)
            pe.wait_ge(s_pm, NT)
            for j in range(NT):
                mm = t.matmul(psum[:, 7, 0:NE], ones[:, :], selall[:, j, :], start=(j == 0), stop=(j == NT - 1))
            mm.then_inc(s_cn, 1)

            def shared_up(i):
                if i == 0:
                    block_ready(pe, ("sh", 0))
                    pe.wait_ge(s_x2, NT)
                if i >= 2:
                    pe.wait_ge(s_hd, i - 1)
                for k in range(KD):
                    mm = t.matmul(bank(i % 2), h2T[:, k, i * P:(i + 1) * P], slot(("sh", 0))[:, k, :], start=(k == 0), stop=(k == KD - 1))
                mm.then_inc(s_H, 1)

            def shared_down(i):
                pe.wait_ge(s_hd, i + 1)
                if i >= 1:
                    pe.wait_ge(s_hc, i)
                for k in range(FK):
                    mm = t.transpose(psum[:, 2, k * P:(k + 1) * P], shh[:, k * P:(k + 1) * P], ident[:, :])
                mm.then_inc(s_ht, 1)
                pe.wait_ge(s_hc, i + 1)
                if i == 0:
                    block_ready(pe, ("sh", 1))
                    pe.wait_ge(s_h2c, NT)
                if i >= 1:
                    pe.wait_ge(s_ya, i)
                    pe.wait_ge(s_yv, i)
                for half in range(2):
                    for k in range(FK):
                        mm = t.matmul(bank(4 + half), shT[:, k, :], shw2[:, k, half * BW:(half + 1) * BW],
                                      start=(k == 0), stop=(k == FK - 1))
                mm.then_inc(s_sO, 1)

            shared_up(0)
            for i in range(NT):
                if i + 1 < NT:
                    shared_up(i + 1)
                shared_down(i)

            def token_list(j, e):
                for i in range(NT):
                    mm = t.matmul(psum[:, 2, 8 * j:8 * j + 2], oh[j][:, i, :], tw[:, i, bass.ds(e, 1), :].rearrange("p o n -> p (o n)"),
                                  start=(i == 0), stop=(i == NT - 1))
                mm.then_inc(e_lst[j], 1)

            def turn_rows(j):
                for k in range(KD):
                    mm = t.transpose(psum[:, k // 4, (k % 4) * P:(k % 4 + 1) * P], xg[j][:, k * P:(k + 1) * P], ident[:, :])
                mm.then_inc(e_T[j], 1)

            def up(j, b):
                for k in range(KD):
                    mm = t.matmul(bank(3 if j == 0 else 4), xgT[j][:, k, :], w13[b][:, k, :], start=(k == 0), stop=(k == KD - 1))
                mm.then_inc(e_H[j], 1)

            def turn_hidden(j):
                for k in range(FK):
                    mm = t.transpose(psum[:, 5, k * P:(k + 1) * P], hid[j][:, k * P:(k + 1) * P], ident[:, :])
                mm.then_inc(e_hT[j], 1)

            def down(j, b):
                for half in range(2):
                    for k in range(FK):
                        mm = t.matmul(bank(6 + half), hidT[j][:, k, :], w2[b][:, k, half * BW:(half + 1) * BW],
                                      start=(k == 0), stop=(k == FK - 1))
                mm.then_inc(e_O[j], 1)

            pe.wait_ge(s_tab, 1)
            pe.wait_ge(s_ya, NT)
            pe.wait_ge(s_yv, NT)
            pe.wait_ge(e_clear, 1)
            for s in (e_lst, e_T, e_H, e_hT, e_O):
                for j in range(3):
                    pe.sem_inc(s[j], 1)
            for j in range(2):
                done(pe, e_oh[j], 1)
                token_list(j, 0)
            pe.wait_ge(e_xg[0], 16)
            turn_rows(0)
            done(pe, e_xg[1], 1)
            with pe.Fori(0, NE // 2) as it:
                for b in range(2):
                    e = 2 * it + b
                    n_e = pe.value_load(cnt[0:1, bass.ds(e, 1)], min_val=0, max_val=T)
                    n_next = pe.value_load(cnt[0:1, bass.ds(e + 1, 1)], min_val=0, max_val=T)
                    done(pe, e_oh[0], e + 2)
                    done(pe, e_idx[0], e + 1)
                    done(pe, e_idx[1], e + 1)
                    done(pe, e_idx[2], ND * e)
                    token_list(0, e + 1)
                    with pe.If(n_next > P):
                        done(pe, e_oh[1], e + 2)
                        token_list(1, e + 1)
                    with pe.Else():
                        skipped(pe, e_lst[1], e + 1)
                    all_done(pe, (e_xT[0], e + 1), (e_xT[2], ND * e))
                    with pe.If(n_e > P):
                        done(pe, e_xg[1], e + 1)
                        turn_rows(1)
                    with pe.Else():
                        skipped(pe, e_T[1], e)
                    pe.wait_ge(e_w[b], 48 * (it + 1))
                    done(pe, e_hid[0], e)
                    up(0, b)
                    with pe.If(n_e > P):
                        done(pe, e_xT[1], e + 1)
                        done(pe, e_hid[1], e)
                        done(pe, e_hid[2], ND * e)
                        up(1, b)
                    with pe.Else():
                        skipped(pe, e_H[1], e)
                    pe.wait_ge(e_xg[0], 16 * (e + 2))
                    done(pe, e_xT[1], e + 1)
                    turn_rows(0)
                    done(pe, e_hid[0], e + 1)
                    done(pe, e_hc[1], e)
                    done(pe, e_hc[2], ND * e)
                    turn_hidden(0)
                    done(pe, e_hc[0], e + 1)
                    for s in (e_oba, e_obv):
                        done(pe, s[1], e)
                        done(pe, s[2], ND * e)
                    down(0, b)
                    with pe.If(n_e > P):
                        done(pe, e_hid[1], e + 1)
                        turn_hidden(1)
                        done(pe, e_hc[1], e + 1)
                        done(pe, e_oba[0], e + 1)
                        done(pe, e_obv[0], e + 1)
                        down(1, b)
                    with pe.Else():
                        skipped(pe, e_hT[1], e)
                        skipped(pe, e_O[1], e)
                    with pe.If(n_e > 2 * P):
                        all_done(pe, (e_xT[0], e + 2), (e_idx[0], e + 2), (e_idx[1], e + 2), (e_oba[1], e + 1), (e_obv[1], e + 1),
                                 (e_hid[1], e + 1))
                        with pe.Fori(0, ND) as c:
                            n = ND * e + c
                            with pe.If(n_e > P * (c + 2)):
                                done(pe, e_oh[2], n + 1)
                                token_list(2, e)
                                done(pe, e_xg[2], n + 1)
                                done(pe, e_xT[2], n)
                                turn_rows(2)
                                done(pe, e_xT[2], n + 1)
                                done(pe, e_hid[2], n)
                                up(2, b)
                                done(pe, e_hid[2], n + 1)
                                turn_hidden(2)
                                done(pe, e_hc[2], n + 1)
                                done(pe, e_oba[2], n)
                                done(pe, e_obv[2], n)
                                down(2, b)
                            with pe.Else():
                                for q in (e_lst, e_T, e_H, e_hT, e_O):
                                    skipped(pe, q[2], n)
                            pe.nop()
                    with pe.Else():
                        for q in (e_lst, e_T, e_H, e_hT, e_O):
                            skipped(pe, q[2], ND * e, ND)
                    pe.nop()

        @block.scalar
        def _(act):
            s = nc.scalar
            link = Chain(act, s_act)
            rows = lambda v, r: v.rearrange("o (r p) -> (o r) p", r=r)
            act.dma_start(vrow[0:48, :], rows(a["ada_b"], 48)).then_inc(s_vec, 16)
            act.dma_start(vrow[48:56, :], rows(a["norm1_g"], 8)).then_inc(s_vec, 16)
            act.dma_start(vrow[56:64, :], rows(a["norm2_g"], 8)).then_inc(s_vec, 16)
            act.dma_start(vrow[64:72, :], rows(a["c"], 8)).then_inc(s_vec, 16)
            act.dma_start(vrow[72:88, :], a["mlstm_conv"][0].rearrange("w (r p) -> (w r) p", p=P)).then_inc(s_vec, 16)
            act.dma_start(bff[:, :], a["fox_bf"].rearrange("o h -> h o")).then_inc(s_vec, 16)
            act.dma_start(bmi[:, :], a["mlstm_bi"].rearrange("o h -> h o")).then_inc(s_nd, 16)
            act.dma_start(bmf[:, :], a["mlstm_bf"].rearrange("o h -> h o")).then_inc(s_nd, 16)
            for dst, name in ((gq, "fox_q_g"), (gk, "fox_k_g"), (gml, "mlstm_norm_g"), (ghg, "hgrn_norm_g")):
                act.dma_start(dst[:, :], a[name].partition_broadcast(P).rearrange("b o n -> b (o n)")).then_inc(s_nd, 16)
            act.wait_ge(s_vc, 1)
            s.activation(cond[:, :], vcol[:, 64:72], ACT.Silu).then_inc(s_cond, 1)
            for i in range(NT):
                act.wait_ge(s_x[i // 4], 16)
                s.activation(xn[:, i, :], xs[:, i, :], ACT.Square, accum_out=stat[:, i:i + 1]).then_inc(s_ss, 1)
            act.wait_ge(s_a1, 1)
            for i in range(NT):
                act.wait_ge(s_xt, i + 1)
                for k in range(4):
                    ins = s.activation(hT[:, k, i * P:(i + 1) * P], psum[:, 2 * (i % 2), k * P:(k + 1) * P], ACT.Identity,
                                       bias=mod[:, k:k + 1], scale=a1[:, k:k + 1])
                ins.then_inc(s_xea, 1)

            for n, (z, o, h) in enumerate(((R[0], R[1], FH), (R[4], R[3], MH))):
                act.wait_ge(s_lr, n + 1)
                link(s.activation(o[0:h, :], z[0:h, :], ACT.Abs))
                link(s.activation(o[0:h, :], o[0:h, :], ACT.Exp, scale=-1.0))
                s.activation(o[0:h, :], o[0:h, :], ACT.Ln, bias=1.0).then_inc(s_er, 1)
            act.wait_ge(s_mr, 2)
            s.activation(R[6][0:MH, :], R[6][0:MH, :], ACT.Exp)
            s.activation(R[8][0:MH, :], R[8][0:MH, :], ACT.Exp, scale=-1.0)
            s.activation(R[1][0:MH, 0:NT], R[1][0:MH, 0:NT], ACT.Exp)
            s.activation(R[9][0:MH, :], R[9][0:MH, :], ACT.Exp).then_inc(s_mf, 1)

            def evacuate(u):
                act.wait_ge(s_pj, u + 1)
                if u < 16:
                    if u >= 2:
                        act.wait_ge(s_qn, u - 1)
                    dst = raw[u % 2]
                elif u < U_B:
                    dst = vf[:, u - 16, :]
                else:
                    dst = stg[u % 4]
                    if u >= U_B + 4:
                        act.wait_ge(s_st[(u - U_B) % 4], 16 * ((u - U_B) // 4))
                s.activation(dst, bank(u % 3), ACT.Copy).then_inc(s_ev, 1)

            def copy_qk(u):
                act.wait_ge(s_qt, u + 1)
                dst, i = (qT, kT)[u // 8], u % 8
                s.activation(dst[:, :, i * P:(i + 1) * P], bank(4).rearrange("p (j n) -> p j n", j=4), ACT.Copy).then_inc(s_qe, 1)

            for u in range(U_B):
                evacuate(u)
                if 2 <= u < 18:
                    copy_qk(u - 2)
                if u == 18:
                    act.wait_ge(s_mct, 1)
                    s.activation(mcol[:, :, :, :].rearrange("p q i h -> p (q i h)"), psum[:, 5, 0:4 * NT * MH], ACT.Copy).then_inc(s_mcc, 1)

            def fox_exp(n):
                N = P * (n % NT + 1)
                act.wait_ge(s_pl, n + 1)
                s.activation(pl[n % 2][:, 0:N], pl[n % 2][:, 0:N], ACT.Exp, bias=stat[:, 16 + n % 2:17 + n % 2],
                             accum_out=stat[:, 18 + n % 4:19 + n % 4]).then_inc(s_p, 1)

            def fox_turned(n):
                N = n % NT + 1
                act.wait_ge(s_T, n + 1)
                if n >= 2:
                    act.wait_ge(s_O, n - 1)
                s.activation(pT[n % 2][:, 0:N, :].rearrange("p s n -> p (s n)"),
                             psum[:, 6:8, :].rearrange("p b n -> p (b n)")[:, 0:N * P], ACT.Copy).then_inc(s_pT, 1)

            for m in range(FSTEPS + 1):
                if m < U_C - U_B:
                    evacuate(U_B + m)
                if m < FSTEPS:
                    fox_exp(m)
                if m >= 1:
                    fox_turned(m - 1)

            nu = U_C
            act.wait_ge(s_O, FSTEPS)
            for i in range(NT):
                act.wait_ge(s_fyt, i + 1)
                s.activation(yTf[:, :, i * P:(i + 1) * P], bank(3 + i % 2).rearrange("p (j n) -> p j n", j=4), ACT.Copy).then_inc(s_fyc, 1)
                if i % 2 == 0:
                    evacuate(nu)
                    nu += 1
            act.wait_ge(s_mo, 16)
            s.activation(mo, mo, ACT.Sigmoid).then_inc(s_mos, 1)
            for j in range(4):
                act.wait_ge(s_cv, j + 1)
                if j < 2:
                    s.activation(mqkT[:, j, :], mqkT[:, j, :], ACT.Silu).then_inc(s_sil, 1)
                else:
                    link(s.activation(mqkT[:, j, :], mqkT[:, j, :], ACT.Silu))
                    s.activation(mqkT[:, j, :], mqkT[:, j, :], ACT.Copy, scale=MQ ** -0.5).then_inc(s_sil, 1)

            def ml_exp(c):
                act.wait_ge(m_w, c + 1)
                s.activation(mw, mw, ACT.Exp).then_inc(m_e, 1)

            def ml_inter(c):
                act.wait_ge(m_B, c + 1)
                if c >= 1:
                    act.wait_ge(m_y, c)
                for h in range(MH):
                    o = (h // 2) * (MV + 1)
                    ins = s.activation(mnum[:, h, :], psum[:, (4, 7)[h % 2], o:o + MV + 1], ACT.Copy, scale=mcol[:, 1, c, h:h + 1])
                ins.then_inc(m_in, 1)

            def ml_turned(c):
                act.wait_ge(m_yt, c + 1)
                s.activation(yTm[:, :, c * P:(c + 1) * P], bank(5).rearrange("p (j n) -> p j n", j=4), ACT.Copy).then_inc(m_yc, 1)

            for c in range(NT):
                if c % 2 == 0:
                    evacuate(nu)
                    nu += 1
                ml_exp(c)
                if c >= 1:
                    ml_turned(c - 1)
                evacuate(nu)
                nu += 1
                ml_inter(c)
            evacuate(nu)
            nu += 1
            ml_turned(NT - 1)

            for h in range(HH):
                act.wait_ge(h_zq, 32 * (h + 1))
                act.wait_ge(h_vg, 32 * (h + 1))
                s.activation(hq, hq, ACT.Silu)
                link(s.activation(hg, hg, ACT.Silu))
                link(s.activation(hE0, hz, ACT.Abs))
                link(s.activation(hE0, hE0, ACT.Exp, scale=-1.0))
                s.activation(hE0, hE0, ACT.Ln, bias=1.0).then_inc(h_ab, 1)
                act.wait_ge(h_lf, h + 1)
                s.activation(hk, hk, ACT.Exp).then_inc(h_k, 1)
                act.wait_ge(h_a, h + 1)
                s.activation(hqe, ha, ACT.Exp).then_inc(h_ea, 1)
                act.wait_ge(h_d, h + 1)
                s.activation(hkd, hkd, ACT.Exp).then_inc(h_de, 1)
                step = 0
                for l in range(8):
                    if (step % 3 != 2 or h == HH - 1) and nu < NU:
                        evacuate(nu)
                        nu += 1
                    step += 1
                    if l < 7:
                        act.wait_ge(h_x, 7 * h + l + 1)
                        s.activation(hE[l % 2], hE[l % 2], ACT.Exp).then_inc(h_e, 1)
                for part in range(4):
                    if (step % 3 != 2 or h == HH - 1) and nu < NU:
                        evacuate(nu)
                        nu += 1
                    step += 1
                    if part == 0:
                        act.wait_ge(h_kt, h + 1)
                        s.activation(hkT, psum[:, 4:6, :].rearrange("p b n -> p (b n)"), ACT.Copy).then_inc(h_kc, 1)
                act.wait_ge(h_yt, h + 1)
                s.activation(yTh[:, h, :], psum[:, 6:8, :].rearrange("p b n -> p (b n)"), ACT.Copy).then_inc(h_yc, 1)

            for n in range(48):
                act.wait_ge(s_g[n % 3], 16 * (n // 3 + 1))
                s.activation(gt[n % 3], gt[n % 3], ACT.Sigmoid).then_inc(s_gs, 1)
            for n in range(8):
                act.wait_ge(s_bc, n + 1)
                v = (g1b, a2b, b2b, g2b)[n // 2]
                s.activation(v[:, (n % 2) * BW:(n % 2 + 1) * BW], bank(4 + n % 2), ACT.Copy).then_inc(s_bcc, 1)

            def squares(i):
                act.wait_ge(s_x2, i + 1)
                if i >= 1:
                    act.wait_ge(s_sq, i)
                s.activation(dsc, x2[i % 2], ACT.Square, accum_out=stat[:, 32 + i:33 + i]).then_inc(s_sq, 1)

            def routed(i):
                act.wait_ge(s_h2t, i + 1)
                s.activation(h2T[:, :, i * P:(i + 1) * P], psum[:, 4:6, :].rearrange("p b (k n) -> p (b k) n", k=4), ACT.Copy).then_inc(s_h2c, 1)
                act.wait_ge(s_rt, i + 1)
                if i >= 1:
                    act.wait_ge(s_sel, i)
                s.activation(sco, psum[:, 6, 0:NE], ACT.Sigmoid).then_inc(s_sg, 1)

            for i in range(NT + 1):
                if i < NT:
                    squares(i)
                if i >= 1:
                    routed(i - 1)
            for i in range(NT):
                act.wait_ge(s_H, i + 1)
                if i >= 1:
                    act.wait_ge(s_hd, i)
                s.activation(sgm, bank(i % 2)[:, 0:FF], ACT.Silu).then_inc(s_si, 1)
                act.wait_ge(s_ht, i + 1)
                if i >= 1:
                    act.wait_ge(s_sO, i)
                s.activation(shT.rearrange("p k n -> p (k n)"), psum[:, 2, 0:FF], ACT.Copy).then_inc(s_hc, 1)
                act.wait_ge(s_sO, i + 1)
                if i >= 2:
                    act.wait_ge(s_ys[i % 2], 16 * (i // 2 + 1 - i % 2))
                s.activation(ysh[i % 2][:, 0:BW], bank(4), ACT.Copy).then_inc(s_ya, 1)

            def rows_turned(j):
                s.activation(xgT[j].rearrange("p k n -> p (k n)"), psum[:, 0:2, :].rearrange("p b n -> p (b n)"), ACT.Copy).then_inc(e_xT[j], 1)

            def silu(j):
                s.activation(sg[j], bank(3 if j == 0 else 4)[:, 0:FF], ACT.Silu).then_inc(e_si[j], 1)

            def hidden_turned(j):
                s.activation(hidT[j].rearrange("p k n -> p (k n)"), psum[:, 5, 0:FF], ACT.Copy).then_inc(e_hc[j], 1)

            def weigh_out(j, b):
                s.activation(ob[j][:, 0:BW], bank(6), ACT.Copy, scale=wts[:, 2 * j + b:2 * j + b + 1]).then_inc(e_oba[j], 1)

            act.wait_ge(s_ys[0], 16 * (NT // 2 + 1))
            act.wait_ge(s_ys[1], 16 * (NT // 2))
            act.wait_ge(s_tab, 1)
            act.wait_ge(e_clear, 1)
            for q in (e_xT, e_si, e_hc, e_oba):
                for j in range(3):
                    act.sem_inc(q[j], 1)
            done(act, e_T[0], 1)
            rows_turned(0)
            with act.Fori(0, NE // 2) as it:
                for b in range(2):
                    e = 2 * it + b
                    n_e = act.value_load(cnt[0:1, bass.ds(e, 1)], min_val=0, max_val=T)
                    with act.If(n_e > P):
                        done(act, e_T[1], e + 1)
                        rows_turned(1)
                    with act.Else():
                        skipped(act, e_xT[1], e)
                    done(act, e_H[0], e + 1)
                    silu(0)
                    with act.If(n_e > P):
                        done(act, e_H[1], e + 1)
                        silu(1)
                    with act.Else():
                        skipped(act, e_si[1], e)
                    done(act, e_T[0], e + 2)
                    rows_turned(0)
                    done(act, e_hT[0], e + 1)
                    hidden_turned(0)
                    done(act, e_O[0], e + 1)
                    done(act, e_sc[0], e)
                    weigh_out(0, b)
                    with act.If(n_e > P):
                        done(act, e_hT[1], e + 1)
                        hidden_turned(1)
                        done(act, e_O[1], e + 1)
                        done(act, e_sc[1], e)
                        weigh_out(1, b)
                    with act.Else():
                        skipped(act, e_hc[1], e)
                        skipped(act, e_oba[1], e)
                    with act.If(n_e > 2 * P):
                        with act.Fori(0, ND) as c:
                            n = ND * e + c
                            with act.If(n_e > P * (c + 2)):
                                done(act, e_T[2], n + 1)
                                rows_turned(2)
                                done(act, e_H[2], n + 1)
                                silu(2)
                                done(act, e_hT[2], n + 1)
                                hidden_turned(2)
                                done(act, e_O[2], n + 1)
                                done(act, e_sc[2], n)
                                weigh_out(2, 0)
                            with act.Else():
                                for q in (e_xT, e_si, e_hc, e_oba):
                                    skipped(act, q[2], n)
                            act.nop()
                    with act.Else():
                        for q in (e_xT, e_si, e_hc, e_oba):
                            skipped(act, q[2], ND * e, ND)
                    act.nop()
            for i in range(NT):
                act.wait_ge(f_s, i + 1)
                act.dma_start(out[0, i * P:(i + 1) * P, :], fy[i % 4]).then_inc(f_o[i % 4], 16)
            for j in range(4):
                act.wait_ge(f_o[j], 16 * (NT // 4))

        @block.vector
        def _(dve):
            v = nc.vector
            link = Chain(dve, s_dve)

            dve.wait_ge(s_iota, 3)
            v.tensor_copy(col_i[:, :], tI)
            v.tensor_copy(tok[:, :], tokI)
            v.tensor_scalar(dump[:, :], sI[:, 0:1], float(T), None, ALU.add)
            link(v.tensor_tensor(xI, sI, tI, ALU.bitwise_xor))
            dve.wait_ge(s_pconst, 4)
            for l in range(7):
                link(v.tensor_scalar(shI, xI, l, None, ALU.logical_shift_right))
                link(v.tensor_scalar(eqf, shI, 1.0, None, ALU.is_equal))
                link(v.tensor_tensor(levels[:, l, :], eqf, upper[:, :], ALU.mult))
            v.tensor_copy(levels[:, 7, :], ident[:, :]).then_inc(s_dconst, 1)
            dve.wait_ge(s_nd, 16 * 6)
            link(v.tensor_scalar(gq[:, :], gq[:, :], FD ** -0.5, None, ALU.mult))
            dve.wait_ge(s_vt, 1)
            v.tensor_copy(vcol[:, :], psum[:, 6, 0:88]).then_inc(s_vc, 1)
            dve.wait_ge(s_vc, 1)
            dve.wait_ge(s_ss, NT)
            rms_scale(link, stat[:, 0:NT], D, stat[:, 8:8 + NT])
            for i in range(NT):
                v.tensor_scalar(xn[:, i, :], xs[:, i, :], stat[:, 8 + i:9 + i], None, ALU.mult).then_inc(s_xn, 1)

            def mod_columns(j):
                dve.wait_ge(s_mod, j + 1)
                v.tensor_tensor(mod[:, 4 * j:4 * j + 4], psum[:, 7, 4 * j:4 * j + 4], vcol[:, 4 * j:4 * j + 4], ALU.add).then_inc(s_modc, 1)

            for j in range(4):
                mod_columns(j)
            dve.wait_ge(s_modc, 4)
            v.scalar_tensor_tensor(out=a1[:, :], in0=mod[:, 8:16], scalar=1.0, in1=vcol[:, 48:56], op0=ALU.add, op1=ALU.mult).then_inc(s_a1, 1)
            dve.wait_ge(s_a1, 1)
            for i in range(NT):
                dve.wait_ge(s_xt, i + 1)
                for k in range(4, 8):
                    ins = v.tensor_scalar(hT[:, k, i * P:(i + 1) * P], psum[:, 2 * (i % 2) + 1, (k - 4) * P:(k - 3) * P],
                                          a1[:, k:k + 1], mod[:, k:k + 1], ALU.mult, ALU.add)
                ins.then_inc(s_xed, 1)
            dve.wait_ge(s_sm, 1)
            v.tensor_copy(sm[:, :, :].rearrange("p i n -> p (i n)"), psum[:, 4, 0:NT * 16]).then_inc(s_smc, 1)
            dve.wait_ge(s_rows, 1)
            dve.wait_ge(s_xea, NT)
            wide = lambda b, n: psum[0:n, b:b + 2, :].rearrange("p b n -> p (b n)")
            r = lambda j, n=MH: R[j][0:n, :]
            for j, b, n, bias in ((0, 0, FH, bff), (3, 2, MH, bmi), (4, 4, MH, bmf)):
                v.tensor_scalar(r(j, n), wide(b, n), bias[:, :], None, ALU.add).then_inc(s_zr, 1)
            dve.wait_ge(s_zr, 3)
            link(v.tensor_copy(r(7), r(3)))
            dve.sem_inc(s_lr, 2)

            def log_gate(j, l, o, n):
                link(v.scalar_tensor_tensor(out=r(o, n), in0=r(j, n), scalar=0.0, in1=r(l, n), op0=ALU.min, op1=ALU.subtract))

            dve.wait_ge(s_er, 1)
            log_gate(0, 1, 0, FH)
            link(v.memset(r(8, FH), 1.0))
            link(v.tensor_tensor_scan(out=r(2, FH), data0=r(8, FH), data1=r(0, FH), initial=0.0, op0=ALU.mult, op1=ALU.add))
            v.tensor_scalar(r(2, FH), r(2, FH), -1.0, None, ALU.mult).then_inc(s_fr, 1)
            dve.wait_ge(s_er, 2)
            log_gate(4, 3, 4, MH)
            link(v.tensor_tensor_scan(out=r(3), data0=r(8), data1=r(4), initial=0.0, op0=ALU.mult, op1=ALU.add))
            link(v.tensor_tensor(r(5), r(7), r(3), ALU.subtract))
            link(v.tensor_tensor_scan(out=r(4), data0=r(5), data1=r(5), initial=0.0, op0=ALU.max, op1=ALU.max))
            link(v.tensor_tensor(r(8), r(3), r(4), ALU.add))
            M3 = r(4).rearrange("p (c t) -> p c t", t=P)
            E0 = R[0][0:MH, 0:NT]
            E1 = R[0][0:MH, NT:2 * NT]
            link(v.memset(R[0][0:MH, 0:1], 0.0))
            link(v.tensor_copy(R[0][0:MH, 1:NT], M3[:, 0:NT - 1, P - 1:P].rearrange("p c o -> p (c o)")))
            link(v.tensor_copy(E1, M3[:, :, P - 1:P].rearrange("p c o -> p (c o)")))
            spread = lambda x: x.unsqueeze(2).to_broadcast([MH, NT, P])
            c3 = lambda x: x.rearrange("p (c t) -> p c t", t=P)
            link(v.tensor_tensor(c3(r(6)), spread(E0), M3, ALU.subtract))
            link(v.tensor_tensor(c3(r(9)), c3(r(5)), spread(E1), ALU.subtract))
            link(v.tensor_tensor(R[1][0:MH, 0:NT], E0, E1, ALU.subtract))
            link(v.tensor_scalar(r(7), r(4), -1.0, None, ALU.mult))
            dve.sem_inc(s_mr, 2)

            def normalise(u):
                gain = (gq, gk)[u // 8]
                x, y = raw[u % 2], qn[u % 2]
                x3, y3 = (z.rearrange("p (h d) -> p h d", d=FD) for z in (x, y))
                dve.wait_ge(s_ev, u + 1)
                if u >= 2:
                    dve.wait_ge(s_qt, u - 1)
                link(v.tensor_tensor(sqb, x, x, ALU.mult))
                link(v.tensor_reduce(stat[:, 24:24 + FH], sqb.rearrange("p (h d) -> p h d", d=FD), AX.X, ALU.add))
                rms_scale(link, stat[:, 24:24 + FH], FD, stat[:, 24:24 + FH])
                link(v.tensor_tensor(y3, x3, stat[:, 24:24 + FH].unsqueeze(2).to_broadcast([P, FH, FD]), ALU.mult))
                v.tensor_tensor(y3, y3, gain[:, :].unsqueeze(1).to_broadcast([P, FH, FD]), ALU.mult).then_inc(s_qn, 1)

            for u in range(U_B):
                if u < 16:
                    normalise(u)
                if u % 8 == 7:
                    for j in (4, 5, 6) if u == 7 else (7, 8, 9) if u == 15 else (10, 11):
                        mod_columns(j)
            dve.wait_ge(s_modc, 12)
            link(v.scalar_tensor_tensor(out=a2[:, :], in0=mod[:, 32:40], scalar=1.0, in1=vcol[:, 56:64], op0=ALU.add, op1=ALU.mult))

            def fox_max(n):
                h, i = divmod(n, NT)
                N, b = P * i, n % 2
                if i == 0:
                    dve.wait_ge(s_nc[h % 2], 16 * (h // 2 + 1))
                nb = ncb[h % 2]
                link(v.tensor_tensor(ncd, nb[:, N:N + P], foxmask[:, :], ALU.add))
                dve.wait_ge(s_S, n + 1)
                if n >= 2:
                    dve.wait_ge(s_T, n - 1)
                lg = psum[:, 4:6, :].rearrange("p b n -> p (b n)")
                if i > 0:
                    v.tensor_tensor_reduce(pl[b][:, 0:N], lg[:, 0:N], nb[:, 0:N], 1.0, -3.0e38, ALU.add, ALU.max, stat[:, 40:41])
                link(v.tensor_tensor_reduce(pl[b][:, N:N + P], lg[:, N:N + P], ncd, 1.0, -3.0e38, ALU.add, ALU.max, stat[:, 41:42]))
                m = stat[:, 40:41] if i > 0 else stat[:, 41:42]
                v.tensor_scalar(stat[:, 16 + b:17 + b], m, stat[:, 41:42], -1.0, ALU.max, ALU.mult).then_inc(s_pl, 1)

            def fox_out(n):
                h, i = divmod(n, NT)
                dve.wait_ge(s_O, n + 1)
                link(v.reciprocal(stat[:, 42:43], stat[:, 18 + n % 4:19 + n % 4]))
                v.tensor_scalar(yf[:, i, h * FD:(h + 1) * FD], psum[:, 3, 0:FD], stat[:, 42:43], None, ALU.mult).then_inc(s_y, 1)

            for m in range(FSTEPS + 2):
                if m < FSTEPS:
                    fox_max(m)
                if m >= 2:
                    fox_out(m - 2)

            dve.wait_ge(s_pad, 2)
            for j in range(4):
                dve.wait_ge(s_cin[j % 2], 16 * (j // 2 + 1))
                tap = lambda w: vcol[:, 72 + 4 * w + j:73 + 4 * w + j]
                x, y = conv_in[j % 2], mqkT[:, j, :]
                link(v.tensor_scalar(y, x[:, 0:T], tap(0), None, ALU.mult))
                for w in range(1, TAPS):
                    ins = v.scalar_tensor_tensor(out=y, in0=x[:, w:w + T], scalar=tap(w), in1=y, op0=ALU.mult, op1=ALU.add)
                    if w < TAPS - 1:
                        link(ins)
                ins.then_inc(s_cv, 1)
            dve.wait_ge(s_rd, 64)
            b3 = lambda x: x.unsqueeze(2).to_broadcast([P, MH, P])
            M1 = MV + 1

            def ml_weights(c):
                dve.wait_ge(s_nm[c % 2], 16 * (c // 2 + 1))
                link(v.tensor_tensor(mw, nmb[c % 2], b3(mcol[:, 0, c, :]), ALU.add))
                v.tensor_scalar(mw, mw, 0.0, None, ALU.min).then_inc(m_w, 1)

            ml_weights(0)
            for c in range(NT):
                dve.wait_ge(m_ST, c + 1)
                kt = psum[:, 3, 0:MH * MQ].rearrange("p (h d) -> p h d", d=MQ)
                v.tensor_tensor(mkw, kt, mcol[:, 3, c, :].unsqueeze(2).to_broadcast([P, MH, MQ]), ALU.mult).then_inc(m_kw, 1)
                dve.wait_ge(m_k, c + 1)
                for b in range(2):
                    ins = v.tensor_tensor(msc[:, b::2, :], psum[:, (4, 7)[b], 0:2 * P].rearrange("p (j n) -> p j n", j=2), mw[:, b::2, :], ALU.mult)
                ins.then_inc(m_sc, 1)
                if c + 1 < NT:
                    dve.wait_ge(m_sc, c + 1)
                    ml_weights(c + 1)
                dve.wait_ge(m_B, c + 1)
                if c == 0:
                    dve.wait_ge(s_pad, 4)
                for h in range(MH):
                    b, j = MQ * (h % 2), h // 2
                    ins = v.scalar_tensor_tensor(out=mC[b:b + MQ, j, :], in0=mC[b:b + MQ, j, :], scalar=mdec[b:b + MQ, h, c:c + 1],
                                                 in1=psum[b:b + MQ, 3, j * M1:(j + 1) * M1], op0=ALU.mult, op1=ALU.add)
                ins.then_inc(m_st, 1)
                dve.wait_ge(m_in, c + 1)
                for j in range(2):
                    ins = v.tensor_tensor(mnum[:, 2 * j:2 * j + 2, :], mnum[:, 2 * j:2 * j + 2, :],
                                          psum[:, 5 + j, 0:2 * M1].rearrange("p (h n) -> p h n", h=2), ALU.add)
                ins.then_inc(m_num, 1)
                dve.wait_ge(m_num, c + 1)
                den = stat[:, 44:44 + MH]
                dsum = mnum[:, :, MV:M1]
                link(v.scalar_tensor_tensor(out=den.unsqueeze(2), in0=dsum, scalar=-1.0, in1=dsum, op0=ALU.mult, op1=ALU.max))
                link(v.tensor_tensor(den, den, mcol[:, 2, c, :], ALU.max))
                link(v.reciprocal(den, den))
                if c >= 1:
                    dve.wait_ge(m_yt, c)
                else:
                    dve.wait_ge(s_mos, 1)
                m3, y3 = mtmp.rearrange("p (h n) -> p h n", h=MH), my.rearrange("p (h n) -> p h n", h=MH)
                link(v.tensor_tensor(m3, mnum[:, :, 0:MV], b3(den), ALU.mult))
                link(v.tensor_tensor(my, mtmp, mtmp, ALU.mult))
                ss = stat[:, 48:48 + MH]
                link(v.tensor_reduce(ss, y3, AX.X, ALU.add))
                rms_scale(link, ss, MV, ss)
                link(v.tensor_tensor(m3, m3, b3(ss), ALU.mult))
                link(v.tensor_tensor(mtmp, mtmp, gml[:, :], ALU.mult))
                v.tensor_tensor(my, mtmp, mo[:, c, :], ALU.mult).then_inc(m_y, 1)

            c8 = lambda x: x.rearrange("p (c t) -> p c t", t=P)
            for h in range(HH):
                dve.wait_ge(h_ab, h + 1)
                if h == 0:
                    dve.wait_ge(m_yt, NT)
                link(v.scalar_tensor_tensor(out=hqe, in0=hz, scalar=0.0, in1=hE0, op0=ALU.min, op1=ALU.subtract))
                v.tensor_tensor(hk, hqe, hz, ALU.subtract).then_inc(h_lf, 1)
                for c in range(NT):
                    ins = v.tensor_tensor_scan(out=ha[:, c * P:(c + 1) * P], data0=ones[:, :], data1=hqe[:, c * P:(c + 1) * P],
                                               initial=0.0, op0=ALU.mult, op1=ALU.add)
                ins.then_inc(h_a, 1)
                dve.wait_ge(h_a, h + 1)
                v.tensor_tensor(c8(hkd), c8(ha)[:, :, P - 1:P].to_broadcast([P, NT, P]), c8(ha), ALU.subtract).then_inc(h_d, 1)

                def halves(x, l):
                    b = 1 << l
                    y = x.rearrange("p (n z b) -> p n z b", z=2, b=b)
                    return y[:, :, 0, :], y[:, :, 1, :]

                def exponents(l):
                    b = 1 << l
                    lo, hi = halves(ha, l)
                    elo, ehi = halves(hE[l % 2], l)
                    ref = lo[:, :, b - 1:b].to_broadcast([P, T // (2 * b), b])
                    v.tensor_tensor(elo, ref, lo, ALU.subtract)
                    v.tensor_tensor(ehi, hi, ref, ALU.subtract).then_inc(h_x, 1)

                def scale_qk(l):
                    dve.wait_ge(h_e, 7 * h + l + 1)
                    elo, ehi = halves(hE[l % 2], l)
                    klo, qhi = halves(hk, l)[0], halves(hq, l)[1]
                    v.tensor_tensor(elo, elo, klo, ALU.mult)
                    v.tensor_tensor(ehi, ehi, qhi, ALU.mult).then_inc(h_qk, 1)

                def take(l):
                    n = 8 * h + l
                    dve.wait_ge(h_S, n + 1)
                    b0 = 4 + 2 * (l % 2)
                    ins = v.copy_predicated(c8(hsc), levels[:, l, :].unsqueeze(1).to_broadcast([P, NT, P]),
                                            psum[:, b0:b0 + 2, :].rearrange("p b (c n) -> p (b c) n", c=4))
                    ins.then_inc(h_sc, 1)

                exponents(0)
                if h >= 1:
                    dve.wait_ge(h_O, h)
                link(v.memset(hsc, 0.0))
                dve.wait_ge(h_k, h + 1)
                dve.wait_ge(h_ea, h + 1)
                link(v.tensor_copy(stat[:, 52:60], c8(hqe)[:, :, P - 1:P].rearrange("p c o -> p (c o)")))
                link(v.tensor_tensor(hqe, hqe, hq, ALU.mult))
                dve.wait_ge(h_de, h + 1)
                v.tensor_tensor(hkd, hkd, hk, ALU.mult).then_inc(h_kd, 1)
                scale_qk(0)
                for l in range(1, 8):
                    if l < 7:
                        if l >= 2:
                            dve.wait_ge(h_S, 8 * h + l - 1)
                        exponents(l)
                        if l >= 1:
                            take(l - 1)
                        scale_qk(l)
                    else:
                        take(6)
                        link(v.tensor_copy(stat[:, 60:61], ones[:, 0:1]))
                        dve.sem_inc(h_qk, 1)
                take(7)
                dve.wait_ge(h_up, h + 1)
                link(v.memset(hst[:, 0:P], 0.0))
                for c in range(NT - 1):
                    ins = v.scalar_tensor_tensor(out=hst[:, (c + 1) * P:(c + 2) * P], in0=hst[:, c * P:(c + 1) * P],
                                                 scalar=stat[:, 52 + c:53 + c], in1=psum[:, 6 + c // 4, (c % 4) * P:(c % 4 + 1) * P],
                                                 op0=ALU.mult, op1=ALU.add)
                    if c < NT - 2:
                        link(ins)
                ins.then_inc(h_st, 1)
                dve.wait_ge(h_O, h + 1)
                o8 = psum[:, 4:6, :].rearrange("p b (c n) -> p (b c) n", c=4)
                link(v.tensor_copy(c8(hE0), o8))
                link(v.tensor_tensor(hE1, hE0, hE0, ALU.mult))
                ss = stat[:, 24:32]
                link(v.tensor_reduce(ss, c8(hE1), AX.X, ALU.add))
                rms_scale(link, ss, P, ss)
                link(v.tensor_tensor(c8(hE0), c8(hE0), ss.unsqueeze(2).to_broadcast([P, NT, P]), ALU.mult))
                link(v.tensor_tensor(c8(hE0), c8(hE0), ghg[:, h * P:(h + 1) * P].unsqueeze(1).to_broadcast([P, NT, P]), ALU.mult))
                v.tensor_tensor(hkT, hE0, hg, ALU.mult).then_inc(h_y, 1)

            dve.wait_ge(h_yt, HH)
            dve.wait_ge(s_pj, NU)
            for n in range(48):
                br, j, half = n // 16, n // 2 % 8, n % 2
                dst = hT[:, j, half * BW:(half + 1) * BW]
                dve.wait_ge(s_gs, n + 1)
                dve.wait_ge(s_br, n + 1)
                if br == 0:
                    v.tensor_tensor(dst, gt[n % 3], bank(n % 3), ALU.mult).then_inc(s_pr, 1)
                else:
                    v.tensor_tensor(prod[n % 2], gt[n % 3], bank(n % 3), ALU.mult).then_inc(s_pr, 1)
                    dve.wait_ge(s_pr, n + 1)
                    v.tensor_tensor(dst, dst, prod[n % 2], ALU.add).then_inc(s_mg, 1)
            dve.wait_ge(s_mg, 32)
            for n in range(8):
                if n >= 2:
                    dve.wait_ge(s_bc, n - 1)
                c = (mod[:, 16:24], a2[:, :], mod[:, 24:32], mod[:, 40:48])[n // 2][:, 4 * (n % 2):4 * (n % 2) + 4]
                v.tensor_tensor(dgb[n % 2], ident[:, :].unsqueeze(1).to_broadcast([P, 4, P]),
                                c.unsqueeze(2).to_broadcast([P, 4, P]), ALU.mult).then_inc(s_dg, 1)
            dve.wait_ge(s_bcc, 8)
            dve.wait_ge(s_rw, 32)

            def residual(i):
                y, z = x2[i % 2], h2[i % 2]
                dve.wait_ge(s_mx, i + 1)
                dve.wait_ge(s_xi[i % 2], 16 * (i // 2 + 1))
                if i >= 2:
                    dve.wait_ge(s_so[i % 2], 32 * (i // 2))
                    dve.wait_ge(s_h2t, i - 1)
                link(v.tensor_tensor(y, banks(2 * (i % 2), 2), g1b, ALU.mult))
                v.tensor_tensor(y, y, xin[i % 2], ALU.add).then_inc(s_x2, 1)
                dve.wait_ge(s_sq, i + 1)
                rms_scale(link, stat[:, 32 + i:33 + i], D, stat[:, 32 + i:33 + i])
                turned = lambda q: q.rearrange("p (d k) -> p k d", k=KD)
                z3 = z.rearrange("p (k d) -> p k d", k=KD)
                link(v.scalar_tensor_tensor(out=z3, in0=turned(y), scalar=stat[:, 32 + i:33 + i], in1=turned(a2b),
                                            op0=ALU.mult, op1=ALU.mult))
                v.tensor_tensor(z3, z3, turned(b2b), ALU.add).then_inc(s_h2, 1)

            def first_of(src, values, kth, keep, n, out_):
                link(v.tensor_scalar(out_, src, kth, None, ALU.is_gt))
                link(v.tensor_reduce(stat[:, 61:62], out_, AX.X, ALU.add))
                link(v.tensor_scalar(stat[:, 61:62], stat[:, 61:62], -1.0, float(n), ALU.mult, ALU.add))
                link(v.tensor_scalar(values, src, kth, None, ALU.is_equal))
                link(v.tensor_tensor_scan(out=keep, data0=ones[:, 0:src.shape[1]], data1=values, initial=0.0, op0=ALU.mult, op1=ALU.add))
                link(v.scalar_tensor_tensor(out=values, in0=keep, scalar=stat[:, 61:62], in1=values, op0=ALU.is_le, op1=ALU.mult))
                link(v.tensor_tensor(out_, out_, values, ALU.add))

            def choose(i):
                dve.wait_ge(s_sg, i + 1)
                link(v.tensor_tensor(cho, sco, rbias, ALU.add))
                for g in range(NG):
                    link(v.max(m8[:, g, :], cho[:, g * GE:(g + 1) * GE]))
                link(v.tensor_tensor(gsc.unsqueeze(2), m8[:, :, 0:1], m8[:, :, 1:2], ALU.add))
                link(v.max(top, gsc))
                first_of(gsc, geq, top[:, TOPG - 1:TOPG], gcu, TOPG, gmk)
                link(v.tensor_scalar(gmk, gmk, 1.0, -NEG, ALU.subtract, ALU.mult))
                link(v.tensor_tensor(cho.rearrange("p (g n) -> p g n", g=NG), cho.rearrange("p (g n) -> p g n", g=NG),
                                     gmk.unsqueeze(2).to_broadcast([P, NG, GE]), ALU.add))
                link(v.max(top, cho))
                first_of(cho, eqt, top[:, TOPK - 1:TOPK], cum, TOPK, selall[:, i, :])
                link(v.tensor_tensor(sel, sco, selall[:, i, :], ALU.mult))
                link(v.tensor_reduce(stat[:, 62:63], sel, AX.X, ALU.add))
                link(v.reciprocal(stat[:, 62:63], stat[:, 62:63]))
                v.tensor_scalar(tw[:, i, 0:NE, 1:2].rearrange("p e o -> p (e o)"), sel, stat[:, 62:63], ROUTE, ALU.mult, ALU.mult).then_inc(s_sel, 1)

            def slots(i):
                dve.wait_ge(s_pos, i + 1)
                link(v.scalar_tensor_tensor(out=msk, in0=psum[:, 7, 0:NE], scalar=1.0, in1=selall[:, i, :], op0=ALU.add, op1=ALU.mult))
                v.tensor_scalar(posm[:, i, 0:NE], msk, 1.0, None, ALU.subtract).then_inc(s_pm, 1)

            for i in range(NT + 2):
                if i < NT:
                    residual(i)
                if 1 <= i <= NT:
                    choose(i - 1)
                if i >= 2:
                    slots(i - 2)
            for i in range(NT):
                link(v.tensor_copy(tw[:, i, :, 0:1].rearrange("p e o -> p (e o)"), tok[:, i:i + 1].to_broadcast([P, NX])))
            link(v.memset(posm[:, :, NE:NX], -1.0))
            link(v.memset(tw[:, :, NE:NX, 1:2], 0.0))
            link(v.memset(cnt[:, NE:NX], 0))
            dve.wait_ge(s_cn, 1)
            v.tensor_copy(cnt[:, 0:NE], psum[:, 7, 0:NE]).then_inc(s_tab, 1)
            for i in range(NT):
                dve.wait_ge(s_si, i + 1)
                if i >= 1:
                    dve.wait_ge(s_ht, i)
                v.tensor_tensor(shh, sgm, bank(i % 2)[:, FF:2 * FF], ALU.mult).then_inc(s_hd, 1)
                dve.wait_ge(s_sO, i + 1)
                if i >= 2:
                    dve.wait_ge(s_ys[i % 2], 16 * (i // 2 + 1 - i % 2))
                v.tensor_copy(ysh[i % 2][:, BW:D], bank(5)).then_inc(s_yv, 1)

            def one_hot(j, e, c):
                v.tensor_tensor(oh[j], slotn[:, bass.ds(c * P, P)].unsqueeze(1).to_broadcast([P, NT, P]), posm[:, :, bass.ds(e, 1)].to_broadcast([P, NT, P]), ALU.is_equal).then_inc(e_oh[j], 1)

            def rows_of(j, b):
                l = psum[:, 2, 8 * j:8 * j + 2]
                v.tensor_copy(wts[:, 2 * j + b:2 * j + b + 1], l[:, 1:2])
                v.tensor_scalar(idx[:, 2 * j + b:2 * j + b + 1], l[:, 0:1], float(FAR), dump[:, :], ALU.add, ALU.min).then_inc(e_idx[j], 1)

            def hidden(j):
                v.tensor_tensor(hid[j], sg[j], bank(3 if j == 0 else 4)[:, FF:2 * FF], ALU.mult).then_inc(e_hid[j], 1)

            def weigh_out(j, b):
                v.tensor_scalar(ob[j][:, BW:D], bank(7), wts[:, 2 * j + b:2 * j + b + 1], None, ALU.mult).then_inc(e_obv[j], 1)

            dve.wait_ge(s_ys[0], 16 * (NT // 2 + 1))
            dve.wait_ge(s_ys[1], 16 * (NT // 2))
            dve.wait_ge(s_so[0], 16 * NT)
            dve.wait_ge(s_so[1], 16 * NT)
            dve.wait_ge(e_clear, 1)
            for q in (e_oh, e_idx, e_hid, e_obv):
                for j in range(3):
                    dve.sem_inc(q[j], 1)
            for c in range(NC):
                ins = v.tensor_scalar(slotn[:, c * P:(c + 1) * P], col_i[:, :], float(c * P), None, ALU.add)
            link(ins)
            for e in range(2):
                if e == 1:
                    done(dve, e_lst[0], 1)
                    done(dve, e_lst[1], 1)
                    for j in range(2):
                        rows_of(j, 0)
                one_hot(0, e, 0)
                one_hot(1, e, 1)
            with dve.Fori(0, NE // 2) as it:
                for b in range(2):
                    e = 2 * it + b
                    n_e = dve.value_load(cnt[0:1, bass.ds(e, 1)], min_val=0, max_val=T)
                    n_next = dve.value_load(cnt[0:1, bass.ds(e + 1, 1)], min_val=0, max_val=T)
                    n_after = dve.value_load(cnt[0:1, bass.ds(e + 2, 1)], min_val=0, max_val=T)
                    done(dve, e_lst[0], e + 2)
                    done(dve, e_lst[1], e + 2)
                    done(dve, e_sc[0], e)
                    done(dve, e_sc[1], e)
                    done(dve, e_oba[0], e)
                    done(dve, e_oba[1], e)
                    rows_of(0, 1 - b)
                    with dve.If(n_next > P):
                        rows_of(1, 1 - b)
                    with dve.Else():
                        skipped(dve, e_idx[1], e + 1)
                    done(dve, e_si[0], e + 1)
                    done(dve, e_hT[0], e)
                    hidden(0)
                    with dve.If(n_e > P):
                        done(dve, e_si[1], e + 1)
                        done(dve, e_hT[1], e)
                        hidden(1)
                    with dve.Else():
                        skipped(dve, e_hid[1], e)
                    one_hot(0, e + 2, 0)
                    with dve.If(n_after > P):
                        done(dve, e_oh[1], e + 2)
                        one_hot(1, e + 2, 1)
                    with dve.Else():
                        skipped(dve, e_oh[1], e + 2)
                    done(dve, e_O[0], e + 1)
                    weigh_out(0, b)
                    with dve.If(n_e > P):
                        done(dve, e_O[1], e + 1)
                        weigh_out(1, b)
                    with dve.Else():
                        skipped(dve, e_obv[1], e)
                    with dve.If(n_e > 2 * P):
                        with dve.Fori(0, ND) as c:
                            n = ND * e + c
                            with dve.If(n_e > P * (c + 2)):
                                one_hot(2, e, c + 2)
                                done(dve, e_lst[2], n + 1)
                                done(dve, e_oba[2], n)
                                done(dve, e_sc[2], n)
                                rows_of(2, 0)
                                done(dve, e_si[2], n + 1)
                                hidden(2)
                                done(dve, e_O[2], n + 1)
                                weigh_out(2, 0)
                            with dve.Else():
                                for q in (e_oh, e_idx, e_hid, e_obv):
                                    skipped(dve, q[2], n)
                            dve.nop()
                    with dve.Else():
                        for q in (e_oh, e_idx, e_hid, e_obv):
                            skipped(dve, q[2], ND * e, ND)
                    dve.nop()
            for i in range(NT):
                dve.wait_ge(f_y[i % 4], 32 * (i // 4 + 1))
                link(v.tensor_tensor(fy[i % 4], fy[i % 4], g2b, ALU.mult))
                v.tensor_tensor(fy[i % 4], fy[i % 4], fx[i % 4], ALU.add).then_inc(f_s, 1)


_INS = ["x", "c", "ada_w", "ada_b", "norm1_g", "norm2_g", "w_in", "fox_bf", "fox_q_g", "fox_k_g", "mlstm_conv",
        "mlstm_bi", "mlstm_bf", "mlstm_norm_g", "hgrn_lower_bounds", "hgrn_norm_g", "w_branch", "w_out", "router_w",
        "router_bias", "exp_w1", "exp_w3", "exp_w2", "sh_w1", "sh_w3", "sh_w2"]


def kernel(**inputs):
    import numpy as _np
    import concourse.bacc as _bacc
    from concourse import mybir as _mybir
    from concourse.bass_utils import run_bass_kernel_spmd as _run

    nc = _bacc.Bacc("TRN2", target_bir_lowering=False, num_devices=1)
    arrays, args = {}, {}
    for name in _INS:
        v = _np.ascontiguousarray(inputs[name])
        arrays[f"in_{name}"] = v
        args[name] = nc.dram_tensor(f"in_{name}", v.shape, _mybir.dt.from_np(v.dtype), kind="ExternalInput").ap()
    out = nc.dram_tensor("out_x", arrays["in_x"].shape, F32, kind="ExternalOutput").ap()
    layer_kernel(nc, args, out)
    r = _run(nc, [arrays], core_ids=[0])
    return r.results[0]["out_x"]
```

```python
from contextlib import ExitStack

import concourse.bass as bass
from concourse import mybir

F32 = mybir.dt.float32
I32 = mybir.dt.int32
BF16 = mybir.dt.bfloat16
ALU = mybir.AluOpType
ACT = mybir.ActivationFunctionType
AX = mybir.AxisListType
P = 128
BW = 512
EPS = 1e-6
NEG = -1.0e30
FAR = 2048


def layer_kernel(nc, a, out):
    T, D = a["x"].shape[1:]
    NT, KD = T // P, D // P
    FH, FD = a["fox_bf"].shape[1], a["fox_q_g"].shape[1]
    MH = a["mlstm_bi"].shape[1]
    W = FH * FD
    MV = W // MH
    MQ = MV // 2
    HH = W // P
    TAPS = a["mlstm_conv"].shape[1]
    NE = a["router_w"].shape[2]
    NG, TOPG, TOPK, ROUTE = 8, 4, 8, 2.5
    GE = NE // NG
    FF = a["exp_w1"].shape[3]
    FK = FF // P
    assert a["x"].shape[0] == 1 and a["w_in"].shape[0] == 1
    assert W == BW and MH * MQ * 2 == BW and 2 * FF == BW and D == 2 * BW and NT == 8 and KD == 8
    w_in = a["w_in"][0]
    widths = [W, W, W, FH, 2 * MH * MQ, W, MH, MH, W, W, W, W, W, 3 * D]
    names = ["fq", "fk", "fv", "ff", "mqk", "mv", "mi", "mf", "mo", "hf", "hq", "hi", "hg", "gates"]
    col = {n: sum(widths[:j]) for j, n in enumerate(names)}

    ctx = ExitStack()
    with ctx:
        sb = lambda name, shape, dt=F32: ctx.enter_context(nc.sbuf_tensor(name, shape, dt))
        sem = lambda name: ctx.enter_context(nc.semaphore(name))
        dram = lambda name, shape: nc.dram_tensor(name, shape, F32, kind="Internal").ap()

        proj_d = dram("proj_d", [13 * 8, P, BW])
        frow_d = dram("frow_d", [FH, T])
        mrow_d = dram("mrow_d", [MH, T])
        mdec_d = dram("mdec_d", [MH, NT])
        x2_d = dram("x2_d", [T, D])
        h2_d = dram("h2_d", [T, D])
        y_d = dram("y_d", [T + P, D])

        psum = ctx.enter_context(nc.psum_tensor("psum", [P, 8, BW], F32))
        bank = lambda b: psum[:, b, :]
        banks = lambda b, n, **kw: psum[:, b:b + n, :].rearrange("p b n -> p (b n)")

        hT = sb("hT", [P, KD, T])
        ring = sb("ring", [P, 3, 8, BW])
        work = sb("work", [P, 27648])
        ident = sb("ident", [P, P])
        ones = sb("ones", [P, P])
        col_i = sb("col_i", [P, P])
        upper = sb("upper", [P, P])
        strict = sb("strict", [P, P])
        foxmask = sb("foxmask", [P, P])
        levels = sb("levels", [P, 8, P], I32)
        vcol = sb("vcol", [P, 88])
        cond = sb("cond", [P, KD])
        mod = sb("mod", [P, 48])
        a1 = sb("a1", [P, KD])
        a2 = sb("a2", [P, KD])
        wsm = sb("wsm", [P, KD, 16])
        sm = sb("sm", [P, NT, 16])
        gq = sb("gq", [P, FD])
        gk = sb("gk", [P, FD])
        gml = sb("gml", [P, W])
        ghg = sb("ghg", [P, W])
        bff = sb("bff", [FH, 1])
        bmi = sb("bmi", [MH, 1])
        bmf = sb("bmf", [MH, 1])
        mcol = sb("mcol", [P, 4, NT, MH])
        mdec = sb("mdec", [P, MH, NT])
        stat = sb("stat", [P, 64])
        newton = sb("newton", [P, 3, 8])
        tok = sb("tok", [P, NT])
        dump = sb("dump", [P, 1])
        cst = sb("cst", [P, 2])

        def view(at, *shape):
            n = 1
            for s in shape:
                n *= s
            v = work[:, at:at + n]
            if len(shape) == 2:
                v = v.rearrange("p (a b) -> p a b", b=shape[1])
            if len(shape) == 3:
                v = v.rearrange("p (a b c) -> p a b c", b=shape[1], c=shape[2])
            return v

        xs, xn = view(0, NT, D), view(8192, NT, D)
        R = [view(12288 + 1024 * j, T) for j in range(10)]
        vrow = view(24000, P)
        sI, tI, xI, shI = (view(24200 + 128 * j, P).bitcast(I32) for j in range(4))
        eqf = view(24800, P)
        tokI = view(25000, NT).bitcast(I32)
        qT, kT, vf = view(0, 4, T), view(4096, 4, T), view(8192, NT, W)
        yf = view(12288, NT, W)
        pl = [view(16384 + 1024 * j, T) for j in range(2)]
        pT = [view(18432 + 1024 * j, NT, P) for j in range(2)]
        ncb = [view(20480 + 1024 * j, T) for j in range(2)]
        raw = [view(22528 + 512 * j, W) for j in range(2)]
        qn = [view(23552 + 512 * j, W) for j in range(2)]
        adax = view(8192, 8, BW)
        part = [view(26624 + 512 * j, BW) for j in range(2)]
        sqb = view(24576, W)
        ncd = view(25088, P)
        stg = [view(25600 + 512 * j, BW) for j in range(4)]
        yTf, yTm, yTh = view(0, 4, T), view(4096, 4, T), view(8192, 4, T)
        yT = [yTf, yTm, yTh]
        mo = view(8192, NT, W)
        vaug = view(12288, NT, MH, MV + 1)
        mqkT = view(16416, 4, T)
        conv_in = [view(20512 + 1032 * j, T + TAPS - 1) for j in range(2)]
        at = 20512
        nmb = [view(at + 512 * j, MH, P) for j in range(2)]
        mw, msc = view(at + 1024, MH, P), view(at + 1536, MH, P)
        mkt, mkw = view(at + 2048, MH * MQ), view(at + 2304, MH, MQ)
        mnum, mtmp, my = view(at + 2560, MH, MV + 1), view(at + 3076, W), view(at + 3588, W)
        mC = view(at + 4100, 2, MV + 1)
        hz, hq, hv, hg, ha, hk, hqe, hkd, hE0, hE1, hsc, hkT, hst = (view(12288 + 1024 * j, T) for j in range(13))
        hE = [hE0, hE1]
        gt = [view(12288 + 512 * j, BW) for j in range(3)]
        prod = [view(13824 + 512 * j, BW) for j in range(2)]
        dgb = [view(24256 + 512 * j, 4, P) for j in range(2)]
        h2T = view(0, KD, T)
        xin = [view(12288 + 1024 * j, D) for j in range(2)]
        g1b, a2b, b2b = (view(14336 + 1024 * j, D) for j in range(3))
        g2b = view(10368, D)
        slotn = view(0, T)
        x2 = [view(18432 + 1024 * j, D) for j in range(2)]
        h2 = [view(20480 + 1024 * j, D) for j in range(2)]
        dsc = view(22528, D)
        rwt = view(23680, KD, NE)
        shw2 = ring[:, 2, 0:4, :].rearrange("p a n -> p (a n)").rearrange("p (k n) -> p k n", k=2)
        rbias = view(24192, NE)
        sco, cho, msk, sel, cum, eqt = (view(24256 + 64 * j, NE) for j in range(6))
        m8 = view(24640, NG, 8)
        gsc, gmk, geq, gcu, top = (view(24704 + 8 * j, 8) for j in range(5))
        sgm, shh = view(24768, FF), view(25024, FF)
        shT = view(25280, FK, P)
        ysh = [view(25600 + 1024 * j, D) for j in range(2)]
        NX = NE + 4
        selall = view(8192, NT, NE)
        posm = view(8704, NT, NX)
        tw = view(9248, NT, NX, 2)
        w13 = [hT[:, 4 * b:4 * b + 4, :].rearrange("p k n -> p (k n)").rearrange("p (k n) -> p k n", k=KD) for b in range(2)]
        w13 += [ring[:, 1 + b] for b in range(2)]
        w2 = [ring[:, 0, 4 * b:4 * b + 4, :].rearrange("p k n -> p (k n)").rearrange("p (k n) -> p k n", k=FK) for b in range(2)]
        w2 += [view(1024 + 2048 * b, FK, D) for b in range(2)]
        twb = view(5120, 3 * NT * NX).bitcast(BF16).rearrange("p (i e s z) -> p i e s z", e=NX, s=3, z=2)
        rest = view(6912, NT, NX, 2)
        xg = [view(12288 + 1024 * j, D) for j in range(3)]
        xgT = [view(15360 + 1024 * j, KD, P) for j in range(3)]
        oh = [view(18432 + 1024 * j, T // 2).bitcast(BF16).rearrange("p (i n) -> p i n", n=P) for j in range(3)]
        ob = [view(21504 + 1024 * j, D) for j in range(3)]
        sg = [view(24576 + 256 * j, FF) for j in range(3)]
        hid = [view(25344 + 256 * j, FF) for j in range(3)]
        hidT = [view(26112 + 256 * j, FK, P) for j in range(3)]
        idx = sb("idx", [P, 12], I32)
        lst = sb("lst", [P, 12, 2])
        fy = [view(12288 + 1024 * j, D) for j in range(4)]
        fx = [view(16384 + 1024 * j, D) for j in range(4)]
        cnt = sb("cnt", [P, NX], I32)

        TBLOCKS = ["fq", "fk", "fv", "mqk", "mv", "mo", "hf", "hq", "hi", "hg"]
        NADA = 6 * D // BW
        order = [("ada", j) for j in range(4)]
        order += [("w", q) for q in range(16)]
        order += [("wb", 0), ("wb", 1), ("wb", 2), ("wo", 0), ("wo", 1), ("sh", 0), ("sh", 1)]
        place = {b: n for n, b in enumerate(order)}
        NDMA = {"sh0": 2}
        TRANSPOSED = {3, 6, 7} | set(range(10, 16))
        NU, U_B, U_C = 8 * 16, 24, 80
        HG_FILL = [3, 0, 1, 0, 1, 0, 1, 0, 0, 0, 1, 1]
        FSTEPS = FH * NT
        slot = lambda b: ring[:, place[b] % 3]
        flat = lambda v: v.rearrange("p a n -> p (a n)")

        R_MQK, R_MV, R_MO, R_HF, R_HQ, R_HI, R_HG, R_G = (8 * j for j in range(8))

        early = ExitStack()
        whole, sem = sem, lambda name: early.enter_context(nc.semaphore(name))
        s_x = [sem(f"s_x{i}") for i in range(2)]
        s_wsm, s_vec, s_ring = sem("s_wsm"), sem("s_vec"), [whole(f"s_ring{i}") for i in range(3)]
        s_iota, s_pconst, s_dconst = sem("s_iota"), sem("s_pconst"), sem("s_dconst")
        s_dve, s_act, s_pool = whole("s_dve"), whole("s_act"), whole("s_pool")
        s_vt, s_vc, s_cond = sem("s_vt"), sem("s_vc"), sem("s_cond")
        s_ada, s_part = whole("s_ada"), sem("s_part")
        s_mod, s_modc, s_a1 = sem("s_mod"), sem("s_modc"), sem("s_a1")
        s_ss, s_xn, s_xt, s_xea, s_xed = (sem(n) for n in ("s_ss", "s_xn", "s_xt", "s_xea", "s_xed"))
        s_sm, s_smc, s_rows, s_zr, s_lr, s_er = (sem(n) for n in ("s_sm", "s_smc", "s_rows", "s_zr", "s_lr", "s_er"))
        s_fr, s_mr, s_mf, s_mct, s_mcc, s_nd = (sem(n) for n in ("s_fr", "s_mr", "s_mf", "s_mct", "s_mcc", "s_nd"))
        s_rd = whole("s_rd")
        s_pj, s_ev = sem("s_pj"), sem("s_ev")
        s_st = [sem(f"s_st{i}") for i in range(4)]
        s_qn, s_qt, s_qe = sem("s_qn"), sem("s_qt"), sem("s_qe")
        s_nc = [whole(f"s_nc{i}") for i in range(2)]
        s_S, s_pl, s_p, s_T, s_pT, s_O, s_y = (sem(n) for n in ("s_S", "s_pl", "s_p", "s_T", "s_pT", "s_O", "s_y"))
        s_fyt, s_fyc = sem("s_fyt"), sem("s_fyc")
        s_pad, s_cv, s_sil, s_mo, s_mos = sem("s_pad"), sem("s_cv"), sem("s_sil"), whole("s_mo"), sem("s_mos")
        s_cin = [whole(f"s_cin{i}") for i in range(2)]
        s_va = whole("s_va")
        s_nm = [whole(f"s_nm{i}") for i in range(2)]
        m_w, m_e, m_k, m_ST, m_sc, m_kw, m_B, m_in, m_num, m_st, m_y, m_yt, m_yc = (sem("m_" + n) for n in (
            "w", "e", "k", "ST", "sc", "kw", "B", "in", "num", "st", "y", "yt", "yc"))
        h_zq, h_vg = whole("h_zq"), whole("h_vg")
        h_ab, h_lf, h_k, h_kd = (sem("h_" + n) for n in ("ab", "lf", "k", "kd"))
        h_a, h_ea, h_d, h_de, h_x, h_e, h_qk, h_S, h_sc = (sem("h_" + n) for n in ("a", "ea", "d", "de", "x", "e", "qk", "S", "sc"))
        h_kt, h_kc, h_up, h_st, h_O, h_y, h_yt, h_yc = (sem("h_" + n) for n in ("kt", "kc", "up", "st", "O", "y", "yt", "yc"))
        sem = whole
        s_g = [sem(f"s_g{i}") for i in range(3)]
        s_gs, s_br, s_pr, s_mg = sem("s_gs"), sem("s_br"), sem("s_pr"), sem("s_mg")
        s_dg, s_bc, s_bcc = sem("s_dg"), sem("s_bc"), sem("s_bcc")
        s_xi = [sem(f"s_xi{i}") for i in range(2)]
        s_rw, s_mx, s_x2, s_sq, s_h2, s_h2t, s_h2c, s_rt, s_sg = (sem(n) for n in (
            "s_rw", "s_mx", "s_x2", "s_sq", "s_h2", "s_h2t", "s_h2c", "s_rt", "s_sg"))
        s_so = [sem(f"s_so{i}") for i in range(2)]
        s_sel, s_pos, s_pm, s_cn, s_tab = (sem(n) for n in ("s_sel", "s_pos", "s_pm", "s_cn", "s_tab"))
        s_H, s_si, s_hd, s_ht, s_hc, s_sO, s_ya, s_yv = (sem(n) for n in ("s_H", "s_si", "s_hd", "s_ht", "s_hc", "s_sO", "s_ya", "s_yv"))
        s_ys = [sem(f"s_ys{i}") for i in range(2)]
        e_w = [sem(f"e_w{b}") for b in range(2)]
        e_clear = sem("e_clear")
        e_dma = sem("e_dma")
        f_y, f_o = [sem(f"f_y{j}") for j in range(4)], [sem(f"f_o{j}") for j in range(4)]
        f_s = sem("f_s")
        early.close()
        three = lambda n: [sem(f"e_{n}{j}") for j in range(3)]
        e_xg, e_sc = three("xg"), three("sc")
        e_oh, e_lst, e_red, e_idx, e_T, e_xT, e_H, e_si, e_hid, e_hT, e_hc, e_O, e_oba, e_obv = (
            three(n) for n in ("oh", "lst", "red", "idx", "T", "xT", "H", "si", "hid", "hT", "hc", "O", "oba", "obv"))
        e_go = sem("e_go")
        e_w += [sem(f"e_w{b}") for b in (2, 3)]

        class Chain:

            def __init__(self, eng, s):
                self.eng, self.s, self.n = eng, s, 0

            def __call__(self, ins):
                self.n += 1
                ins.then_inc(self.s, 1)
                self.eng.wait_ge(self.s, self.n)

        def block_ready(eng, b):
            n = sum(NDMA.get(f"{k}{j}", 1) for k, j in order[place[b] % 3:place[b] + 1:3])
            eng.wait_ge(s_ring[place[b] % 3], 16 * n)

        def block_done(eng, b):
            kind, j = b
            if kind == "ada":
                eng.wait_ge(s_part, j + 1)
            elif kind == "w":
                eng.wait_ge(s_pj, 8 * (j + 1))
            elif kind == "wb":
                eng.wait_ge(s_br, 16 * (j + 1))
            else:
                eng.wait_ge(s_mx, NT)

        def rows_stored(eng, row, n):
            for r in range(max(row, row + n - 4), row + n):
                eng.wait_ge(s_st[r % 4], 16 * (r // 4 + 1))

        def rms_scale(link, ss, width, out_):
            v, n = nc.vector, ss.shape[1]
            x, y, z = (newton[:, j, 0:n] for j in range(3))
            link(v.tensor_scalar(x, ss, 1.0 / width, EPS, ALU.mult, ALU.add))
            link(v.tensor_scalar(y.bitcast(I32), x.bitcast(I32), 1, None, ALU.logical_shift_right))
            link(v.tensor_scalar(y.bitcast(I32), y.bitcast(I32), -1.0, float(0x5F3759DF), ALU.mult, ALU.add))
            for step in range(3):
                link(v.tensor_tensor(z, y, y, ALU.mult))
                link(v.tensor_tensor(z, z, x, ALU.mult))
                link(v.tensor_scalar(z, z, -0.5, 1.5, ALU.mult, ALU.add))
                link(v.tensor_tensor(out_ if step == 2 else y, y, z, ALU.mult))

        def done(eng, s, n):
            eng.wait_ge(s, n + 1)

        def all_done(eng, *items):
            for s, n in items:
                done(eng, s, n)
            eng.sem_inc(e_go, 1)

        def skipped(eng, s, n, k=1):
            done(eng, s, n)
            eng.sem_inc(s, k)

        NC = T // P
        ND = NC - 2
        block = ctx.enter_context(nc.Block())

        @block.sync
        def _(sp):
            rows = lambda v, r: v.rearrange("o (r p) -> (o r) p", r=r)
            sp.dma_start(vrow[0:48, :], rows(a["ada_b"], 48)).then_inc(s_vec, 16)
            sp.dma_start(vrow[48:56, :], rows(a["norm1_g"], 8)).then_inc(s_vec, 16)
            sp.dma_start(vrow[56:64, :], rows(a["norm2_g"], 8)).then_inc(s_vec, 16)
            sp.dma_start(vrow[64:72, :], rows(a["c"], 8)).then_inc(s_vec, 16)
            sp.dma_start(vrow[72:88, :], a["mlstm_conv"][0].rearrange("w (r p) -> (w r) p", p=P)).then_inc(s_vec, 16)
            sp.dma_start(bff[:, :], a["fox_bf"].rearrange("o h -> h o")).then_inc(s_vec, 16)
            for n in range(2):
                sp.dma_start(xs[:, 4 * n:4 * n + 4, :],
                             a["x"][0, 4 * P * n:4 * P * (n + 1), :].rearrange("(i p) d -> p i d", p=P)).then_inc(s_x[n], 16)
            for c0, n, name in ((0, FH, "ff"), (FH, 2 * MH, "mi")):
                sp.dma_start(wsm[:, :, c0:c0 + n],
                             w_in[:, col[name]:col[name] + n].rearrange("(k p) n -> p k n", p=P)).then_inc(s_wsm, 16)

            sp.dma_start(bmi[:, :], a["mlstm_bi"].rearrange("o h -> h o")).then_inc(s_nd, 16)
            sp.dma_start(bmf[:, :], a["mlstm_bf"].rearrange("o h -> h o")).then_inc(s_nd, 16)
            for dst, name in ((gq, "fox_q_g"), (gk, "fox_k_g"), (gml, "mlstm_norm_g"), (ghg, "hgrn_norm_g")):
                sp.dma_start(dst[:, :], a[name].partition_broadcast(P).rearrange("b o n -> b (o n)")).then_inc(s_nd, 16)

            def load_block(n):
                kind, j = order[n]
                if n >= 3:
                    block_done(sp, order[n - 3])
                dst = ring[:, n % 3]
                if kind == "ada":
                    src = a["ada_w"][0][:, j * BW:(j + 1) * BW].rearrange("(k p) n -> p k n", p=P)
                elif kind == "w":
                    c0 = col[TBLOCKS[j]] if j < 10 else col["gates"] + BW * (j - 10)
                    src = w_in[:, c0:c0 + BW].rearrange("(k p) n -> p k n", p=P)
                elif kind == "wb":
                    src = a["w_branch"][0, j].rearrange("(k p) n -> p k n", p=P)
                    dst = flat(dst).rearrange("p (k n) -> p k n", k=4)
                elif kind == "wo":
                    src = a["w_out"][0][:, BW * j:BW * (j + 1)].rearrange("(k p) n -> p k n", p=P)
                elif j == 0:
                    sp.dma_start(dst[:, :, 0:FF], a["sh_w1"][0].rearrange("(p k) f -> p k f", k=KD)).then_inc(s_ring[n % 3], 16)
                    src, dst = a["sh_w3"][0].rearrange("(p k) f -> p k f", k=KD), dst[:, :, FF:2 * FF]
                else:
                    src, dst = a["sh_w2"][0].rearrange("(k p) n -> p k n", p=P), shw2
                sp.dma_start(dst, src).then_inc(s_ring[n % 3], 16)

            nxt = 0

            def store_rows(u):
                sp.wait_ge(s_ev, u + 1)
                sp.dma_start(proj_d[u - U_B], stg[u % 4]).then_inc(s_st[(u - U_B) % 4], 16)

            for u in range(U_B, NU + 1):
                while nxt < len(order) - 1 and (nxt < 3 or order[nxt - 3][0] == "ada" or
                                                (order[nxt - 3][0] == "w" and 8 * order[nxt - 3][1] + 7 <= u)):
                    load_block(nxt)
                    nxt += 1
                if u < NU:
                    store_rows(u)
            while nxt < len(order) - 1:
                load_block(nxt)
                nxt += 1
            for i in range(NT):
                sp.wait_ge(s_x2, i + 1)
                sp.dma_start(x2_d[i * P:(i + 1) * P, :], x2[i % 2]).then_inc(s_so[i % 2], 16)
                sp.wait_ge(s_h2, i + 1)
                sp.dma_start(h2_d[i * P:(i + 1) * P, :], h2[i % 2]).then_inc(s_so[i % 2], 16)
            load_block(len(order) - 1)

            def load_expert(e, b):
                sp.dma_start(w13[b][:, :, 0:FF], a["exp_w1"][0, e].rearrange("(p k) f -> p k f", k=KD)).then_inc(e_w[b], 16)
                sp.dma_start(w13[b][:, :, FF:2 * FF], a["exp_w3"][0, e].rearrange("(p k) f -> p k f", k=KD)).then_inc(e_w[b], 16)
                sp.dma_start(w2[b], a["exp_w2"][0, e].rearrange("(k p) n -> p k n", p=P)).then_inc(e_w[b], 16)

            for b in range(2):
                load_expert(b, b)
            for i in range(NT):
                sp.wait_ge(s_ya, i + 1)
                sp.wait_ge(s_yv, i + 1)
                if i == 0:
                    sp.dma_start(y_d[T:T + P, :], ysh[0]).then_inc(s_ys[0], 16)
                sp.dma_start(y_d[i * P:(i + 1) * P, :], ysh[i % 2]).then_inc(s_ys[i % 2], 16)
            sp.wait_ge(e_clear, 1)
            for b in range(2, 4):
                load_expert(b, b)
            with sp.Fori(1, NE // 4) as it:
                for q in range(4):
                    e = 4 * it + q
                    for j, n in ((0, e - 3), (1, e - 3), (2, ND * (e - 3))):
                        done(sp, e_oba[j], n)
                        done(sp, e_obv[j], n)
                    load_expert(e, q)
            for j, n in ((0, NE), (1, NE), (2, ND * NE)):
                done(sp, e_sc[j], n)
            for i in range(NT):
                if i >= 4:
                    sp.wait_ge(f_o[i % 4], 16 * (i // 4))
                sp.dma_start(fy[i % 4], y_d[i * P:(i + 1) * P, :]).then_inc(f_y[i % 4], 16)
                sp.dma_start(fx[i % 4], x2_d[i * P:(i + 1) * P, :]).then_inc(f_y[i % 4], 16)
            for j in range(4):
                sp.wait_ge(f_o[j], 16 * (NT // 4))

        @block.gpsimd
        def _(pool):
            g = nc.gpsimd
            link = Chain(pool, s_pool)
            g.iota(sI, pattern=[[0, P]], base=0, channel_multiplier=1).then_inc(s_iota, 1)
            g.iota(tI, pattern=[[1, P]], base=0, channel_multiplier=0).then_inc(s_iota, 1)
            g.iota(tokI, pattern=[[P, NT]], base=-FAR, channel_multiplier=1).then_inc(s_iota, 1)
            link(g.memset(ident[:, :], 0.0))
            link(g.memset(ones[:, :], 1.0))
            link(g.memset(foxmask[:, :], 0.0))
            g.affine_select(out=ident[:, :], in_=ident[:, :], compare_op=ALU.not_equal, fill=1.0, base=0,
                            pattern=[[-1, P]], channel_multiplier=1).then_inc(s_pconst, 1)
            g.affine_select(out=upper[:, :], in_=ones[:, :], compare_op=ALU.is_ge, fill=0.0, base=0,
                            pattern=[[1, P]], channel_multiplier=-1).then_inc(s_pconst, 1)
            g.affine_select(out=strict[:, :], in_=ones[:, :], compare_op=ALU.is_ge, fill=0.0, base=-1,
                            pattern=[[1, P]], channel_multiplier=-1).then_inc(s_pconst, 1)
            g.affine_select(out=foxmask[:, :], in_=foxmask[:, :], compare_op=ALU.is_ge, fill=NEG, base=0,
                            pattern=[[-1, P]], channel_multiplier=1).then_inc(s_pconst, 1)
            pool.wait_ge(s_xt, NT)
            for j in range(4, NADA):
                if j > 4:
                    pool.wait_ge(s_part, j)
                g.dma_start(adax, a["ada_w"][0][:, j * BW:(j + 1) * BW].rearrange("(k p) n -> p k n", p=P)).then_inc(s_ada, 16)
            pool.wait_ge(s_fr, 1)
            g.dma_start(frow_d, R[2][0:FH, :]).then_inc(s_rd, 16)
            pool.wait_ge(s_mr, 1)
            g.dma_start(mrow_d, R[7][0:MH, :]).then_inc(s_rd, 16)
            pool.wait_ge(s_mf, 1)
            g.dma_start(mdec_d, R[1][0:MH, 0:NT]).then_inc(s_rd, 16)
            pool.wait_ge(s_rd, 48)
            g.dma_start(mdec[:, :, :], mdec_d.partition_broadcast(P)).then_inc(s_rd, 16)
            pool.wait_ge(s_mct, 1)
            for h in range(FH):
                if h >= 2:
                    pool.wait_ge(s_pl, NT * (h - 1))
                g.dma_start(ncb[h % 2], frow_d[h:h + 1, :].partition_broadcast(P).rearrange("b o t -> b (o t)")
                            ).then_inc(s_nc[h % 2], 16)
            pool.wait_ge(s_y, FSTEPS)
            for j in range(2):
                g.memset(conv_in[j][:, 0:TAPS - 1], 0.0).then_inc(s_pad, 1)
            rows_stored(pool, R_MO, 8)
            g.dma_start(mo, proj_d[R_MO:R_MO + 8].rearrange("r p n -> p r n")).then_inc(s_mo, 16)
            for j in range(4):
                if j >= 2:
                    pool.wait_ge(s_cv, j - 1)
                if j == 0:
                    pool.wait_ge(s_pad, 2)
                rows_stored(pool, R_MQK + 2 * j, 2)
                g.dma_start(conv_in[j % 2][:, TAPS - 1:TAPS - 1 + T].rearrange("p (r n) -> p r n", r=2),
                            proj_d[R_MQK + 2 * j:R_MQK + 2 * j + 2].rearrange("r p n -> p r n")).then_inc(s_cin[j % 2], 16)
            pool.wait_ge(s_fyt, NT)
            g.memset(vaug[:, :, :, MV:MV + 1], 1.0).then_inc(s_pad, 1)
            rows_stored(pool, R_MV, 8)
            for i in range(NT):
                g.dma_start(vaug[:, i, :, 0:MV], proj_d[R_MV + i].rearrange("p (h v) -> p h v", h=MH)).then_inc(s_va, 16)
            pool.wait_ge(s_cv, 4)
            g.memset(mC, 0.0).then_inc(s_pad, 1)

            def spread_m(c):
                g.dma_start(nmb[c % 2], mrow_d[:, c * P:(c + 1) * P].partition_broadcast(P)).then_inc(s_nm[c % 2], 16)

            spread_m(0)
            spread_m(1)
            for c in range(NT):
                pool.wait_ge(m_e, c + 1)
                g.tensor_tensor(mw, mw, upper[:, :].unsqueeze(1).to_broadcast([P, MH, P]), ALU.mult).then_inc(m_k, 1)
                if c + 2 < NT:
                    pool.wait_ge(m_w, c + 1)
                    spread_m(c + 2)
            def load_zq(h):
                for dst, r in ((hz, R_HF), (hq, R_HQ)):
                    g.dma_start(dst.rearrange("p (r n) -> p r n", r=2),
                                proj_d[r + 2 * h:r + 2 * h + 2].rearrange("r p n -> p r n")).then_inc(h_zq, 16)

            def load_vg(h):
                for dst, r in ((hv, R_HI), (hg, R_HG)):
                    g.dma_start(dst.rearrange("p (r n) -> p r n", r=NT),
                                proj_d[r:r + NT, :, h * P:(h + 1) * P].rearrange("r p n -> p r n")).then_inc(h_vg, 16)

            pool.wait_ge(m_yt, NT)
            pool.wait_ge(m_st, NT)
            load_zq(0)
            load_vg(0)
            for h in range(1, HH):
                pool.wait_ge(h_S, 8 * h)
                load_zq(h)
                pool.wait_ge(h_y, h)
                load_vg(h)
            pool.wait_ge(h_yt, HH)
            for n in range(48):
                br, j, half = n // 16, n // 2 % 8, n % 2
                row = R_G + (br * 2 + j // 4) * 8 + (j % 4) * 2 + half
                if n >= 3:
                    pool.wait_ge(s_pr, n - 2)
                rows_stored(pool, row, 1)
                g.dma_start(gt[n % 3], proj_d[row]).then_inc(s_g[n % 3], 16)
            pool.wait_ge(s_mg, 32)
            g.dma_start(rwt, a["router_w"][0].rearrange("(p k) e -> p k e", k=KD)).then_inc(s_rw, 16)
            pool.wait_ge(s_bc, 8)
            g.dma_start(rbias, a["router_bias"][0:1, :].partition_broadcast(P).rearrange("b o e -> b (o e)")).then_inc(s_rw, 16)
            for i in range(NT):
                if i >= 2:
                    pool.wait_ge(s_x2, i - 1)
                g.dma_start(xin[i % 2], a["x"][0, i * P:(i + 1) * P, :]).then_inc(s_xi[i % 2], 16)
            pool.wait_ge(s_sO, NT)
            pool.wait_ge(s_ys[0], 16 * (NT // 2 + 1))
            pool.wait_ge(s_ys[1], 16 * (NT // 2))
            pool.wait_ge(s_so[0], 16 * NT)
            pool.wait_ge(s_so[1], 16 * NT)
            pool.wait_ge(s_ya, NT)
            pool.wait_ge(s_yv, NT)
            for q in (e_oh, e_lst, e_red, e_idx, e_xg, e_T, e_xT, e_H, e_si, e_hid, e_hT, e_hc, e_O, e_oba, e_obv, e_sc):
                for j in range(3):
                    pool.sem_clear(q[j])
            for x in (e_go, *e_w[2:]):
                pool.sem_clear(x)
            pool.sem_inc(e_clear, 1)
            for j in range(3):
                link(g.memset(xg[j], 0.0))
            for q in (e_xg[1:], e_sc):
                for x in q:
                    pool.sem_inc(x, 1)

            def gather(j, q):
                return g.indirect_dma_start(xg[j], None, h2_d, bass.IndirectOffsetOnAxis(ap=idx[:, 4 * j + q:4 * j + q + 1], axis=0),
                                            bounds_check=T - 1, oob_is_err=False)

            landings = pool.alloc_register("landings")
            pool.reg_mov(landings, 0)

            def landed(s):
                pool.reg_add(landings, landings, 16)
                pool.wait_ge(e_dma, pool.snap(landings))
                pool.sem_inc(s, 1)

            def scatter(j, q):
                g.indirect_dma_start(y_d, bass.IndirectOffsetOnAxis(ap=idx[:, 4 * j + q:4 * j + q + 1], axis=0), ob[j], None,
                                     bounds_check=T + P - 1, oob_is_err=True, compute_op=ALU.add).then_inc(e_dma, 16)

            done(pool, e_idx[0], 1)
            done(pool, e_idx[1], 1)
            gather(0, 0).then_inc(e_xg[0], 16)
            gather(1, 0).then_inc(e_dma, 16)
            landed(e_xg[1])
            done(pool, e_T[0], 1)
            done(pool, e_idx[0], 2)
            gather(0, 1).then_inc(e_xg[0], 16)
            with pool.Fori(0, NE // 4) as it:
                for q in range(4):
                    e = 4 * it + q
                    n_e = pool.value_load(cnt[0:1, bass.ds(e, 1)], min_val=0, max_val=T)
                    n_next = pool.value_load(cnt[0:1, bass.ds(e + 1, 1)], min_val=0, max_val=T)
                    all_done(pool, (e_T[1], e + 1), (e_idx[1], e + 2))
                    with pool.If(n_next > P):
                        gather(1, (q + 1) % 4).then_inc(e_dma, 16)
                        landed(e_xg[1])
                    with pool.Else():
                        pool.sem_inc(e_xg[1], 1)
                    all_done(pool, (e_idx[0], e + 3), (e_T[0], e + 2))
                    gather(0, (q + 2) % 4).then_inc(e_xg[0], 16)
                    all_done(pool, (e_oba[0], e + 1), (e_obv[0], e + 1))
                    scatter(0, q)
                    landed(e_sc[0])
                    with pool.If(n_e > P):
                        all_done(pool, (e_oba[1], e + 1), (e_obv[1], e + 1))
                        scatter(1, q)
                        landed(e_sc[1])
                    with pool.Else():
                        pool.sem_inc(e_sc[1], 1)
                    with pool.If(n_e > 2 * P):
                        with pool.Fori(0, ND) as c:
                            n = ND * e + c
                            with pool.If(n_e > P * (c + 2)):
                                all_done(pool, (e_idx[2], n + 1), (e_T[2], n))
                                gather(2, 0).then_inc(e_dma, 16)
                                landed(e_xg[2])
                                all_done(pool, (e_oba[2], n + 1), (e_obv[2], n + 1))
                                scatter(2, 0)
                                landed(e_sc[2])
                            with pool.Else():
                                pool.sem_inc(e_xg[2], 1)
                                pool.sem_inc(e_sc[2], 1)
                            pool.nop()
                    with pool.Else():
                        pool.sem_inc(e_xg[2], ND)
                        pool.sem_inc(e_sc[2], ND)
                    pool.nop()

        @block.tensor
        def _(pe):
            t = nc.tensor

            def ada(j):
                pe.wait_ge(s_part, j + 1)
                if j > 0:
                    pe.wait_ge(s_modc, j)
                for c in range(4):
                    mm = t.matmul(psum[:, 7, 4 * j + c:4 * j + c + 1], part[j % 2][:, c * P:(c + 1) * P], ones[:, 0:1],
                                  start=True, stop=True)
                mm.then_inc(s_mod, 1)

            def project(u):
                q, v = divmod(u, 8)
                if v == 0:
                    block_ready(pe, ("w", q))
                if u >= 3:
                    pe.wait_ge(s_ev, u - 2)
                w = slot(("w", q))
                for k in range(KD):
                    if q in TRANSPOSED:
                        l, r = w[:, k, (v // 2) * P:(v // 2 + 1) * P], hT[:, k, (v % 2) * BW:(v % 2 + 1) * BW]
                    else:
                        l, r = hT[:, k, v * P:(v + 1) * P], w[:, k, :]
                    mm = t.matmul(bank(u % 3), l, r, start=(k == 0), stop=(k == KD - 1))
                mm.then_inc(s_pj, 1)

            pe.wait_ge(s_vec, 16 * 6)
            pe.wait_ge(s_pconst, 4)
            t.transpose(psum[:, 6, 0:88], vrow[0:88, :], ident[0:88, 0:88]).then_inc(s_vt, 1)
            for j in range(4):
                ada(j)
            for i in range(NT):
                pe.wait_ge(s_xn, i + 1)
                if i >= 2:
                    pe.wait_ge(s_xea, i - 1)
                    pe.wait_ge(s_xed, i - 1)
                for k in range(KD):
                    mm = t.transpose(psum[:, 2 * (i % 2) + k // 4, (k % 4) * P:(k % 4 + 1) * P],
                                     xn[:, i, k * P:(k + 1) * P], ident[:, :])
                mm.then_inc(s_xt, 1)
            pe.wait_ge(s_xea, NT)
            pe.wait_ge(s_xed, NT)
            pe.wait_ge(s_wsm, 32)
            for i in range(NT):
                for k in range(KD):
                    mm = t.matmul(psum[:, 4, i * 16:(i + 1) * 16], hT[:, k, i * P:(i + 1) * P], wsm[:, k, :],
                                  start=(k == 0), stop=(k == KD - 1))
            mm.then_inc(s_sm, 1)
            pe.wait_ge(s_smc, 1)
            for c0, n, b0 in ((0, FH, 0), (FH, MH, 2), (FH + MH, MH, 4)):
                for i in range(NT):
                    mm = t.transpose(psum[0:n, b0 + i // 4, (i % 4) * P:(i % 4 + 1) * P], sm[:, i, c0:c0 + n], ident[:, :])
            mm.then_inc(s_rows, 1)
            pe.wait_ge(s_zr, 3)

            def turn_qk(u):
                pe.wait_ge(s_qn, u + 1)
                if u >= 1:
                    pe.wait_ge(s_qe, u)
                for j in range(4):
                    mm = t.transpose(psum[:, 4, j * P:(j + 1) * P], qn[u % 2][:, j * P:(j + 1) * P], ident[:, :])
                mm.then_inc(s_qt, 1)

            for u in range(U_B):
                project(u)
                if u % 2 == 1 and 3 <= u < 19:
                    ada(4 + (u - 3) // 2)
                if 2 <= u < 18:
                    turn_qk(u - 2)
                if u == 18:
                    pe.wait_ge(s_mf, 1)
                    for q in range(4):
                        for i in range(NT):
                            mm = t.transpose(psum[:, 5, (q * NT + i) * MH:(q * NT + i + 1) * MH],
                                             R[[5, 6, 8, 9][q]][0:MH, i * P:(i + 1) * P], ident[0:MH, 0:MH])
                    mm.then_inc(s_mct, 1)
            pe.wait_ge(s_mcc, 1)
            pe.wait_ge(s_modc, NADA)
            pe.wait_ge(s_qe, 16)
            pe.wait_ge(s_ev, U_B)

            def logits(n):
                h, i = divmod(n, NT)
                b, j, N = FD * (h % 2), h // 2, P * (i + 1)
                if n >= 1:
                    pe.wait_ge(s_pl, n)
                for z in range(-(-N // BW)):
                    m = min(BW, N - BW * z)
                    mm = t.matmul(psum[:, 4 + z, 0:m], qT[b:b + FD, j, i * P:(i + 1) * P],
                                  kT[b:b + FD, j, BW * z:BW * z + m], start=True, stop=True)
                mm.then_inc(s_S, 1)

            def turn_p(n):
                pe.wait_ge(s_p, n + 1)
                if n >= 1:
                    pe.wait_ge(s_pT, n)
                for s in range(n % NT + 1):
                    mm = t.transpose(psum[:, 6 + s // 4, (s % 4) * P:(s % 4 + 1) * P], pl[n % 2][:, s * P:(s + 1) * P], ident[:, :])
                mm.then_inc(s_T, 1)

            def weigh(n):
                h, i = divmod(n, NT)
                pe.wait_ge(s_pT, n + 1)
                if n >= 1:
                    pe.wait_ge(s_y, n)
                for s in range(i + 1):
                    mm = t.matmul(psum[:, 3, 0:FD], pT[n % 2][:, s, :], vf[:, s, h * FD:(h + 1) * FD],
                                  start=(s == 0), stop=(s == i))
                mm.then_inc(s_O, 1)

            for m in range(FSTEPS + 2):
                if m < U_C - U_B:
                    project(U_B + m)
                if m < FSTEPS:
                    logits(m)
                if 1 <= m < FSTEPS + 1:
                    turn_p(m - 1)
                if m >= 2:
                    weigh(m - 2)

            nu = U_C

            def turn4(b, src, s):
                for j in range(4):
                    mm = t.transpose(psum[:, b, j * P:(j + 1) * P], src[:, j * P:(j + 1) * P], ident[:, :])
                mm.then_inc(s, 1)

            pe.wait_ge(s_y, FSTEPS)
            for i in range(NT):
                if i >= 2:
                    pe.wait_ge(s_fyc, i - 1)
                turn4(3 + i % 2, yf[:, i, :], s_fyt)
                if i % 2 == 0:
                    project(nu)
                    nu += 1
            pe.wait_ge(s_fyc, NT)

            def ml_scores(c):
                if c >= 1:
                    pe.wait_ge(m_st, c)
                    pe.wait_ge(m_in, c)
                else:
                    pe.wait_ge(s_sil, 4)
                for j in range(2):
                    t.transpose(psum[:, 3, j * P:(j + 1) * P], mqkT[:, 2 + j, c * P:(c + 1) * P], ident[:, :])
                for h in range(MH):
                    b, j = MQ * (h % 2), h // 2
                    mm = t.matmul(psum[:, (4, 7)[h % 2], j * P:(j + 1) * P], mqkT[b:b + MQ, 2 + j, c * P:(c + 1) * P],
                                  mqkT[b:b + MQ, j, c * P:(c + 1) * P], start=True, stop=True)
                mm.then_inc(m_ST, 1)

            def ml_apply(c):
                pe.wait_ge(m_sc, c + 1)
                pe.wait_ge(m_kw, c + 1)
                if c == 0:
                    pe.wait_ge(s_va, 16 * NT)
                    pe.wait_ge(s_pad, 4)
                else:
                    pe.wait_ge(m_st, c)
                    pe.wait_ge(m_num, c)
                    pe.wait_ge(m_yc, c)
                M1 = MV + 1
                for h in range(MH):
                    b, j, o = MQ * (h % 2), h // 2, (h % 2) * M1
                    t.matmul(psum[:, 5 + j, o:o + M1], msc[:, h, :], vaug[:, c, h, :], start=True, stop=True)
                    t.matmul(psum[:, (4, 7)[h % 2], j * M1:(j + 1) * M1], mqkT[b:b + MQ, j, c * P:(c + 1) * P], mC[b:b + MQ, j, :],
                             start=True, stop=True)
                for h in range(MH):
                    b, j = MQ * (h % 2), h // 2
                    mm = t.matmul(psum[b:b + MQ, 3, j * M1:(j + 1) * M1], mkw[:, h, :], vaug[:, c, h, :], start=True, stop=True)
                mm.then_inc(m_B, 1)

            for c in range(NT):
                project(nu)
                nu += 1
                ml_scores(c)
                if c >= 1:
                    pe.wait_ge(m_y, c)
                    turn4(5, my, m_yt)
                if c % 2 == 0:
                    project(nu)
                    nu += 1
                ml_apply(c)
            project(nu)
            nu += 1
            pe.wait_ge(m_y, NT)
            turn4(5, my, m_yt)
            pe.wait_ge(m_yc, NT)

            for h in range(HH):
                def between(step):
                    nonlocal nu
                    for _ in range(HG_FILL[step]):
                        if nu < NU:
                            project(nu)
                            nu += 1

                for l in range(8):
                    between(l)
                    n = 8 * h + l
                    pe.wait_ge(h_qk, n + 1)
                    if l >= 2:
                        pe.wait_ge(h_sc, n - 1)
                    elif h >= 1:
                        pe.wait_ge(h_yc, h) if l == 1 else pe.wait_ge(h_y, h)
                    b0 = 4 + 2 * (l % 2)
                    for c in range(NT):
                        cs = slice(c * P, (c + 1) * P)
                        if l < 7:
                            x, y = hE[l % 2][:, cs], hE[l % 2][:, cs]
                        else:
                            x, y = hk[:, cs], hq[:, cs]
                        mm = t.matmul(psum[:, b0 + c // 4, (c % 4) * P:(c % 4 + 1) * P], x, y, start=True, stop=True)
                    mm.then_inc(h_S, 1)
                between(8)
                pe.wait_ge(h_kd, h + 1)
                pe.wait_ge(h_sc, 8 * h + 7)
                for c in range(NT):
                    mm = t.transpose(psum[:, 4 + c // 4, (c % 4) * P:(c % 4 + 1) * P], hkd[:, c * P:(c + 1) * P], ident[:, :])
                mm.then_inc(h_kt, 1)
                between(9)
                pe.wait_ge(h_kc, h + 1)
                pe.wait_ge(h_vg, 32 * (h + 1))
                pe.wait_ge(h_sc, 8 * h + 8)
                for c in range(NT):
                    mm = t.matmul(psum[:, 6 + c // 4, (c % 4) * P:(c % 4 + 1) * P], hkT[:, c * P:(c + 1) * P],
                                  hv[:, c * P:(c + 1) * P], start=True, stop=True)
                mm.then_inc(h_up, 1)
                between(10)
                pe.wait_ge(h_st, h + 1)
                for c in range(NT):
                    cs = slice(c * P, (c + 1) * P)
                    o = psum[:, 4 + c // 4, (c % 4) * P:(c % 4 + 1) * P]
                    t.matmul(o, hsc[:, cs], hv[:, cs], start=True, stop=False)
                    mm = t.matmul(o, hqe[:, cs], hst[:, cs], start=False, stop=True)
                mm.then_inc(h_O, 1)
                between(11)
                pe.wait_ge(h_y, h + 1)
                for c in range(NT):
                    mm = t.transpose(psum[:, 6 + c // 4, (c % 4) * P:(c % 4 + 1) * P], hkT[:, c * P:(c + 1) * P], ident[:, :])
                mm.then_inc(h_yt, 1)
            assert nu == NU

            pe.wait_ge(h_yc, HH)
            pe.wait_ge(s_ev, NU)
            for n in range(48):
                br, j, half = n // 16, n // 2 % 8, n % 2
                if n % 16 == 0:
                    block_ready(pe, ("wb", br))
                w = flat(slot(("wb", br))).rearrange("p (k n) -> p k n", k=4)
                if n >= 3:
                    pe.wait_ge(s_pr, n - 2)
                for k in range(4):
                    mm = t.matmul(bank(n % 3), w[:, k, j * P:(j + 1) * P], yT[br][:, k, half * BW:(half + 1) * BW],
                                  start=(k == 0), stop=(k == 3))
                mm.then_inc(s_br, 1)
            for n in range(8):
                pe.wait_ge(s_dg, n + 1)
                if n >= 2:
                    pe.wait_ge(s_bcc, n - 1)
                t.matmul(bank(4 + n % 2), ones[:, :], dgb[n % 2].rearrange("p k n -> p (k n)"),
                         start=True, stop=True).then_inc(s_bc, 1)
            pe.wait_ge(s_mg, 32)
            pe.wait_ge(s_bcc, 8)

            def out_proj(i):
                if i == 0:
                    block_ready(pe, ("wo", 0))
                    block_ready(pe, ("wo", 1))
                if i >= 2:
                    pe.wait_ge(s_x2, i - 1)
                for half in range(2):
                    for k in range(KD):
                        mm = t.matmul(bank(2 * (i % 2) + half), hT[:, k, i * P:(i + 1) * P], slot(("wo", half))[:, k, :],
                                      start=(k == 0), stop=(k == KD - 1))
                mm.then_inc(s_mx, 1)

            def route(i):
                pe.wait_ge(s_h2, i + 1)
                if i >= 1:
                    pe.wait_ge(s_h2c, i)
                for k in range(KD):
                    mm = t.transpose(psum[:, 4 + k // 4, (k % 4) * P:(k % 4 + 1) * P], h2[i % 2][:, k * P:(k + 1) * P], ident[:, :])
                mm.then_inc(s_h2t, 1)
                pe.wait_ge(s_h2c, i + 1)
                pe.wait_ge(s_rw, 32)
                if i >= 1:
                    pe.wait_ge(s_sg, i)
                for k in range(KD):
                    mm = t.matmul(psum[:, 6, 0:NE], h2T[:, k, i * P:(i + 1) * P], rwt[:, k, :], start=(k == 0), stop=(k == KD - 1))
                mm.then_inc(s_rt, 1)

            def rank(i):
                pe.wait_ge(s_sel, i + 1)
                if i >= 1:
                    pe.wait_ge(s_pm, i)
                for j in range(i + 1):
                    mm = t.matmul(psum[:, 7, 0:NE], strict[:, :] if j == i else ones[:, :], selall[:, j, :],
                                  start=(j == 0), stop=(j == i))
                mm.then_inc(s_pos, 1)

            for i in range(NT + 2):
                if i < NT:
                    out_proj(i)
                if 1 <= i <= NT:
                    route(i - 1)
                if i >= 2:
                    rank(i - 2)
            pe.wait_ge(s_pm, NT)
            for j in range(NT):
                mm = t.matmul(psum[:, 7, 0:NE], ones[:, :], selall[:, j, :], start=(j == 0), stop=(j == NT - 1))
            mm.then_inc(s_cn, 1)

            def shared_up(i):
                if i == 0:
                    block_ready(pe, ("sh", 0))
                    pe.wait_ge(s_x2, NT)
                if i >= 2:
                    pe.wait_ge(s_hd, i - 1)
                for k in range(KD):
                    mm = t.matmul(bank(i % 2), h2T[:, k, i * P:(i + 1) * P], slot(("sh", 0))[:, k, :], start=(k == 0), stop=(k == KD - 1))
                mm.then_inc(s_H, 1)

            def shared_down(i):
                pe.wait_ge(s_hd, i + 1)
                if i >= 1:
                    pe.wait_ge(s_hc, i)
                for k in range(FK):
                    mm = t.transpose(psum[:, 2, k * P:(k + 1) * P], shh[:, k * P:(k + 1) * P], ident[:, :])
                mm.then_inc(s_ht, 1)
                pe.wait_ge(s_hc, i + 1)
                if i == 0:
                    block_ready(pe, ("sh", 1))
                    pe.wait_ge(s_h2c, NT)
                if i >= 1:
                    pe.wait_ge(s_ya, i)
                    pe.wait_ge(s_yv, i)
                for half in range(2):
                    for k in range(FK):
                        mm = t.matmul(bank(4 + half), shT[:, k, :], shw2[:, k, half * BW:(half + 1) * BW],
                                      start=(k == 0), stop=(k == FK - 1))
                mm.then_inc(s_sO, 1)

            shared_up(0)
            for i in range(NT):
                if i + 1 < NT:
                    shared_up(i + 1)
                shared_down(i)

            def token_list(j, e):
                for i in range(NT):
                    mm = t.matmul(psum[:, 2, 8 * j:8 * j + 6], oh[j][:, i, :], twb[:, i, bass.ds(e, 1), :, :].rearrange("p o s z -> p (o s z)"),
                                  start=(i == 0), stop=(i == NT - 1))
                mm.then_inc(e_lst[j], 1)

            def turn_rows(j):
                for k in range(KD):
                    mm = t.transpose(psum[:, k // 4, (k % 4) * P:(k % 4 + 1) * P], xg[j][:, k * P:(k + 1) * P], ident[:, :])
                mm.then_inc(e_T[j], 1)

            def up(j, b):
                for k in range(KD):
                    mm = t.matmul(bank(3 if j == 0 else 4), xgT[j][:, k, :], w13[b][:, k, :], start=(k == 0), stop=(k == KD - 1))
                mm.then_inc(e_H[j], 1)

            def turn_hidden(j):
                for k in range(FK):
                    mm = t.transpose(psum[:, 5, k * P:(k + 1) * P], hid[j][:, k * P:(k + 1) * P], ident[:, :])
                mm.then_inc(e_hT[j], 1)

            def down(j, b, n):
                for half in range(2):
                    out_read = (e_oba, e_obv)[half]
                    done(pe, out_read[0], e + 1 if j else e)
                    done(pe, out_read[1], e + 1 if j == 2 else e)
                    done(pe, out_read[2], n if j == 2 else ND * e)
                    for k in range(FK):
                        mm = t.matmul(bank(6 + half), hidT[j][:, k, :], w2[b][:, k, half * BW:(half + 1) * BW],
                                      start=(k == 0), stop=(k == FK - 1))
                    mm.then_inc(e_O[j], 1)

            pe.wait_ge(s_tab, 1)
            pe.wait_ge(s_ya, NT)
            pe.wait_ge(s_yv, NT)
            pe.wait_ge(e_clear, 1)
            for s in (e_lst, e_T, e_H, e_hT, e_O):
                for j in range(3):
                    pe.sem_inc(s[j], 1)
            for e in range(2):
                for j in range(2):
                    done(pe, e_oh[j], e + 1)
                    if e == 1:
                        done(pe, e_idx[j], 1)
                    token_list(j, e)
            pe.wait_ge(e_xg[0], 16)
            turn_rows(0)
            done(pe, e_xg[1], 1)
            with pe.Fori(0, NE // 4) as it:
                for q in range(4):
                    e = 4 * it + q
                    n_e = pe.value_load(cnt[0:1, bass.ds(e, 1)], min_val=0, max_val=T)
                    n_after = pe.value_load(cnt[0:1, bass.ds(e + 2, 1)], min_val=0, max_val=T)
                    all_done(pe, (e_xT[0], e + 1), (e_xT[2], ND * e))
                    with pe.If(n_e > P):
                        done(pe, e_xg[1], e + 1)
                        turn_rows(1)
                    with pe.Else():
                        skipped(pe, e_T[1], e)
                    pe.wait_ge(e_w[q], 48 * (it + 1))
                    done(pe, e_hid[0], e)
                    up(0, q)
                    done(pe, e_oh[0], e + 3)
                    done(pe, e_idx[0], e + 2)
                    done(pe, e_idx[1], e + 2)
                    done(pe, e_idx[2], ND * e)
                    all_done(pe, (e_oh[1], e + 3))
                    token_list(0, e + 2)
                    with pe.If(n_after > P):
                        token_list(1, e + 2)
                    with pe.Else():
                        skipped(pe, e_lst[1], e + 2)
                    with pe.If(n_e > P):
                        done(pe, e_xT[1], e + 1)
                        done(pe, e_hid[1], e)
                        done(pe, e_hid[2], ND * e)
                        up(1, q)
                    with pe.Else():
                        skipped(pe, e_H[1], e)
                    done(pe, e_hid[0], e + 1)
                    done(pe, e_hc[1], e)
                    done(pe, e_hc[2], ND * e)
                    turn_hidden(0)
                    pe.wait_ge(e_xg[0], 16 * (e + 2))
                    done(pe, e_xT[1], e + 1)
                    turn_rows(0)
                    all_done(pe, (e_hc[0], e + 1))
                    with pe.If(n_e > P):
                        done(pe, e_hid[1], e + 1)
                        turn_hidden(1)
                    with pe.Else():
                        skipped(pe, e_hT[1], e)
                    down(0, q, e)
                    with pe.If(n_e > P):
                        done(pe, e_hc[1], e + 1)
                        down(1, q, e)
                    with pe.Else():
                        skipped(pe, e_O[1], 2 * e, 2)
                    with pe.If(n_e > 2 * P):
                        all_done(pe, (e_xT[0], e + 2), (e_idx[0], e + 3), (e_idx[1], e + 3), (e_hid[1], e + 1), (e_hc[1], e + 1))
                        with pe.Fori(0, ND) as c:
                            n = ND * e + c
                            with pe.If(n_e > P * (c + 2)):
                                done(pe, e_oh[2], n + 1)
                                token_list(2, e)
                                done(pe, e_xg[2], n + 1)
                                done(pe, e_xT[2], n)
                                turn_rows(2)
                                done(pe, e_xT[2], n + 1)
                                done(pe, e_hid[2], n)
                                up(2, q)
                                done(pe, e_hid[2], n + 1)
                                turn_hidden(2)
                                done(pe, e_hc[2], n + 1)
                                down(2, q, n)
                            with pe.Else():
                                for s in (e_lst, e_T, e_H, e_hT):
                                    skipped(pe, s[2], n)
                                skipped(pe, e_O[2], 2 * n, 2)
                            pe.nop()
                    with pe.Else():
                        for s in (e_lst, e_T, e_H, e_hT):
                            skipped(pe, s[2], ND * e, ND)
                        skipped(pe, e_O[2], 2 * ND * e, 2 * ND)
                    pe.nop()

        @block.scalar
        def _(act):
            s = nc.scalar
            link = Chain(act, s_act)
            act.wait_ge(s_vc, 1)
            s.activation(cond[:, :], vcol[:, 64:72], ACT.Silu).then_inc(s_cond, 1)
            for i in range(NT):
                act.wait_ge(s_x[i // 4], 16)
                s.activation(xn[:, i, :], xs[:, i, :], ACT.Square, accum_out=stat[:, i:i + 1]).then_inc(s_ss, 1)
            act.wait_ge(s_a1, 1)
            for i in range(NT):
                act.wait_ge(s_xt, i + 1)
                for k in range(4):
                    ins = s.activation(hT[:, k, i * P:(i + 1) * P], psum[:, 2 * (i % 2), k * P:(k + 1) * P], ACT.Identity,
                                       bias=mod[:, k:k + 1], scale=a1[:, k:k + 1])
                ins.then_inc(s_xea, 1)

            for n, (z, o, h) in enumerate(((R[0], R[1], FH), (R[4], R[3], MH))):
                act.wait_ge(s_lr, n + 1)
                link(s.activation(o[0:h, :], z[0:h, :], ACT.Abs))
                link(s.activation(o[0:h, :], o[0:h, :], ACT.Exp, scale=-1.0))
                s.activation(o[0:h, :], o[0:h, :], ACT.Ln, bias=1.0).then_inc(s_er, 1)
            act.wait_ge(s_mr, 2)
            s.activation(R[6][0:MH, :], R[6][0:MH, :], ACT.Exp)
            s.activation(R[8][0:MH, :], R[8][0:MH, :], ACT.Exp, scale=-1.0)
            s.activation(R[1][0:MH, 0:NT], R[1][0:MH, 0:NT], ACT.Exp)
            s.activation(R[9][0:MH, :], R[9][0:MH, :], ACT.Exp).then_inc(s_mf, 1)

            def evacuate(u):
                act.wait_ge(s_pj, u + 1)
                if u < 16:
                    if u >= 2:
                        act.wait_ge(s_qn, u - 1)
                    dst = raw[u % 2]
                elif u < U_B:
                    if u == 16:
                        act.wait_ge(s_part, NADA)
                    dst = vf[:, u - 16, :]
                else:
                    dst = stg[u % 4]
                    if u == U_B:
                        act.wait_ge(s_mod, NADA)
                    if u >= U_B + 4:
                        act.wait_ge(s_st[(u - U_B) % 4], 16 * ((u - U_B) // 4))
                s.activation(dst, bank(u % 3), ACT.Copy).then_inc(s_ev, 1)

            def copy_qk(u):
                act.wait_ge(s_qt, u + 1)
                dst, i = (qT, kT)[u // 8], u % 8
                s.activation(dst[:, :, i * P:(i + 1) * P], bank(4).rearrange("p (j n) -> p j n", j=4), ACT.Copy).then_inc(s_qe, 1)

            for u in range(U_B):
                evacuate(u)
                if 2 <= u < 18:
                    copy_qk(u - 2)
                if u == 18:
                    act.wait_ge(s_mct, 1)
                    s.activation(mcol[:, :, :, :].rearrange("p q i h -> p (q i h)"), psum[:, 5, 0:4 * NT * MH], ACT.Copy).then_inc(s_mcc, 1)

            def fox_exp(n):
                N = P * (n % NT + 1)
                act.wait_ge(s_pl, n + 1)
                s.activation(pl[n % 2][:, 0:N], pl[n % 2][:, 0:N], ACT.Exp, bias=stat[:, 16 + n % 2:17 + n % 2],
                             accum_out=stat[:, 18 + n % 4:19 + n % 4]).then_inc(s_p, 1)

            def fox_turned(n):
                N = n % NT + 1
                act.wait_ge(s_T, n + 1)
                if n >= 2:
                    act.wait_ge(s_O, n - 1)
                s.activation(pT[n % 2][:, 0:N, :].rearrange("p s n -> p (s n)"),
                             psum[:, 6:8, :].rearrange("p b n -> p (b n)")[:, 0:N * P], ACT.Copy).then_inc(s_pT, 1)

            for m in range(FSTEPS + 1):
                if m < U_C - U_B:
                    evacuate(U_B + m)
                if m < FSTEPS:
                    fox_exp(m)
                if m >= 1:
                    fox_turned(m - 1)

            nu = U_C
            act.wait_ge(s_O, FSTEPS)
            for i in range(NT):
                act.wait_ge(s_fyt, i + 1)
                s.activation(yTf[:, :, i * P:(i + 1) * P], bank(3 + i % 2).rearrange("p (j n) -> p j n", j=4), ACT.Copy).then_inc(s_fyc, 1)
                if i % 2 == 0:
                    evacuate(nu)
                    nu += 1
            act.wait_ge(s_mo, 16)
            s.activation(mo, mo, ACT.Sigmoid).then_inc(s_mos, 1)
            for j in range(4):
                act.wait_ge(s_cv, j + 1)
                if j < 2:
                    s.activation(mqkT[:, j, :], mqkT[:, j, :], ACT.Silu).then_inc(s_sil, 1)
                else:
                    link(s.activation(mqkT[:, j, :], mqkT[:, j, :], ACT.Silu))
                    s.activation(mqkT[:, j, :], mqkT[:, j, :], ACT.Copy, scale=MQ ** -0.5).then_inc(s_sil, 1)

            def ml_exp(c):
                act.wait_ge(m_w, c + 1)
                s.activation(mw, mw, ACT.Exp).then_inc(m_e, 1)

            def ml_inter(c):
                act.wait_ge(m_B, c + 1)
                if c >= 1:
                    act.wait_ge(m_y, c)
                for h in range(MH):
                    o = (h // 2) * (MV + 1)
                    ins = s.activation(mnum[:, h, :], psum[:, (4, 7)[h % 2], o:o + MV + 1], ACT.Copy, scale=mcol[:, 1, c, h:h + 1])
                ins.then_inc(m_in, 1)

            def ml_turned(c):
                act.wait_ge(m_yt, c + 1)
                s.activation(yTm[:, :, c * P:(c + 1) * P], bank(5).rearrange("p (j n) -> p j n", j=4), ACT.Copy).then_inc(m_yc, 1)

            for c in range(NT):
                ml_exp(c)
                evacuate(nu)
                nu += 1
                if c >= 1:
                    ml_turned(c - 1)
                if c % 2 == 0:
                    evacuate(nu)
                    nu += 1
                ml_inter(c)
            evacuate(nu)
            nu += 1
            ml_turned(NT - 1)

            for h in range(HH):
                act.wait_ge(h_zq, 32 * (h + 1))
                act.wait_ge(h_vg, 32 * (h + 1))
                s.activation(hq, hq, ACT.Silu)
                link(s.activation(hg, hg, ACT.Silu))
                link(s.activation(hE0, hz, ACT.Abs))
                link(s.activation(hE0, hE0, ACT.Exp, scale=-1.0))
                s.activation(hE0, hE0, ACT.Ln, bias=1.0).then_inc(h_ab, 1)
                evacuate(nu)
                nu += 1
                act.wait_ge(h_lf, h + 1)
                s.activation(hk, hk, ACT.Exp).then_inc(h_k, 1)
                act.wait_ge(h_a, h + 1)
                s.activation(hqe, ha, ACT.Exp).then_inc(h_ea, 1)
                act.wait_ge(h_d, h + 1)
                s.activation(hkd, hkd, ACT.Exp).then_inc(h_de, 1)
                for step in range(12):
                    if step < 7:
                        act.wait_ge(h_x, 7 * h + step + 1)
                        s.activation(hE[step % 2], hE[step % 2], ACT.Exp).then_inc(h_e, 1)
                    for n in range(HG_FILL[step]):
                        if (step > 0 or n > 0) and nu < NU:
                            evacuate(nu)
                            nu += 1
                    if step == 8:
                        act.wait_ge(h_kt, h + 1)
                        s.activation(hkT, psum[:, 4:6, :].rearrange("p b n -> p (b n)"), ACT.Copy).then_inc(h_kc, 1)
                act.wait_ge(h_yt, h + 1)
                s.activation(yTh[:, h, :], psum[:, 6:8, :].rearrange("p b n -> p (b n)"), ACT.Copy).then_inc(h_yc, 1)

            for n in range(48):
                act.wait_ge(s_g[n % 3], 16 * (n // 3 + 1))
                s.activation(gt[n % 3], gt[n % 3], ACT.Sigmoid).then_inc(s_gs, 1)
            for n in range(8):
                act.wait_ge(s_bc, n + 1)
                v = (g1b, a2b, b2b, g2b)[n // 2]
                s.activation(v[:, (n % 2) * BW:(n % 2 + 1) * BW], bank(4 + n % 2), ACT.Copy).then_inc(s_bcc, 1)

            def squares(i):
                act.wait_ge(s_x2, i + 1)
                if i >= 1:
                    act.wait_ge(s_sq, i)
                s.activation(dsc, x2[i % 2], ACT.Square, accum_out=stat[:, 32 + i:33 + i]).then_inc(s_sq, 1)

            def routed(i):
                act.wait_ge(s_h2t, i + 1)
                s.activation(h2T[:, :, i * P:(i + 1) * P], psum[:, 4:6, :].rearrange("p b (k n) -> p (b k) n", k=4), ACT.Copy).then_inc(s_h2c, 1)
                act.wait_ge(s_rt, i + 1)
                if i >= 1:
                    act.wait_ge(s_sel, i)
                s.activation(sco, psum[:, 6, 0:NE], ACT.Sigmoid).then_inc(s_sg, 1)

            for i in range(NT + 1):
                if i < NT:
                    squares(i)
                if i >= 1:
                    routed(i - 1)
            for i in range(NT):
                act.wait_ge(s_H, i + 1)
                if i >= 1:
                    act.wait_ge(s_hd, i)
                s.activation(sgm, bank(i % 2)[:, 0:FF], ACT.Silu).then_inc(s_si, 1)
                act.wait_ge(s_ht, i + 1)
                if i >= 1:
                    act.wait_ge(s_sO, i)
                s.activation(shT.rearrange("p k n -> p (k n)"), psum[:, 2, 0:FF], ACT.Copy).then_inc(s_hc, 1)
                act.wait_ge(s_sO, i + 1)
                if i >= 2:
                    act.wait_ge(s_ys[i % 2], 16 * (i // 2 + 1 - i % 2))
                s.activation(ysh[i % 2][:, 0:BW], bank(4), ACT.Copy).then_inc(s_ya, 1)

            def rows_turned(j):
                s.activation(xgT[j].rearrange("p k n -> p (k n)"), psum[:, 0:2, :].rearrange("p b n -> p (b n)"), ACT.Copy).then_inc(e_xT[j], 1)

            def silu(j):
                s.activation(sg[j], bank(3 if j == 0 else 4)[:, 0:FF], ACT.Silu).then_inc(e_si[j], 1)

            def hidden_turned(j):
                s.activation(hidT[j].rearrange("p k n -> p (k n)"), psum[:, 5, 0:FF], ACT.Copy).then_inc(e_hc[j], 1)

            def weigh_out(j, q):
                s.activation(ob[j][:, 0:BW], bank(6), ACT.Copy, scale=lst[:, 4 * j + q, 1:2]).then_inc(e_oba[j], 1)

            act.wait_ge(s_ys[0], 16 * (NT // 2 + 1))
            act.wait_ge(s_ys[1], 16 * (NT // 2))
            act.wait_ge(s_tab, 1)
            act.wait_ge(e_clear, 1)
            for q in (e_xT, e_si, e_hc, e_oba):
                for j in range(3):
                    act.sem_inc(q[j], 1)
            done(act, e_T[0], 1)
            rows_turned(0)
            with act.Fori(0, NE // 4) as it:
                for q in range(4):
                    e = 4 * it + q
                    n_e = act.value_load(cnt[0:1, bass.ds(e, 1)], min_val=0, max_val=T)
                    with act.If(n_e > P):
                        done(act, e_T[1], e + 1)
                        rows_turned(1)
                    with act.Else():
                        skipped(act, e_xT[1], e)
                    done(act, e_H[0], e + 1)
                    silu(0)
                    with act.If(n_e > P):
                        done(act, e_H[1], e + 1)
                        silu(1)
                    with act.Else():
                        skipped(act, e_si[1], e)
                    done(act, e_hT[0], e + 1)
                    hidden_turned(0)
                    done(act, e_T[0], e + 2)
                    rows_turned(0)
                    with act.If(n_e > P):
                        done(act, e_hT[1], e + 1)
                        hidden_turned(1)
                    with act.Else():
                        skipped(act, e_hc[1], e)
                    done(act, e_O[0], 2 * e + 1)
                    done(act, e_sc[0], e)
                    weigh_out(0, q)
                    with act.If(n_e > P):
                        done(act, e_O[1], 2 * e + 1)
                        done(act, e_sc[1], e)
                        weigh_out(1, q)
                    with act.Else():
                        skipped(act, e_oba[1], e)
                    with act.If(n_e > 2 * P):
                        with act.Fori(0, ND) as c:
                            n = ND * e + c
                            with act.If(n_e > P * (c + 2)):
                                done(act, e_T[2], n + 1)
                                rows_turned(2)
                                done(act, e_H[2], n + 1)
                                silu(2)
                                done(act, e_hT[2], n + 1)
                                hidden_turned(2)
                                done(act, e_O[2], 2 * n + 1)
                                done(act, e_sc[2], n)
                                weigh_out(2, 0)
                            with act.Else():
                                for x in (e_xT, e_si, e_hc, e_oba):
                                    skipped(act, x[2], n)
                            act.nop()
                    with act.Else():
                        for x in (e_xT, e_si, e_hc, e_oba):
                            skipped(act, x[2], ND * e, ND)
                    act.nop()
            for i in range(NT):
                act.wait_ge(f_s, i + 1)
                act.dma_start(out[0, i * P:(i + 1) * P, :], fy[i % 4]).then_inc(f_o[i % 4], 16)
            for j in range(4):
                act.wait_ge(f_o[j], 16 * (NT // 4))

        @block.vector
        def _(dve):
            v = nc.vector
            link = Chain(dve, s_dve)

            dve.wait_ge(s_iota, 3)
            v.tensor_copy(col_i[:, :], tI)
            v.tensor_copy(tok[:, :], tokI)
            v.tensor_scalar(dump[:, :], sI[:, 0:1], float(T), None, ALU.add)
            link(v.tensor_tensor(xI, sI, tI, ALU.bitwise_xor))
            dve.wait_ge(s_pconst, 4)
            for l in range(7):
                link(v.tensor_scalar(shI, xI, l, None, ALU.logical_shift_right))
                link(v.tensor_scalar(eqf, shI, 1.0, None, ALU.is_equal))
                link(v.tensor_tensor(levels[:, l, :], eqf, upper[:, :], ALU.mult))
            v.tensor_copy(levels[:, 7, :], ident[:, :]).then_inc(s_dconst, 1)
            dve.wait_ge(s_vt, 1)
            v.tensor_copy(vcol[:, :], psum[:, 6, 0:88]).then_inc(s_vc, 1)
            dve.wait_ge(s_vc, 1)
            dve.wait_ge(s_ss, NT)
            rms_scale(link, stat[:, 0:NT], D, stat[:, 8:8 + NT])
            for i in range(NT):
                v.tensor_scalar(xn[:, i, :], xs[:, i, :], stat[:, 8 + i:9 + i], None, ALU.mult).then_inc(s_xn, 1)

            def mod_columns(j):
                dve.wait_ge(s_mod, j + 1)
                v.tensor_tensor(mod[:, 4 * j:4 * j + 4], psum[:, 7, 4 * j:4 * j + 4], vcol[:, 4 * j:4 * j + 4], ALU.add).then_inc(s_modc, 1)

            def partial_sums(j):
                if j < 4:
                    block_ready(dve, ("ada", j))
                else:
                    dve.wait_ge(s_ada, 16 * (j - 3))
                if j >= 2:
                    dve.wait_ge(s_mod, j - 1)
                w, y = slot(("ada", j)) if j < 4 else adax, part[j % 2]
                link(v.tensor_scalar(y, w[:, 0, :], cond[:, 0:1], None, ALU.mult))
                for k in range(1, KD):
                    ins = v.scalar_tensor_tensor(out=y, in0=w[:, k, :], scalar=cond[:, k:k + 1], in1=y, op0=ALU.mult, op1=ALU.add)
                    if k < KD - 1:
                        link(ins)
                ins.then_inc(s_part, 1)

            dve.wait_ge(s_cond, 1)
            for j in range(4):
                partial_sums(j)
                if j >= 1:
                    mod_columns(j - 1)
            mod_columns(3)
            dve.wait_ge(s_modc, 4)
            v.scalar_tensor_tensor(out=a1[:, :], in0=mod[:, 8:16], scalar=1.0, in1=vcol[:, 48:56], op0=ALU.add, op1=ALU.mult).then_inc(s_a1, 1)
            dve.wait_ge(s_a1, 1)
            for i in range(NT):
                dve.wait_ge(s_xt, i + 1)
                for k in range(4, 8):
                    ins = v.tensor_scalar(hT[:, k, i * P:(i + 1) * P], psum[:, 2 * (i % 2) + 1, (k - 4) * P:(k - 3) * P],
                                          a1[:, k:k + 1], mod[:, k:k + 1], ALU.mult, ALU.add)
                ins.then_inc(s_xed, 1)
            dve.wait_ge(s_nd, 16 * 6)
            link(v.tensor_scalar(gq[:, :], gq[:, :], FD ** -0.5, None, ALU.mult))
            dve.wait_ge(s_sm, 1)
            v.tensor_copy(sm[:, :, :].rearrange("p i n -> p (i n)"), psum[:, 4, 0:NT * 16]).then_inc(s_smc, 1)
            dve.wait_ge(s_rows, 1)
            dve.wait_ge(s_xea, NT)
            wide = lambda b, n: psum[0:n, b:b + 2, :].rearrange("p b n -> p (b n)")
            r = lambda j, n=MH: R[j][0:n, :]
            for j, b, n, bias in ((0, 0, FH, bff), (3, 2, MH, bmi), (4, 4, MH, bmf)):
                v.tensor_scalar(r(j, n), wide(b, n), bias[:, :], None, ALU.add).then_inc(s_zr, 1)
            dve.wait_ge(s_zr, 3)
            link(v.tensor_copy(r(7), r(3)))
            dve.sem_inc(s_lr, 2)

            def log_gate(j, l, o, n):
                link(v.scalar_tensor_tensor(out=r(o, n), in0=r(j, n), scalar=0.0, in1=r(l, n), op0=ALU.min, op1=ALU.subtract))

            dve.wait_ge(s_er, 1)
            log_gate(0, 1, 0, FH)
            link(v.memset(r(8, FH), 1.0))
            link(v.tensor_tensor_scan(out=r(2, FH), data0=r(8, FH), data1=r(0, FH), initial=0.0, op0=ALU.mult, op1=ALU.add))
            v.tensor_scalar(r(2, FH), r(2, FH), -1.0, None, ALU.mult).then_inc(s_fr, 1)
            dve.wait_ge(s_er, 2)
            log_gate(4, 3, 4, MH)
            link(v.tensor_tensor_scan(out=r(3), data0=r(8), data1=r(4), initial=0.0, op0=ALU.mult, op1=ALU.add))
            link(v.tensor_tensor(r(5), r(7), r(3), ALU.subtract))
            link(v.tensor_tensor_scan(out=r(4), data0=r(5), data1=r(5), initial=0.0, op0=ALU.max, op1=ALU.max))
            link(v.tensor_tensor(r(8), r(3), r(4), ALU.add))
            M3 = r(4).rearrange("p (c t) -> p c t", t=P)
            E0 = R[0][0:MH, 0:NT]
            E1 = R[0][0:MH, NT:2 * NT]
            link(v.memset(R[0][0:MH, 0:1], 0.0))
            link(v.tensor_copy(R[0][0:MH, 1:NT], M3[:, 0:NT - 1, P - 1:P].rearrange("p c o -> p (c o)")))
            link(v.tensor_copy(E1, M3[:, :, P - 1:P].rearrange("p c o -> p (c o)")))
            spread = lambda x: x.unsqueeze(2).to_broadcast([MH, NT, P])
            c3 = lambda x: x.rearrange("p (c t) -> p c t", t=P)
            link(v.tensor_tensor(c3(r(6)), spread(E0), M3, ALU.subtract))
            link(v.tensor_tensor(c3(r(9)), c3(r(5)), spread(E1), ALU.subtract))
            link(v.tensor_tensor(R[1][0:MH, 0:NT], E0, E1, ALU.subtract))
            link(v.tensor_scalar(r(7), r(4), -1.0, None, ALU.mult))
            dve.sem_inc(s_mr, 2)

            def normalise(u):
                gain = (gq, gk)[u // 8]
                x, y = raw[u % 2], qn[u % 2]
                x3, y3 = (z.rearrange("p (h d) -> p h d", d=FD) for z in (x, y))
                dve.wait_ge(s_ev, u + 1)
                if u >= 2:
                    dve.wait_ge(s_qt, u - 1)
                link(v.tensor_tensor(sqb, x, x, ALU.mult))
                link(v.tensor_reduce(stat[:, 24:24 + FH], sqb.rearrange("p (h d) -> p h d", d=FD), AX.X, ALU.add))
                rms_scale(link, stat[:, 24:24 + FH], FD, stat[:, 24:24 + FH])
                link(v.tensor_tensor(y3, x3, stat[:, 24:24 + FH].unsqueeze(2).to_broadcast([P, FH, FD]), ALU.mult))
                v.tensor_tensor(y3, y3, gain[:, :].unsqueeze(1).to_broadcast([P, FH, FD]), ALU.mult).then_inc(s_qn, 1)

            for u in range(U_B):
                if u % 2 == 1 and u < 16:
                    partial_sums(4 + u // 2)
                if u % 2 == 0 and 4 <= u < 20:
                    mod_columns(4 + (u - 4) // 2)
                if u < 16:
                    normalise(u)
            dve.wait_ge(s_modc, NADA)
            link(v.scalar_tensor_tensor(out=a2[:, :], in0=mod[:, 32:40], scalar=1.0, in1=vcol[:, 56:64], op0=ALU.add, op1=ALU.mult))

            def fox_max(n):
                h, i = divmod(n, NT)
                N, b = P * i, n % 2
                if i == 0:
                    dve.wait_ge(s_nc[h % 2], 16 * (h // 2 + 1))
                nb = ncb[h % 2]
                link(v.tensor_tensor(ncd, nb[:, N:N + P], foxmask[:, :], ALU.add))
                dve.wait_ge(s_S, n + 1)
                if n >= 2:
                    dve.wait_ge(s_T, n - 1)
                lg = psum[:, 4:6, :].rearrange("p b n -> p (b n)")
                if i > 0:
                    v.tensor_tensor_reduce(pl[b][:, 0:N], lg[:, 0:N], nb[:, 0:N], 1.0, -3.0e38, ALU.add, ALU.max, stat[:, 40:41])
                link(v.tensor_tensor_reduce(pl[b][:, N:N + P], lg[:, N:N + P], ncd, 1.0, -3.0e38, ALU.add, ALU.max, stat[:, 41:42]))
                m = stat[:, 40:41] if i > 0 else stat[:, 41:42]
                v.tensor_scalar(stat[:, 16 + b:17 + b], m, stat[:, 41:42], -1.0, ALU.max, ALU.mult).then_inc(s_pl, 1)

            def fox_out(n):
                h, i = divmod(n, NT)
                dve.wait_ge(s_O, n + 1)
                link(v.reciprocal(stat[:, 42:43], stat[:, 18 + n % 4:19 + n % 4]))
                v.tensor_scalar(yf[:, i, h * FD:(h + 1) * FD], psum[:, 3, 0:FD], stat[:, 42:43], None, ALU.mult).then_inc(s_y, 1)

            for m in range(FSTEPS + 2):
                if m < FSTEPS:
                    fox_max(m)
                if m >= 2:
                    fox_out(m - 2)

            dve.wait_ge(s_pad, 2)
            for j in range(4):
                dve.wait_ge(s_cin[j % 2], 16 * (j // 2 + 1))
                tap = lambda w: vcol[:, 72 + 4 * w + j:73 + 4 * w + j]
                x, y = conv_in[j % 2], mqkT[:, j, :]
                link(v.tensor_scalar(y, x[:, 0:T], tap(0), None, ALU.mult))
                for w in range(1, TAPS):
                    ins = v.scalar_tensor_tensor(out=y, in0=x[:, w:w + T], scalar=tap(w), in1=y, op0=ALU.mult, op1=ALU.add)
                    if w < TAPS - 1:
                        link(ins)
                ins.then_inc(s_cv, 1)
            dve.wait_ge(s_rd, 64)
            b3 = lambda x: x.unsqueeze(2).to_broadcast([P, MH, P])
            M1 = MV + 1

            def ml_weights(c):
                dve.wait_ge(s_nm[c % 2], 16 * (c // 2 + 1))
                link(v.tensor_tensor(mw, nmb[c % 2], b3(mcol[:, 0, c, :]), ALU.add))
                v.tensor_scalar(mw, mw, 0.0, None, ALU.min).then_inc(m_w, 1)

            ml_weights(0)
            for c in range(NT):
                dve.wait_ge(m_ST, c + 1)
                kt = psum[:, 3, 0:MH * MQ].rearrange("p (h d) -> p h d", d=MQ)
                v.tensor_tensor(mkw, kt, mcol[:, 3, c, :].unsqueeze(2).to_broadcast([P, MH, MQ]), ALU.mult).then_inc(m_kw, 1)
                dve.wait_ge(m_k, c + 1)
                for b in range(2):
                    ins = v.tensor_tensor(msc[:, b::2, :], psum[:, (4, 7)[b], 0:2 * P].rearrange("p (j n) -> p j n", j=2), mw[:, b::2, :], ALU.mult)
                ins.then_inc(m_sc, 1)
                if c + 1 < NT:
                    dve.wait_ge(m_sc, c + 1)
                    ml_weights(c + 1)
                dve.wait_ge(m_B, c + 1)
                if c == 0:
                    dve.wait_ge(s_pad, 4)
                for h in range(MH):
                    b, j = MQ * (h % 2), h // 2
                    ins = v.scalar_tensor_tensor(out=mC[b:b + MQ, j, :], in0=mC[b:b + MQ, j, :], scalar=mdec[b:b + MQ, h, c:c + 1],
                                                 in1=psum[b:b + MQ, 3, j * M1:(j + 1) * M1], op0=ALU.mult, op1=ALU.add)
                ins.then_inc(m_st, 1)
                dve.wait_ge(m_in, c + 1)
                for j in range(2):
                    ins = v.tensor_tensor(mnum[:, 2 * j:2 * j + 2, :], mnum[:, 2 * j:2 * j + 2, :],
                                          psum[:, 5 + j, 0:2 * M1].rearrange("p (h n) -> p h n", h=2), ALU.add)
                ins.then_inc(m_num, 1)
                dve.wait_ge(m_num, c + 1)
                den = stat[:, 44:44 + MH]
                dsum = mnum[:, :, MV:M1]
                link(v.scalar_tensor_tensor(out=den.unsqueeze(2), in0=dsum, scalar=-1.0, in1=dsum, op0=ALU.mult, op1=ALU.max))
                link(v.tensor_tensor(den, den, mcol[:, 2, c, :], ALU.max))
                link(v.reciprocal(den, den))
                if c >= 1:
                    dve.wait_ge(m_yt, c)
                else:
                    dve.wait_ge(s_mos, 1)
                m3, y3 = mtmp.rearrange("p (h n) -> p h n", h=MH), my.rearrange("p (h n) -> p h n", h=MH)
                link(v.tensor_tensor(m3, mnum[:, :, 0:MV], b3(den), ALU.mult))
                link(v.tensor_tensor(my, mtmp, mtmp, ALU.mult))
                ss = stat[:, 48:48 + MH]
                link(v.tensor_reduce(ss, y3, AX.X, ALU.add))
                rms_scale(link, ss, MV, ss)
                link(v.tensor_tensor(m3, m3, b3(ss), ALU.mult))
                link(v.tensor_tensor(mtmp, mtmp, gml[:, :], ALU.mult))
                v.tensor_tensor(my, mtmp, mo[:, c, :], ALU.mult).then_inc(m_y, 1)

            c8 = lambda x: x.rearrange("p (c t) -> p c t", t=P)
            for h in range(HH):
                dve.wait_ge(h_ab, h + 1)
                if h == 0:
                    dve.wait_ge(m_yt, NT)
                link(v.scalar_tensor_tensor(out=hqe, in0=hz, scalar=0.0, in1=hE0, op0=ALU.min, op1=ALU.subtract))
                v.tensor_tensor(hk, hqe, hz, ALU.subtract).then_inc(h_lf, 1)
                for c in range(NT):
                    ins = v.tensor_tensor_scan(out=ha[:, c * P:(c + 1) * P], data0=ones[:, :], data1=hqe[:, c * P:(c + 1) * P],
                                               initial=0.0, op0=ALU.mult, op1=ALU.add)
                ins.then_inc(h_a, 1)
                dve.wait_ge(h_a, h + 1)
                v.tensor_tensor(c8(hkd), c8(ha)[:, :, P - 1:P].to_broadcast([P, NT, P]), c8(ha), ALU.subtract).then_inc(h_d, 1)

                def halves(x, l):
                    b = 1 << l
                    y = x.rearrange("p (n z b) -> p n z b", z=2, b=b)
                    return y[:, :, 0, :], y[:, :, 1, :]

                def exponents(l):
                    b = 1 << l
                    lo, hi = halves(ha, l)
                    elo, ehi = halves(hE[l % 2], l)
                    ref = lo[:, :, b - 1:b].to_broadcast([P, T // (2 * b), b])
                    v.tensor_tensor(elo, ref, lo, ALU.subtract)
                    v.tensor_tensor(ehi, hi, ref, ALU.subtract).then_inc(h_x, 1)

                def scale_qk(l):
                    dve.wait_ge(h_e, 7 * h + l + 1)
                    elo, ehi = halves(hE[l % 2], l)
                    klo, qhi = halves(hk, l)[0], halves(hq, l)[1]
                    v.tensor_tensor(elo, elo, klo, ALU.mult)
                    v.tensor_tensor(ehi, ehi, qhi, ALU.mult).then_inc(h_qk, 1)

                def take(l):
                    n = 8 * h + l
                    dve.wait_ge(h_S, n + 1)
                    b0 = 4 + 2 * (l % 2)
                    ins = v.copy_predicated(c8(hsc), levels[:, l, :].unsqueeze(1).to_broadcast([P, NT, P]),
                                            psum[:, b0:b0 + 2, :].rearrange("p b (c n) -> p (b c) n", c=4))
                    ins.then_inc(h_sc, 1)

                exponents(0)
                if h >= 1:
                    dve.wait_ge(h_O, h)
                link(v.memset(hsc, 0.0))
                dve.wait_ge(h_k, h + 1)
                dve.wait_ge(h_ea, h + 1)
                link(v.tensor_copy(stat[:, 52:60], c8(hqe)[:, :, P - 1:P].rearrange("p c o -> p (c o)")))
                link(v.tensor_tensor(hqe, hqe, hq, ALU.mult))
                dve.wait_ge(h_de, h + 1)
                v.tensor_tensor(hkd, hkd, hk, ALU.mult).then_inc(h_kd, 1)
                scale_qk(0)
                for l in range(1, 8):
                    if l < 7:
                        if l >= 2:
                            dve.wait_ge(h_S, 8 * h + l - 1)
                        exponents(l)
                        if l >= 1:
                            take(l - 1)
                        scale_qk(l)
                    else:
                        take(6)
                        link(v.tensor_copy(stat[:, 60:61], ones[:, 0:1]))
                        dve.sem_inc(h_qk, 1)
                take(7)
                dve.wait_ge(h_up, h + 1)
                link(v.memset(hst[:, 0:P], 0.0))
                for c in range(NT - 1):
                    ins = v.scalar_tensor_tensor(out=hst[:, (c + 1) * P:(c + 2) * P], in0=hst[:, c * P:(c + 1) * P],
                                                 scalar=stat[:, 52 + c:53 + c], in1=psum[:, 6 + c // 4, (c % 4) * P:(c % 4 + 1) * P],
                                                 op0=ALU.mult, op1=ALU.add)
                    if c < NT - 2:
                        link(ins)
                ins.then_inc(h_st, 1)
                dve.wait_ge(h_O, h + 1)
                o8 = psum[:, 4:6, :].rearrange("p b (c n) -> p (b c) n", c=4)
                link(v.tensor_copy(c8(hE0), o8))
                link(v.tensor_tensor(hE1, hE0, hE0, ALU.mult))
                ss = stat[:, 24:32]
                link(v.tensor_reduce(ss, c8(hE1), AX.X, ALU.add))
                rms_scale(link, ss, P, ss)
                link(v.tensor_tensor(c8(hE0), c8(hE0), ss.unsqueeze(2).to_broadcast([P, NT, P]), ALU.mult))
                link(v.tensor_tensor(c8(hE0), c8(hE0), ghg[:, h * P:(h + 1) * P].unsqueeze(1).to_broadcast([P, NT, P]), ALU.mult))
                v.tensor_tensor(hkT, hE0, hg, ALU.mult).then_inc(h_y, 1)

            dve.wait_ge(h_yt, HH)
            dve.wait_ge(s_pj, NU)
            for n in range(48):
                br, j, half = n // 16, n // 2 % 8, n % 2
                dst = hT[:, j, half * BW:(half + 1) * BW]
                dve.wait_ge(s_gs, n + 1)
                dve.wait_ge(s_br, n + 1)
                if br == 0:
                    v.tensor_tensor(dst, gt[n % 3], bank(n % 3), ALU.mult).then_inc(s_pr, 1)
                else:
                    v.tensor_tensor(prod[n % 2], gt[n % 3], bank(n % 3), ALU.mult).then_inc(s_pr, 1)
                    dve.wait_ge(s_pr, n + 1)
                    v.tensor_tensor(dst, dst, prod[n % 2], ALU.add).then_inc(s_mg, 1)
            dve.wait_ge(s_mg, 32)
            for n in range(8):
                if n >= 2:
                    dve.wait_ge(s_bc, n - 1)
                c = (mod[:, 16:24], a2[:, :], mod[:, 24:32], mod[:, 40:48])[n // 2][:, 4 * (n % 2):4 * (n % 2) + 4]
                v.tensor_tensor(dgb[n % 2], ident[:, :].unsqueeze(1).to_broadcast([P, 4, P]),
                                c.unsqueeze(2).to_broadcast([P, 4, P]), ALU.mult).then_inc(s_dg, 1)
            dve.wait_ge(s_bcc, 8)
            dve.wait_ge(s_rw, 32)

            def residual(i):
                y, z = x2[i % 2], h2[i % 2]
                dve.wait_ge(s_mx, i + 1)
                dve.wait_ge(s_xi[i % 2], 16 * (i // 2 + 1))
                if i >= 2:
                    dve.wait_ge(s_so[i % 2], 32 * (i // 2))
                    dve.wait_ge(s_h2t, i - 1)
                link(v.tensor_tensor(y, banks(2 * (i % 2), 2), g1b, ALU.mult))
                v.tensor_tensor(y, y, xin[i % 2], ALU.add).then_inc(s_x2, 1)
                dve.wait_ge(s_sq, i + 1)
                rms_scale(link, stat[:, 32 + i:33 + i], D, stat[:, 32 + i:33 + i])
                turned = lambda q: q.rearrange("p (d k) -> p k d", k=KD)
                z3 = z.rearrange("p (k d) -> p k d", k=KD)
                link(v.scalar_tensor_tensor(out=z3, in0=turned(y), scalar=stat[:, 32 + i:33 + i], in1=turned(a2b),
                                            op0=ALU.mult, op1=ALU.mult))
                v.tensor_tensor(z3, z3, turned(b2b), ALU.add).then_inc(s_h2, 1)

            def first_of(src, values, kth, keep, n, out_):
                link(v.tensor_scalar(out_, src, kth, None, ALU.is_gt))
                link(v.tensor_reduce(stat[:, 61:62], out_, AX.X, ALU.add))
                link(v.tensor_scalar(stat[:, 61:62], stat[:, 61:62], -1.0, float(n), ALU.mult, ALU.add))
                link(v.tensor_scalar(values, src, kth, None, ALU.is_equal))
                link(v.tensor_tensor_scan(out=keep, data0=ones[:, 0:src.shape[1]], data1=values, initial=0.0, op0=ALU.mult, op1=ALU.add))
                link(v.scalar_tensor_tensor(out=values, in0=keep, scalar=stat[:, 61:62], in1=values, op0=ALU.is_le, op1=ALU.mult))
                link(v.tensor_tensor(out_, out_, values, ALU.add))

            def choose(i):
                dve.wait_ge(s_sg, i + 1)
                link(v.tensor_tensor(cho, sco, rbias, ALU.add))
                for g in range(NG):
                    link(v.max(m8[:, g, :], cho[:, g * GE:(g + 1) * GE]))
                link(v.tensor_tensor(gsc.unsqueeze(2), m8[:, :, 0:1], m8[:, :, 1:2], ALU.add))
                link(v.max(top, gsc))
                first_of(gsc, geq, top[:, TOPG - 1:TOPG], gcu, TOPG, gmk)
                link(v.tensor_scalar(gmk, gmk, 1.0, -NEG, ALU.subtract, ALU.mult))
                link(v.tensor_tensor(cho.rearrange("p (g n) -> p g n", g=NG), cho.rearrange("p (g n) -> p g n", g=NG),
                                     gmk.unsqueeze(2).to_broadcast([P, NG, GE]), ALU.add))
                link(v.max(top, cho))
                first_of(cho, eqt, top[:, TOPK - 1:TOPK], cum, TOPK, selall[:, i, :])
                link(v.tensor_tensor(sel, sco, selall[:, i, :], ALU.mult))
                link(v.tensor_reduce(stat[:, 62:63], sel, AX.X, ALU.add))
                link(v.reciprocal(stat[:, 62:63], stat[:, 62:63]))
                v.tensor_scalar(tw[:, i, 0:NE, 1:2].rearrange("p e o -> p (e o)"), sel, stat[:, 62:63], ROUTE, ALU.mult, ALU.mult).then_inc(s_sel, 1)

            def slots(i):
                dve.wait_ge(s_pos, i + 1)
                link(v.scalar_tensor_tensor(out=msk, in0=psum[:, 7, 0:NE], scalar=1.0, in1=selall[:, i, :], op0=ALU.add, op1=ALU.mult))
                v.tensor_scalar(posm[:, i, 0:NE], msk, 1.0, None, ALU.subtract).then_inc(s_pm, 1)

            for i in range(NT + 2):
                if i < NT:
                    residual(i)
                if 1 <= i <= NT:
                    choose(i - 1)
                if i >= 2:
                    slots(i - 2)
            for i in range(NT):
                link(v.tensor_copy(tw[:, i, :, 0:1].rearrange("p e o -> p (e o)"), tok[:, i:i + 1].to_broadcast([P, NX])))
            link(v.memset(posm[:, :, NE:NX], -1.0))
            link(v.memset(tw[:, :, NE:NX, 1:2], 0.0))
            link(v.memset(cnt[:, NE:NX], 0))
            dve.wait_ge(s_cn, 1)
            v.tensor_copy(cnt[:, 0:NE], psum[:, 7, 0:NE]).then_inc(s_tab, 1)
            for i in range(NT):
                dve.wait_ge(s_si, i + 1)
                if i >= 1:
                    dve.wait_ge(s_ht, i)
                v.tensor_tensor(shh, sgm, bank(i % 2)[:, FF:2 * FF], ALU.mult).then_inc(s_hd, 1)
                dve.wait_ge(s_sO, i + 1)
                if i >= 2:
                    dve.wait_ge(s_ys[i % 2], 16 * (i // 2 + 1 - i % 2))
                v.tensor_copy(ysh[i % 2][:, BW:D], bank(5)).then_inc(s_yv, 1)

            def one_hot(j, e, c):
                v.tensor_tensor(oh[j], slotn[:, bass.ds(c * P, P)].unsqueeze(1).to_broadcast([P, NT, P]), posm[:, :, bass.ds(e, 1)].to_broadcast([P, NT, P]), ALU.is_equal).then_inc(e_oh[j], 1)

            def rows_of(j, q, n):
                l = lst[:, 4 * j + q, :]
                v.tensor_reduce(l, psum[:, 2, 8 * j:8 * j + 6].rearrange("p (s z) -> p z s", z=2), AX.X, ALU.add).then_inc(e_red[j], 1)
                done(dve, e_red[j], n + 1)
                v.tensor_scalar(idx[:, 4 * j + q:4 * j + q + 1], l[:, 0:1], float(FAR), dump[:, :], ALU.add, ALU.min).then_inc(e_idx[j], 1)

            def hidden(j):
                v.tensor_tensor(hid[j], sg[j], bank(3 if j == 0 else 4)[:, FF:2 * FF], ALU.mult).then_inc(e_hid[j], 1)

            def weigh_out(j, q):
                v.tensor_scalar(ob[j][:, BW:D], bank(7), lst[:, 4 * j + q, 1:2], None, ALU.mult).then_inc(e_obv[j], 1)

            dve.wait_ge(s_ys[0], 16 * (NT // 2 + 1))
            dve.wait_ge(s_ys[1], 16 * (NT // 2))
            dve.wait_ge(s_so[0], 16 * NT)
            dve.wait_ge(s_so[1], 16 * NT)
            dve.wait_ge(e_clear, 1)
            for q in (e_oh, e_red, e_idx, e_hid, e_obv):
                for j in range(3):
                    dve.sem_inc(q[j], 1)
            link(v.tensor_copy(twb[:, :, :, 0, :], tw))
            for part_n in (1, 2):
                link(v.tensor_tensor(rest, tw if part_n == 1 else rest, twb[:, :, :, part_n - 1, :], ALU.subtract))
                link(v.tensor_copy(twb[:, :, :, part_n, :], rest))
            for c in range(NC):
                ins = v.tensor_scalar(slotn[:, c * P:(c + 1) * P], col_i[:, :], float(c * P), None, ALU.add)
            link(ins)
            for e in range(3):
                if e >= 1:
                    done(dve, e_lst[0], e)
                    done(dve, e_lst[1], e)
                    for j in range(2):
                        rows_of(j, e - 1, e - 1)
                one_hot(0, e, 0)
                one_hot(1, e, 1)
            with dve.Fori(0, NE // 4) as it:
                for q in range(4):
                    e, q2 = 4 * it + q, (q + 2) % 4
                    n_e = dve.value_load(cnt[0:1, bass.ds(e, 1)], min_val=0, max_val=T)
                    n_2 = dve.value_load(cnt[0:1, bass.ds(e + 2, 1)], min_val=0, max_val=T)
                    n_3 = dve.value_load(cnt[0:1, bass.ds(e + 3, 1)], min_val=0, max_val=T)
                    done(dve, e_si[0], e + 1)
                    done(dve, e_hT[0], e)
                    hidden(0)
                    done(dve, e_lst[0], e + 3)
                    done(dve, e_lst[1], e + 3)
                    done(dve, e_idx[1], e + 2)
                    rows_of(0, q2, e + 2)
                    with dve.If(n_2 > P):
                        rows_of(1, q2, e + 2)
                    with dve.Else():
                        skipped(dve, e_red[1], e + 2)
                        skipped(dve, e_idx[1], e + 2)
                    one_hot(0, e + 3, 0)
                    with dve.If(n_e > P):
                        done(dve, e_si[1], e + 1)
                        done(dve, e_hT[1], e)
                        hidden(1)
                    with dve.Else():
                        skipped(dve, e_hid[1], e)
                    with dve.If(n_3 > P):
                        done(dve, e_oh[1], e + 3)
                        one_hot(1, e + 3, 1)
                    with dve.Else():
                        skipped(dve, e_oh[1], e + 3)
                    done(dve, e_O[0], 2 * e + 2)
                    done(dve, e_sc[0], e)
                    weigh_out(0, q)
                    with dve.If(n_e > P):
                        done(dve, e_O[1], 2 * e + 2)
                        done(dve, e_sc[1], e)
                        weigh_out(1, q)
                    with dve.Else():
                        skipped(dve, e_obv[1], e)
                    all_done(dve, (e_sc[1], e))
                    with dve.If(n_e > 2 * P):
                        with dve.Fori(0, ND) as c:
                            n = ND * e + c
                            with dve.If(n_e > P * (c + 2)):
                                one_hot(2, e, c + 2)
                                done(dve, e_lst[2], n + 1)
                                done(dve, e_oba[2], n)
                                done(dve, e_sc[2], n)
                                rows_of(2, 0, n)
                                done(dve, e_si[2], n + 1)
                                hidden(2)
                                done(dve, e_O[2], 2 * n + 2)
                                weigh_out(2, 0)
                            with dve.Else():
                                for x in (e_oh, e_red, e_idx, e_hid, e_obv):
                                    skipped(dve, x[2], n)
                            dve.nop()
                    with dve.Else():
                        for x in (e_oh, e_red, e_idx, e_hid, e_obv):
                            skipped(dve, x[2], ND * e, ND)
                    dve.nop()
            for i in range(NT):
                dve.wait_ge(f_y[i % 4], 32 * (i // 4 + 1))
                link(v.tensor_tensor(fy[i % 4], fy[i % 4], g2b, ALU.mult))
                v.tensor_tensor(fy[i % 4], fy[i % 4], fx[i % 4], ALU.add).then_inc(f_s, 1)


_INS = ["x", "c", "ada_w", "ada_b", "norm1_g", "norm2_g", "w_in", "fox_bf", "fox_q_g", "fox_k_g", "mlstm_conv",
        "mlstm_bi", "mlstm_bf", "mlstm_norm_g", "hgrn_lower_bounds", "hgrn_norm_g", "w_branch", "w_out", "router_w",
        "router_bias", "exp_w1", "exp_w3", "exp_w2", "sh_w1", "sh_w3", "sh_w2"]


def kernel(**inputs):
    import numpy as _np
    import concourse.bacc as _bacc
    from concourse import mybir as _mybir
    from concourse.bass_utils import run_bass_kernel_spmd as _run

    nc = _bacc.Bacc("TRN2", target_bir_lowering=False, num_devices=1)
    arrays, args = {}, {}
    for name in _INS:
        v = _np.ascontiguousarray(inputs[name])
        arrays[f"in_{name}"] = v
        args[name] = nc.dram_tensor(f"in_{name}", v.shape, _mybir.dt.from_np(v.dtype), kind="ExternalInput").ap()
    out = nc.dram_tensor("out_x", arrays["in_x"].shape, F32, kind="ExternalOutput").ap()
    layer_kernel(nc, args, out)
    r = _run(nc, [arrays], core_ids=[0])
    return r.results[0]["out_x"]
```
